# Optimizing a Trainium2 kernel written in Bass

```python
import math
import jax, jax.numpy as jnp
from jax import lax
import numpy as np

D_MODEL = 1024
BATCH = 1
SEQ = 512
DEPTH = 2

DA_HEADS = 4
DA_QK = 64
DA_V = 2 * DA_QK
DA_WIDTH = DA_HEADS * DA_V
ROPE_DIM = DA_QK // 4
ROPE_THETA = 500000.0
Q_BLOCK = 128
SC_WIDTH = 256
SC_CONV = 3
S5_WIDTH = 256
S5_GROUP = 16
S5_GROUPS = S5_WIDTH // S5_GROUP
S5_STATE = 64
M2_HEADS = 4
M2_HEAD_DIM = 64
M2_WIDTH = M2_HEADS * M2_HEAD_DIM
M2_GROUPS = 2
M2_STATE = 128
M2_CONV = 4
M2_CHUNK = 128
M2_XBC = M2_WIDTH + 2 * M2_GROUPS * M2_STATE
D_MIX = DA_WIDTH + SC_WIDTH + S5_WIDTH + M2_WIDTH
OFF_Q = 0
OFF_K = OFF_Q + DA_WIDTH
OFF_V = OFF_K + DA_WIDTH
OFF_SC = OFF_V + DA_WIDTH
OFF_S5 = OFF_SC + 3 * SC_WIDTH
OFF_M2Z = OFF_S5 + S5_WIDTH
OFF_M2XBC = OFF_M2Z + M2_WIDTH
OFF_M2DT = OFF_M2XBC + M2_XBC
D_PROJ = OFF_M2DT + M2_HEADS
D_FF = 2816
FFN_CONV = 3
EPS = 1e-6

kernel_name = "hybrid_parallel_heads_diffattn_shortconv_s5_ssd"

def rmsnorm(x, g):
    xf = x.astype(jnp.float32)
    y = xf * lax.rsqrt(jnp.mean(xf * xf, axis=-1, keepdims=True) + EPS)
    return (y * g.astype(jnp.float32)).astype(x.dtype)

def causal_dwconv(x, w):
    k_w, ch = w.shape
    return lax.conv_general_dilated(
        x, w[:, None, :].astype(x.dtype), window_strides=(1,), padding=[(k_w - 1, 0)],
        dimension_numbers=('NWC', 'WIO', 'NWC'), feature_group_count=ch)

def rope_tables(seq):
    inv = 1.0 / (ROPE_THETA ** (jnp.arange(0, ROPE_DIM, 2, dtype=jnp.float32) / ROPE_DIM))
    ang = jnp.arange(seq, dtype=jnp.float32)[:, None] * inv[None, :]
    return jnp.cos(ang), jnp.sin(ang)

def partial_rope(x, cos, sin):
    xr = x[..., :ROPE_DIM].astype(jnp.float32)
    half = ROPE_DIM // 2
    x1, x2 = xr[..., :half], xr[..., half:]
    c = cos[:, None, None, :]
    s = sin[:, None, None, :]
    rot = jnp.concatenate([x1 * c - x2 * s, x1 * s + x2 * c], axis=-1).astype(x.dtype)
    return jnp.concatenate([rot, x[..., ROPE_DIM:]], axis=-1)

def diff_attention(q, k, v, lam, lambda_init, sub_g):
    bsz, seq, nh, _, d = q.shape
    nb = seq // Q_BLOCK
    scale = d ** -0.5
    qb = q.reshape(bsz, nb, Q_BLOCK, nh, 2, d).transpose(1, 0, 2, 3, 4, 5)
    kpos = jnp.arange(seq)

    def block(args):
        qi, i = args
        s = jnp.einsum('bqhcd,bkhcd->bhcqk', qi, k).astype(jnp.float32) * scale
        qpos = i * Q_BLOCK + jnp.arange(Q_BLOCK)
        s = jnp.where(kpos[None, :] <= qpos[:, None], s, -jnp.inf)
        p = jax.nn.softmax(s, axis=-1)
        a = p[:, :, 0] - lam * p[:, :, 1]
        return jnp.einsum('bhqk,bkhe->bqhe', a.astype(v.dtype), v)

    o = lax.map(block, (qb, jnp.arange(nb)))
    o = o.transpose(1, 0, 2, 3, 4).reshape(bsz, seq, nh, 2 * d)
    o = rmsnorm(o, sub_g) * (1.0 - lambda_init)
    return o.reshape(bsz, seq, nh * 2 * d)

def s5_mixer(u, lam_re, lam_im, log_dt, b_re, b_im, c_re, c_im, d_skip, w_glu, b_glu):
    bsz, seq, _ = u.shape
    f32 = jnp.float32
    uf = u.astype(f32).reshape(bsz, seq, S5_GROUPS, S5_GROUP)
    lam = lax.complex(lam_re.astype(f32), lam_im.astype(f32))
    dt = jnp.exp(log_dt.astype(f32))[:, None]
    lam_bar = jnp.exp(lam * dt)
    b = lax.complex(b_re.astype(f32), b_im.astype(f32))
    b_bar = ((lam_bar - 1.0) / lam)[..., None] * b
    bu = jnp.einsum('bsgh,gph->bsgp', uf.astype(jnp.complex64), b_bar)
    a = jnp.broadcast_to(lam_bar, bu.shape)

    def comb(e1, e2):
        a1, x1 = e1
        a2, x2 = e2
        return a2 * a1, a2 * x1 + x2

    _, xs = lax.associative_scan(comb, (a, bu), axis=1)
    c = lax.complex(c_re.astype(f32), c_im.astype(f32))
    y = jnp.einsum('bsgp,ghp->bsgh', xs, c).real \
        + d_skip.astype(f32).reshape(S5_GROUPS, S5_GROUP) * uf
    y = y.reshape(bsz, seq, S5_WIDTH)
    g = jax.nn.gelu(y)
    out = g * jax.nn.sigmoid(g @ w_glu.astype(f32) + b_glu.astype(f32))
    return out.astype(u.dtype)

def segsum(a):
    cs = jnp.cumsum(a, axis=-1)
    seg = cs[..., :, None] - cs[..., None, :]
    n = a.shape[-1]
    return jnp.where(jnp.tril(jnp.ones((n, n), dtype=bool)), seg, -jnp.inf)

def ssd_chunked(x, a, b, c):
    bsz, seq, nh, hp = x.shape
    ns = b.shape[-1]
    nc = seq // M2_CHUNK
    x = x.reshape(bsz, nc, M2_CHUNK, nh, hp)
    b = b.reshape(bsz, nc, M2_CHUNK, nh, ns)
    c = c.reshape(bsz, nc, M2_CHUNK, nh, ns)
    a = a.reshape(bsz, nc, M2_CHUNK, nh).transpose(0, 3, 1, 2)
    a_cs = jnp.cumsum(a, axis=-1)
    decay = jnp.exp(segsum(a))
    scores = jnp.einsum('bclhn,bcshn->bhcls', c, b) * decay
    y_diag = jnp.einsum('bhcls,bcshp->bclhp', scores, x)
    decay_states = jnp.exp(a_cs[..., -1:] - a_cs)
    states = jnp.einsum('bclhn,bhcl,bclhp->bchpn', b, decay_states, x)
    chunk_decay = jnp.exp(a_cs[..., -1])

    def step(h, inp):
        st, dec = inp
        return dec[..., None, None] * h + st, h

    h0 = jnp.zeros((bsz, nh, hp, ns), jnp.float32)
    _, h_in = lax.scan(step, h0, (states.transpose(1, 0, 2, 3, 4), chunk_decay.transpose(2, 0, 1)))
    h_in = h_in.transpose(1, 0, 2, 3, 4)
    y_off = jnp.einsum('bclhn,bchpn,bhcl->bclhp', c, h_in, jnp.exp(a_cs))
    return (y_diag + y_off).reshape(bsz, seq, nh, hp)

def mamba2_mixer(z, xbc, dt_raw, conv_w, conv_b, dt_bias, a_log, d_skip, norm_g):
    bsz, seq, _ = z.shape
    f32 = jnp.float32
    xbc = jax.nn.silu((causal_dwconv(xbc, conv_w) + conv_b.astype(xbc.dtype)).astype(f32))
    xs = xbc[..., :M2_WIDTH].reshape(bsz, seq, M2_HEADS, M2_HEAD_DIM)
    bm = xbc[..., M2_WIDTH:M2_WIDTH + M2_GROUPS * M2_STATE].reshape(bsz, seq, M2_GROUPS, M2_STATE)
    cm = xbc[..., M2_WIDTH + M2_GROUPS * M2_STATE:].reshape(bsz, seq, M2_GROUPS, M2_STATE)
    rep = M2_HEADS // M2_GROUPS
    bm = jnp.repeat(bm, rep, axis=2)
    cm = jnp.repeat(cm, rep, axis=2)
    dt = jax.nn.softplus(dt_raw.astype(f32) + dt_bias.astype(f32))
    a = -jnp.exp(a_log.astype(f32))
    y = ssd_chunked(xs * dt[..., None], a * dt, bm, cm)
    y = y + d_skip.astype(f32)[:, None] * xs
    y = y.reshape(bsz, seq, M2_WIDTH)
    y = rmsnorm(y * jax.nn.silu(z.astype(f32)), norm_g)
    return y.astype(z.dtype)

def setup_inputs(seed: int = 0) -> dict:
    key = jax.random.key(seed)
    ks = iter(jax.random.split(key, 48))
    f32 = jnp.float32

    def nrm(shape, scale):
        return jax.random.normal(next(ks), shape, f32) * scale

    L = DEPTH
    n = jnp.arange(S5_STATE, dtype=f32)
    m2_dt = jnp.exp(jax.random.uniform(next(ks), (L, M2_HEADS), f32, math.log(1e-3), math.log(1e-1)))
    return {
        "x": nrm((BATCH, SEQ, D_MODEL), 1.0),
        "ln1_g": 1.0 + nrm((L, D_MODEL), 0.02),
        "w_in": nrm((L, D_MODEL, D_PROJ), D_MODEL ** -0.5),
        "qk_norm_g": 1.0 + nrm((L, 2, DA_QK), 0.02),
        "da_lambda": nrm((L, 4, DA_QK), 0.1),
        "subln_g": 1.0 + nrm((L, DA_V), 0.02),
        "sc_conv_w": nrm((L, SC_CONV, SC_WIDTH), SC_CONV ** -0.5),
        "s5_lam_re": -0.5 + nrm((L, S5_GROUPS, S5_STATE), 0.01),
        "s5_lam_im": math.pi * n + nrm((L, S5_GROUPS, S5_STATE), 0.01),
        "s5_log_dt": jax.random.uniform(next(ks), (L, S5_GROUPS), f32, math.log(1e-3), math.log(1e-1)),
        "s5_b_re": nrm((L, S5_GROUPS, S5_STATE, S5_GROUP), (2 * S5_GROUP) ** -0.5),
        "s5_b_im": nrm((L, S5_GROUPS, S5_STATE, S5_GROUP), (2 * S5_GROUP) ** -0.5),
        "s5_c_re": nrm((L, S5_GROUPS, S5_GROUP, S5_STATE), (2 * S5_STATE) ** -0.5),
        "s5_c_im": nrm((L, S5_GROUPS, S5_GROUP, S5_STATE), (2 * S5_STATE) ** -0.5),
        "s5_d": nrm((L, S5_WIDTH), 1.0),
        "s5_w_glu": nrm((L, S5_WIDTH, S5_WIDTH), S5_WIDTH ** -0.5),
        "s5_b_glu": nrm((L, S5_WIDTH), 0.01),
        "m2_conv_w": nrm((L, M2_CONV, M2_XBC), M2_CONV ** -0.5),
        "m2_conv_b": nrm((L, M2_XBC), 0.01),
        "m2_dt_bias": m2_dt + jnp.log(-jnp.expm1(-m2_dt)),
        "m2_a_log": jnp.log(jax.random.uniform(next(ks), (L, M2_HEADS), f32, 1.0, 16.0)),
        "m2_d": 1.0 + nrm((L, M2_HEADS), 0.1),
        "m2_norm_g": 1.0 + nrm((L, M2_WIDTH), 0.02),
        "w_out": nrm((L, D_MIX, D_MODEL), D_MIX ** -0.5),
        "ln2_g": 1.0 + nrm((L, D_MODEL), 0.02),
        "ffn_w_gate": nrm((L, D_MODEL, D_FF), D_MODEL ** -0.5),
        "ffn_w_up": nrm((L, D_MODEL, D_FF), D_MODEL ** -0.5),
        "ffn_conv_w": nrm((L, FFN_CONV, D_FF), FFN_CONV ** -0.5),
        "ffn_w_down": nrm((L, D_FF, D_MODEL), D_FF ** -0.5),
    }

def reference(x, ln1_g, w_in, qk_norm_g, da_lambda, subln_g, sc_conv_w,
              s5_lam_re, s5_lam_im, s5_log_dt, s5_b_re, s5_b_im, s5_c_re, s5_c_im,
              s5_d, s5_w_glu, s5_b_glu, m2_conv_w, m2_conv_b, m2_dt_bias, m2_a_log,
              m2_d, m2_norm_g, w_out, ln2_g, ffn_w_gate, ffn_w_up, ffn_conv_w, ffn_w_down):
    bsz, seq, _ = x.shape
    cos, sin = rope_tables(seq)
    for l in range(DEPTH):
        h = rmsnorm(x, ln1_g[l])
        proj = h @ w_in[l]

        q = proj[..., OFF_Q:OFF_K].reshape(bsz, seq, DA_HEADS, 2, DA_QK)
        k = proj[..., OFF_K:OFF_V].reshape(bsz, seq, DA_HEADS, 2, DA_QK)
        v = proj[..., OFF_V:OFF_SC].reshape(bsz, seq, DA_HEADS, DA_V)
        q = partial_rope(rmsnorm(q, qk_norm_g[l, 0]), cos, sin)
        k = partial_rope(rmsnorm(k, qk_norm_g[l, 1]), cos, sin)
        lam_p = da_lambda[l].astype(jnp.float32)
        lambda_init = 0.8 - 0.6 * math.exp(-0.3 * l)
        lam = jnp.exp(jnp.sum(lam_p[0] * lam_p[1])) - jnp.exp(jnp.sum(lam_p[2] * lam_p[3])) + lambda_init
        o_a = diff_attention(q, k, v, lam, lambda_init, subln_g[l])

        sc_b = proj[..., OFF_SC:OFF_SC + SC_WIDTH]
        sc_c = proj[..., OFF_SC + SC_WIDTH:OFF_SC + 2 * SC_WIDTH]
        sc_h = proj[..., OFF_SC + 2 * SC_WIDTH:OFF_S5]
        o_b = sc_b * causal_dwconv(sc_c * sc_h, sc_conv_w[l])

        o_c = s5_mixer(proj[..., OFF_S5:OFF_M2Z], s5_lam_re[l], s5_lam_im[l], s5_log_dt[l],
                       s5_b_re[l], s5_b_im[l], s5_c_re[l], s5_c_im[l], s5_d[l],
                       s5_w_glu[l], s5_b_glu[l])

        o_d = mamba2_mixer(proj[..., OFF_M2Z:OFF_M2XBC], proj[..., OFF_M2XBC:OFF_M2DT],
                           proj[..., OFF_M2DT:D_PROJ], m2_conv_w[l], m2_conv_b[l],
                           m2_dt_bias[l], m2_a_log[l], m2_d[l], m2_norm_g[l])

        mixed = jnp.concatenate([o_a.astype(x.dtype), o_b.astype(x.dtype),
                                 o_c.astype(x.dtype), o_d.astype(x.dtype)], axis=-1)
        x = x + mixed @ w_out[l]

        h2 = rmsnorm(x, ln2_g[l])
        g = causal_dwconv(h2 @ ffn_w_gate[l], ffn_conv_w[l])
        x = x + (jax.nn.silu(g) * (h2 @ ffn_w_up[l])) @ ffn_w_down[l]
    return x


_drawn_inputs = setup_inputs


def setup_inputs(seed=0):
    import zlib

    import numpy as np

    out = dict(_drawn_inputs(seed))
    spreads = {}
    factors = {'qk_norm_g': 3.908,
     'subln_g': 4.395,
     's5_lam_re': 64.0,
     's5_lam_im': 40.824,
     's5_log_dt': 43.856,
     's5_b_re': 56.184,
     's5_b_im': 57.08,
     's5_c_re': 56.608,
     's5_c_im': 57.816,
     's5_b_glu': 64.0,
     'm2_conv_b': 8.0,
     'm2_d': 6.594,
     'm2_norm_g': 5.089,
     'ln2_g': 3.127}
    for name, (base, spread) in spreads.items():
        noise = np.random.default_rng([zlib.crc32(name.encode()), seed]).standard_normal(out[name].shape)
        drawn = base * np.exp(spread * noise) if base else spread * noise
        out[name] = __import__('jax').numpy.asarray(drawn.astype(out[name].dtype))
    for name, factor in factors.items():
        out[name] = (out[name] * factor).astype(out[name].dtype)
    return out
```

```python
from contextlib import ExitStack

import numpy as np

import concourse.bass as bass
from concourse import mybir

F32 = mybir.dt.float32
F32R = mybir.dt.float32r
BF16 = mybir.dt.bfloat16
ALU = mybir.AluOpType
ACT = mybir.ActivationFunctionType
AX = mybir.AxisListType.X

L = 2
D, T, P = 1024, 512, 128
KD = D // P
NQ = T // P
HEADS, QK = 4, 64
ROPE = 16
THETA = 500000.0
SJ, SH = 8, 32
M2H, M2P = 4, 64
FF, FHALF = 22, 11
MIXA, MIXB, MIXC, MIXD = 0, 4, 6, 8
MIXED = 10
KEARLY = MIXED - HEADS
EPS = 1e-6
NIN = 28
FINE, COARSE = 32, 16
NT = FINE + COARSE
NEG = -1e30
INV2PI = float(np.float32(1 / (2 * np.pi)))
ROUND = float(1.5 * 2**23)
C1 = 6.28125
C2 = float(np.float32(np.round((2 * np.pi - C1) * 2**21) / 2**21))
C3 = float(np.float32(2 * np.pi - C1 - C2))
PI_CAP = 3.1415925

CONSTS, _o = {}, 0
for _name, _n in [("ident", P), ("ones", P), ("tri", P), ("perm", P), ("block", P), ("cap", P), ("mask", P),
                  ("cos", T), ("sin", T), ("steps", NT), ("eps", 1)]:
    CONSTS[_name] = slice(_o, _o + _n)
    _o += _n
NCONST = _o
PARAMS, _o = {}, 0
for _name, _n in [("g1", KD), ("g2", KD), ("qkg", 2), ("subg", 1), ("linit", 1), ("oneml", 1), ("scw", 6),
                  ("lre", SJ), ("lim", SJ), ("ldt", SJ), ("s5d", 2), ("bglu", 2), ("m2w", 24), ("m2b", 6),
                  ("dtb", M2H), ("alog", M2H), ("m2d", 2), ("m2g", 2), ("ffw", 3 * FF), ("dal", 4 * QK),
                  ("wdt", KD * M2H)]:
    PARAMS[_name] = (_o, _n)
    _o += _n
NPAR = _o


def build(nc, A):
    with ExitStack() as ctx:
        arena_end = [0]

        def sb(name, shape, dt=F32, at=None):
            size = int(np.prod(shape[1:])) * (2 if dt == BF16 else 4)
            size = -(-size // 32) * 32
            off = arena_end[0] if at is None else at
            if at is None:
                arena_end[0] += size
            offsets[name] = off
            return nc.alloc_sbuf_tensor_at(name, list(shape), dt, offset=base + off)

        def sem(name):
            return ctx.enter_context(nc.semaphore(name))

        offsets = {}
        base = -(-nc.sbuf_base // 32) * 32
        arena_bytes = nc.sbuf_bytes_remaining - 32

        x = sb("x", [P, KD, T])
        xh = sb("xh", [P, KD, T], F32R)
        xl = sb("xl", [P, KD, T], F32R)
        mh = sb("mh", [P, FHALF, T], F32R)
        ml = sb("ml", [P, FHALF, T], F32R)
        raw = sb("raw", [P, 2, FHALF * P])
        wh = sb("wh", [P, 2, FHALF * P], F32R)
        wl = sb("wl", [P, 2, FHALF * P], F32R)
        qk = sb("qk", [P, 8, T])
        v = sb("v", [P, NQ, HEADS * P])
        xbc = sb("xbc", [P, 6, T], at=offsets["qk"])
        z = sb("z", [P, 2, T], at=offsets["qk"] + 6 * T * 4)
        xbt = sb("xbt", [P, NQ, 4, P], at=offsets["v"])
        u = sb("u", [P, 2, T])
        pad = sb("pad", [P, 2, 4 + T])
        G = sb("G", [P, 6, T])
        rbc = sb("rbc", [P, T])
        ssum = sb("ssum", [P, T])
        sA, sB, sC, sD = [sb(f"s5{n}", [P, T], at=offsets["mh"] + i * T * 4) for i, n in enumerate("abcd")]
        sE, rotc, rots, s5t = [sb(f"s5{n}", [P, T], at=offsets["ml"] + i * T * 4) for i, n in enumerate("efgh")]
        bmat = sb("bmat", [P, 2, 2, P])
        cmat = sb("cmat", [P, 2, SJ, SH])
        cf = sb("cf", [P, 2, SJ, SH])
        wglu = sb("wglu", [P, 2, 256])
        xds = sb("xds", [P, NQ - 1, M2H, M2P])
        hst = sb("hst", [P, NQ - 1, M2H, M2P])
        rot = sb("rot", [P, 2, SJ, NT])
        par_all = sb("par_all", [P, L, NPAR])
        par = sb("par", [P, NPAR])
        cst = sb("cst", [P, NCONST])
        cbf = sb("cbf", [P, 2, P], BF16)
        wdth = sb("wdth", [P, KD, M2H], F32R)
        wdtl = sb("wdtl", [P, KD, M2H], F32R)
        thh = sb("thh", [P, SJ], F32R)
        s8 = sb("s8", [P, 16, SJ])
        s16 = sb("s16", [P, 12, NQ * M2H])
        rtok = sb("rtok", [P, 2, NQ, 2])
        lamb = sb("lamb", [P, 8])
        soft = sb("soft", [P, 2, 8])
        assert arena_end[0] <= arena_bytes, (arena_end[0], arena_bytes)

        bank = [ctx.enter_context(nc.psum_tensor(f"bank{b}", [P, T], F32)) for b in range(8)]

        def col(name, i=0, n=1):
            return par[:, PARAMS[name][0] + i:PARAMS[name][0] + i + n]

        ident, ones, tri, perm, block1, cap = [cst[:, CONSTS[k]] for k in ("ident", "ones", "tri", "perm", "block", "cap")]
        cosT, sinT, steps = cst[:, CONSTS["cos"]], cst[:, CONSTS["sin"]], cst[:, CONSTS["steps"]]
        eps = cst[:, CONSTS["eps"]]
        adt = s16[:, 3, :]

        bank_free = [sem(f"bank_free{b}") for b in range(8)]
        dve_bank = [sem(f"dve_bank{b}") for b in range(8)]
        act_bank = [sem(f"act_bank{b}") for b in range(8)]
        raw_full, raw_free = [sem(f"raw_full{p}") for p in range(2)], sem("raw_free")
        wh_full, wh_free, wh_low = sem("wh_full"), sem("wh_free"), sem("wh_low")
        wl_full, wl_free = sem("wl_full"), sem("wl_free")
        x_loaded, par_loaded, cst_loaded = sem("x_loaded"), sem("par_loaded"), sem("cst_loaded")
        act_go, pe_go, pool_go = sem("act_go"), sem("pe_go"), sem("pool_go")
        mats_full, mats_free = sem("mats_full"), sem("mats_free")
        out_ready, out_done = sem("out_ready"), sem("out_done")
        dve_own, act_own, pool_own = sem("dve_own"), sem("act_own"), sem("pool_own")
        x_ready = sem("x_ready")
        sq_full, sq_free = sem("sq_full"), sem("sq_free")
        xk_ready, ssum_ready = sem("xk_ready"), sem("ssum_ready")
        rms_ready = sem("rms_ready")
        ask_act, act_says = sem("ask_act"), sem("act_says")
        exp_go, exp_done, osq_go, onorm_done = sem("exp_go"), sem("exp_done"), sem("osq_go"), sem("onorm_done")
        em_full, em_high = sem("em_full"), sem("em_high")
        wdt_ready, adt_ready = sem("wdt_ready"), sem("adt_ready")
        u_ready, s5x_ready, s5x_read = sem("u_ready"), sem("s5x_ready"), sem("s5x_read")
        glu_in = sem("glu_in")
        conv_ready, xbt_ready, hst_ready = sem("conv_ready"), sem("xbt_ready"), sem("hst_ready")
        mix_ready, mix_read, m2sq_ready = sem("mix_ready"), sem("mix_read"), sem("m2sq_ready")
        sqk_ready, qkn_ready = sem("sqk_ready"), sem("qkn_ready")
        v_ready, probs_ready, probsT_ready = sem("v_ready"), sem("probs_ready"), sem("probsT_ready")
        osq_ready = sem("osq_ready")
        mixed_ready, hid_ready = sem("mixed_ready"), sem("hid_ready")
        rot_ready, tab_full, tab_free = sem("rot_ready"), sem("tab_full"), sem("tab_free")

        def linker(eng, own):
            def link(*ins):
                for i in ins:
                    i.then_inc(own, 1)
                eng.wait_ge(own, len(ins)).then_inc(own, -(len(ins)))
            return link

        def say(eng, *sems):
            for s in sems:
                eng.sem_inc(s, 1)

        G_IN, G_OE, G_OL, G_GU, G_DN = (A["w_in"], KD * P), (A["w_oe"], KEARLY * P), (A["w_ol"], HEADS * P), \
            (A["w_gu"], KD * P), (A["w_dn"], FHALF * P)

        blk = ctx.enter_context(nc.Block())

        @blk.sync
        def _(sp):
            for i in range(KD):
                sp.dma_start(x[:, i, :], A["x"][:, i, :]).then_inc(x_loaded, 16)
            sp.dma_start(par_all[:, :, :], A["par"]).then_inc(par_loaded, 16)
            sp.dma_start(cst[:, :], A["cst"]).then_inc(cst_loaded, 16)

            def stream(group, l, first, n):
                src, cols = group
                with sp.Fori(0, n // 2) as i:
                    for p in range(2):
                        sp.wait_ge(raw_free, 1).then_inc(raw_free, -1)
                        sp.dma_start(raw[:, p, 0:cols], src[bass.ds(l, 1), bass.ds(i * 2 + (first + p), 1)]
                                     .rearrange("a b p c -> (a b p) c")).then_inc(raw_full[p], 16)

            with sp.Fori(0, L) as l:
                stream(G_IN, l, 0, 2)
                sp.wait_ge(mats_free, 1).then_inc(mats_free, -1)
                for dst, name in ((bmat, "bmat"), (cmat, "cmat"), (wglu, "wglu")):
                    src = A[name][bass.ds(l, 1)]
                    flat = "p a b c -> p (a b c)" if name != "wglu" else "p a b -> p (a b)"
                    sp.dma_start(dst[:].rearrange(flat), src.rearrange("l p c -> (l p) c")).then_inc(mats_full, 16)
                stream(G_IN, l, 2, NIN - 2)
                stream(G_OE, l, 0, 8)
                stream(G_OL, l, 0, 8)
                for half in range(2):
                    stream(G_GU, l, half * 2 * FHALF, 2 * FHALF)
                    stream(G_DN, l, half * 8, 8)
            sp.wait_ge(out_ready, 1).then_inc(out_ready, -1)
            for i in range(KD):
                sp.dma_start(A["out"][:, i, :], x[:, i, :]).then_inc(out_done, 16)
            sp.wait_ge(out_done, 16 * KD)

        @blk.gpsimd
        def _(pool):
            link = linker(pool, pool_own)

            def low(p, cols):
                pool.wait_ge(wh_low, 1).then_inc(wh_low, -1)
                pool.wait_ge(wl_free, 1).then_inc(wl_free, -1)
                link(nc.gpsimd.tensor_tensor(wl[:, p, 0:cols], raw[:, p, 0:cols], wh[:, p, 0:cols].bitcast(F32),
                                             ALU.subtract))
                say(pool, wl_full, raw_free)

            def lows(cols, n):
                with pool.Fori(0, n // 2):
                    for p in range(2):
                        low(p, cols)

            def table(j):
                if j == 0:
                    pool.wait_ge(rot_ready, 1).then_inc(rot_ready, -1)
                pool.wait_ge(tab_free, 1).then_inc(tab_free, -1)
                shape = [P, COARSE, FINE]
                cc, sc = [rot[:, i, j, FINE:NT].unsqueeze(2).broadcast_to(shape) for i in range(2)]
                cfn, sfn = [rot[:, i, j, 0:FINE].unsqueeze(1).broadcast_to(shape) for i in range(2)]
                c3, s3, t3 = [t[:, :].rearrange("p (a b) -> p a b", a=COARSE) for t in (rotc, rots, s5t)]
                tt = nc.gpsimd.tensor_tensor
                link(tt(c3, cc, cfn, ALU.mult), tt(t3, sc, sfn, ALU.mult))
                link(tt(rotc[:, :], rotc[:, :], s5t[:, :], ALU.subtract), tt(s3, sc, cfn, ALU.mult))
                link(tt(t3, cc, sfn, ALU.mult))
                link(tt(rots[:, :], rots[:, :], s5t[:, :], ALU.add))
                say(pool, tab_full)

            say(pool, raw_free, raw_free, wl_free)
            with pool.Fori(0, L):
                done = 0
                for until, tables in ((12, [0]), (14, [1]), (16, [2, 3]), (18, [4]), (24, [5]), (26, [6]), (28, [7])):
                    lows(KD * P, until - done)
                    done = until
                    for j in tables:
                        table(j)
                lows(KEARLY * P, 8)
                lows(HEADS * P, 8)
                for half in range(2):
                    lows(KD * P, 2 * FHALF)
                    lows(FHALF * P, 8)

        @blk.tensor
        def _(pe):
            mm = nc.tensor.matmul

            def unit(p, K, hi, lo, ready=None):
                pe.wait_ge(wh_full, 1).then_inc(wh_full, -1)
                pe.wait_ge(bank_free[p], 1).then_inc(bank_free[p], -1)
                for k in range(K):
                    if ready is not None:
                        pe.wait_ge(ready, 1).then_inc(ready, -1)
                    w = mm(bank[p][:, :], wh[:, p, k * P:(k + 1) * P], lo[:, k, :], start=(k == 0), stop=False)
                    if k == 0:
                        w.then_inc(wl_free, 1)
                for k in range(K):
                    w = mm(bank[p][:, :], wh[:, p, k * P:(k + 1) * P], hi[:, k, :], start=False, stop=False)
                w.then_inc(wh_free, 1)
                pe.wait_ge(wl_full, 1).then_inc(wl_full, -1)
                for k in range(K):
                    w = mm(bank[p][:, :], wl[:, p, k * P:(k + 1) * P], hi[:, k, :], start=False, stop=(k == K - 1))
                w.then_inc(dve_bank[p], 1)

            def units(n, K, hi, lo, ready=None):
                if ready is not None:
                    unit(0, K, hi, lo, ready)
                    unit(1, K, hi, lo)
                    n -= 2
                with pe.Fori(0, n // 2):
                    unit(0, K, hi, lo)
                    unit(1, K, hi, lo)

            def rms_sum():
                pe.wait_ge(ssum_ready, 1).then_inc(ssum_ready, -1)
                pe.wait_ge(bank_free[7], 1).then_inc(bank_free[7], -1)
                mm(bank[7][:, :], ones, ssum[:, :], start=True, stop=True).then_inc(act_bank[7], 1)

            def token_sums():
                pe.wait_ge(bank_free[6], 1).then_inc(bank_free[6], -1)
                for t in range(NQ):
                    w = mm(bank[6][:, 2 * t:2 * t + 2], ssum[:, t * P:(t + 1) * P], ones[:, 0:2], start=True, stop=True)
                w.then_inc(act_bank[6], 1)

            def dt_columns():
                pe.wait_ge(wdt_ready, 1).then_inc(wdt_ready, -1)
                pe.wait_ge(bank_free[5], 1).then_inc(bank_free[5], -1)
                for t in range(NQ):
                    out = bank[5][:, t * M2H:(t + 1) * M2H]
                    for n, (a, b) in enumerate(((xl, wdth), (xh, wdth), (xh, wdtl))):
                        for k in range(KD):
                            w = mm(out, a[:, k, t * P:(t + 1) * P], b[:, k, :], start=(n == k == 0),
                                   stop=(n == 2 and k == KD - 1))
                w.then_inc(dve_bank[5], 1)

            def s5_in(j):
                if j == 0:
                    pe.wait_ge(u_ready, 1).then_inc(u_ready, -1)
                r = SH * (j % 4)
                for c in range(2):
                    pe.wait_ge(bank_free[2 + c], 1).then_inc(bank_free[2 + c], -1)
                    mm(bank[2 + c][:, :], bmat[r:r + SH, c, j // 4, :],
                       u[r:r + SH, j // 4, :], start=True, stop=True).then_inc(dve_bank[2 + c], 1)

            def s5_out(j):
                r = SH * (j % 4)
                if j % 4 == 0:
                    pe.wait_ge(bank_free[6], 1).then_inc(bank_free[6], -1)
                pe.wait_ge(s5x_ready, 1).then_inc(s5x_ready, -1)
                mm(bank[6][r:r + SH, :], cf[:, 0, j, :], sE[:, :], start=True, stop=False)
                w = mm(bank[6][r:r + SH, :], cf[:, 1, j, :], sA[:, :], start=False, stop=True)
                w.then_inc(s5x_read, 1)

            def s5_glu():
                pe.wait_ge(glu_in, 1).then_inc(glu_in, -1)
                for i in range(2):
                    pe.wait_ge(bank_free[2 + i], 1).then_inc(bank_free[2 + i], -1)
                    for k in range(2):
                        w = mm(bank[2 + i][:, :], wglu[:, k, i * P:(i + 1) * P], u[:, k, :], start=(k == 0), stop=(k == 1))
                    w.then_inc(act_bank[2 + i], 1)

            def m2_chunks():
                pe.wait_ge(adt_ready, 1).then_inc(adt_ready, -1)
                pe.wait_ge(bank_free[7], 1).then_inc(bank_free[7], -1)
                mm(bank[7][:, 0:16], tri, adt, start=True, stop=True)
                mm(bank[7][:, 16:32], ones, adt, start=True, stop=True).then_inc(dve_bank[7], 1)
                pe.wait_ge(conv_ready, 1).then_inc(conv_ready, -1)
                for t in range(NQ):
                    pe.wait_ge(bank_free[4], 1).then_inc(bank_free[4], -1)
                    for i in range(4 if t < NQ - 1 else 2):
                        w = nc.tensor.transpose(bank[4][:, i * P:(i + 1) * P], xbc[:, i, t * P:(t + 1) * P], ident)
                    w.then_inc(dve_bank[4], 1)
                for t in range(NQ - 1):
                    pe.wait_ge(xbt_ready, 1).then_inc(xbt_ready, -1)
                    pe.wait_ge(bank_free[5], 1).then_inc(bank_free[5], -1)
                    for g in range(2):
                        w = mm(bank[5][:, g * P:(g + 1) * P], xbt[:, t, 2 + g, :],
                               xds[:, t, 2 * g:2 * g + 2, :].rearrange("p h c -> p (h c)"), start=True, stop=True)
                    w.then_inc(dve_bank[5], 1)
                pe.wait_ge(xbt_ready, 1).then_inc(xbt_ready, -1)

            def m2_head(h):
                if h % 2 == 0:
                    pe.wait_ge(bank_free[7], 1).then_inc(bank_free[7], -1)
                    for t in range(NQ):
                        c = slice(t * P, (t + 1) * P)
                        w = mm(bank[7][:, c], xbc[:, 2 + h // 2, c], xbc[:, 4 + h // 2, c], start=True, stop=True)
                    w.then_inc(dve_bank[7], 1)
                pe.wait_ge(bank_free[4], 1).then_inc(bank_free[4], -1)
                for t in range(NQ):
                    c = slice(t * P, (t + 1) * P)
                    w = mm(bank[4][:, c], adt[:, t * M2H + h:t * M2H + h + 1].broadcast_to([P, P]), tri, start=True, stop=True)
                w.then_inc(dve_bank[4], 1)

            def m2_apply(h):
                pe.wait_ge(mix_ready, 1).then_inc(mix_ready, -1)
                if h == 0:
                    pe.wait_ge(hst_ready, 1).then_inc(hst_ready, -1)
                if h % 2 == 0:
                    pe.wait_ge(bank_free[5], 1).then_inc(bank_free[5], -1)
                r = slice(M2P * (h % 2), M2P * (h % 2) + M2P)
                for t in range(NQ):
                    c = slice(t * P, (t + 1) * P)
                    w = mm(bank[5][r, c], xbt[:, t, h // 2, r], G[:, 1, c], start=True, stop=(t == 0))
                    if t > 0:
                        w = mm(bank[5][r, c], hst[:, t - 1, h, :], G[:, 2, c], start=False, stop=True)
                w.then_inc(mix_read, 1)

            def m2_norm():
                pe.wait_ge(bank_free[7], 1).then_inc(bank_free[7], -1)
                for i in range(2):
                    pe.wait_ge(m2sq_ready, 1).then_inc(m2sq_ready, -1)
                    w = mm(bank[7][:, :], ones, G[:, 3 + i, :], start=(i == 0), stop=(i == 1))
                w.then_inc(act_bank[7], 1)

            def qk_mean():
                pe.wait_ge(sqk_ready, 1).then_inc(sqk_ready, -1)
                pe.wait_ge(bank_free[4], 1).then_inc(bank_free[4], -1)
                return mm(bank[4][:, :], block1, G[:, 2, :], start=True, stop=True).then_inc(act_bank[4], 1)

            def qk_turn(t):
                pe.wait_ge(qkn_ready, 1).then_inc(qkn_ready, -1)
                pe.wait_ge(bank_free[5], 1).then_inc(bank_free[5], -1)
                mm(bank[5][:, :], perm, qk[:, bass.ds(t, 1), :].rearrange("p a b -> p (a b)"),
                   start=True, stop=True).then_inc(dve_bank[5], 1)

            def values():
                banks = (0, 1, 2, 3)
                for b in banks:
                    pe.wait_ge(bank_free[b], 1).then_inc(bank_free[b], -1)
                for n in range(4):
                    p = n % 2
                    pe.wait_ge(wh_full, 1).then_inc(wh_full, -1)
                    pe.wait_ge(wl_full, 1).then_inc(wl_full, -1)
                    for a, w8, m in ((xl, wh, 0), (xh, wh, 1), (xh, wl, 2)):
                        for t in range(NQ):
                            for j in range(2):
                                k = 2 * n + j
                                w = mm(bank[t][:, :], a[:, k, t * P:(t + 1) * P], w8[:, p, j * T:(j + 1) * T],
                                       start=(n == m == j == 0), stop=(n == 3 and m == 2 and j == 1))
                                if m == t == j == 0:
                                    w.then_inc(wl_free, 1)
                                if n == 3 and m == 2 and j == 1:
                                    w.then_inc(dve_bank[t], 1)
                        if m == 1:
                            w.then_inc(wh_free, 1)

            def scores(n):
                h, q = n // NQ, n % NQ
                for c in range(2):
                    b = (2, 3, 6, 7)[2 * (n % 2) + c]
                    pe.wait_ge(bank_free[b], 1).then_inc(bank_free[b], -1)
                    r = slice(QK * c, QK * c + QK)
                    qs, last = qk[r, 2 * h, q * P:(q + 1) * P], slice(q * P, (q + 1) * P)
                    if q:
                        mm(bank[b][:, 0:q * P], qs, qk[r, 2 * h + 1, 0:q * P], start=True, stop=True)
                    mm(bank[b][:, last], qs, qk[r, 2 * h + 1, last], start=True, stop=False)
                    mm(bank[b][:, last], cbf[:, 0, :], cbf[:, 1, :], start=False, stop=True).then_inc(dve_bank[b], 1)

            def turn(n):
                pe.wait_ge(probs_ready, 1).then_inc(probs_ready, -1)
                pe.wait_ge(bank_free[4], 1).then_inc(bank_free[4], -1)
                for k in range(n % NQ + 1):
                    w = nc.tensor.transpose(bank[4][:, k * P:(k + 1) * P], G[:, 2 * (n % 2), k * P:(k + 1) * P], ident)
                w.then_inc(act_bank[4], 1)

            def attend(n):
                h, q = n // NQ, n % NQ
                if q == 0:
                    pe.wait_ge(bank_free[5], 1).then_inc(bank_free[5], -1)
                pe.wait_ge(probsT_ready, 1).then_inc(probsT_ready, -1)
                for k in range(q + 1):
                    w = mm(bank[5][:, q * P:(q + 1) * P], v[:, k, h * P:(h + 1) * P], G[:, 4 + n % 2, k * P:(k + 1) * P],
                           start=(k == 0), stop=(k == q))
                if q == NQ - 1:
                    w.then_inc(dve_bank[5], 1)

            def head_sum():
                pe.wait_ge(osq_ready, 1).then_inc(osq_ready, -1)
                pe.wait_ge(bank_free[1], 1).then_inc(bank_free[1], -1)
                mm(bank[1][:, :], ones, pad[:, 0, 4:4 + T], start=True, stop=True).then_inc(act_bank[1], 1)

            pe.wait_ge(pe_go, 1).then_inc(pe_go, -1)
            with pe.Fori(0, L):
                unit(0, KD, xh, xl, xk_ready)
                rms_sum()
                token_sums()
                unit(1, KD, xh, xl)
                dt_columns()
                units(8, KD, xh, xl)
                m2_chunks()
                units(2, KD, xh, xl)
                s5_in(0)
                m2_head(0)
                units(2, KD, xh, xl)
                s5_out(0)
                m2_apply(0)
                s5_in(1)
                m2_head(1)
                units(2, KD, xh, xl)
                s5_out(1)
                m2_apply(1)
                for j in (2, 3):
                    s5_in(j)
                    m2_head(j)
                    s5_out(j)
                    m2_apply(j)
                m2_norm()
                unit(0, KD, xh, xl)
                unit(1, KD, xh, xl)
                qk_mean()
                with pe.Fori(0, 3) as t:
                    for p in range(2):
                        unit(p, KD, xh, xl)
                        qk_mean()
                        qk_turn(t * 2 + p)
                qk_mean()
                qk_turn(6)
                qk_turn(7)
                s5_in(4)
                s5_out(4)
                s5_in(5)
                s5_out(5)
                values()
                s5_in(6)
                s5_out(6)
                s5_in(7)
                s5_out(7)
                s5_glu()
                pe.wait_ge(v_ready, 1).then_inc(v_ready, -1)
                scores(0)
                for n in range(4 * HEADS):
                    if n + 1 < 4 * HEADS:
                        scores(n + 1)
                    turn(n)
                    if n == 0:
                        for _ in range(KEARLY):
                            pe.wait_ge(mixed_ready, 1).then_inc(mixed_ready, -1)
                    if n % 2 == 0:
                        unit(n // 2 % 2, KEARLY, mh[:, MIXB:MIXED, :], ml[:, MIXB:MIXED, :])
                    attend(n)
                    if n >= NQ and n % NQ == 0:
                        head_sum()
                head_sum()
                units(8, HEADS, mh, ml, mixed_ready)
                unit(0, KD, xh, xl, xk_ready)
                rms_sum()
                unit(1, KD, xh, xl)
                units(2 * FHALF - 2, KD, xh, xl)
                units(8, FHALF, mh, ml, hid_ready)
                units(2 * FHALF, KD, xh, xl)
                units(8, FHALF, mh, ml, hid_ready)

        @blk.scalar
        def _(act):
            link = linker(act, act_own)
            fn = nc.scalar.activation

            def prep(p, cols):
                act.wait_ge(raw_full[p], 16).then_inc(raw_full[p], -16)
                act.wait_ge(wh_free, 1).then_inc(wh_free, -1)
                link(fn(wh[:, p, 0:cols], raw[:, p, 0:cols], ACT.Copy))
                say(act, wh_full, wh_low)

            def preps(n, cols):
                with act.Fori(0, n // 2):
                    prep(0, cols)
                    prep(1, cols)

            def inputs(gain):
                act.wait_ge(x_ready, 1).then_inc(x_ready, -1)
                for k in range(KD):
                    act.wait_ge(sq_free, 1).then_inc(sq_free, -1)
                    link(fn(G[:, k % 2, :], x[:, k, :], ACT.Square),
                         fn(xh[:, k, :], x[:, k, :], ACT.Copy, scale=col(gain, k)))
                    say(act, sq_full)

            def rsqrt_mean(out, in_, n):
                link(fn(out, in_, ACT.Ln, scale=1.0 / n, bias=eps))
                link(fn(out, out, ACT.Exp, scale=-0.5))

            def rms():
                act.wait_ge(act_bank[7], 1).then_inc(act_bank[7], -1)
                rsqrt_mean(rbc[:, :], bank[7][:, :], D)
                say(act, bank_free[7])

            def high(dst, src):
                link(fn(dst, src, ACT.Copy))

            def emit(tile, buf):
                act.wait_ge(em_full, 1).then_inc(em_full, -1)
                high(mh[:, tile, :], buf)
                say(act, em_high)

            say(act, wh_free, wh_free)
            act.wait_ge(act_go, 1).then_inc(act_go, -1)
            with act.Fori(0, L):
                prep(0, KD * P)
                prep(1, KD * P)
                inputs("g1")
                link(fn(s16[:, 8, 0:M2H], col("alog", 0, M2H), ACT.Exp),
                     fn(lamb[:, 2:4], lamb[:, 0:2], ACT.Exp))
                prep(0, KD * P)
                rms()
                act.wait_ge(act_bank[6], 1).then_inc(act_bank[6], -1)
                rt = rtok[:, 0].rearrange("p a b -> p (a b)")
                rsqrt_mean(rt, bank[6][:, 0:2 * NQ], D)
                say(act, bank_free[6], rms_ready)
                prep(1, KD * P)
                act.wait_ge(ask_act, 1).then_inc(ask_act, -1)
                link(fn(s16[:, 1, :], s16[:, 1, :], ACT.Exp, scale=-1.0))
                say(act, act_says)
                for i in range(6):
                    prep(i % 2, KD * P)
                    act.wait_ge(ask_act, 1).then_inc(ask_act, -1)
                    link(fn(xbc[:, i, :], G[:, i % 2, :], ACT.Silu))
                    say(act, act_says)
                for i in range(2):
                    prep(i, KD * P)
                    act.wait_ge(ask_act, 1).then_inc(ask_act, -1)
                    link(fn(z[:, i, :], z[:, i, :], ACT.Silu))
                    say(act, act_says)
                act.wait_ge(ask_act, 1).then_inc(ask_act, -1)
                link(fn(s8[:, 0, :], col("ldt", 0, SJ), ACT.Exp))
                say(act, act_says)
                act.wait_ge(ask_act, 1).then_inc(ask_act, -1)
                link(fn(rot[:, 1].rearrange("p a b -> p (a b)"), sA[:, 0:SJ * NT], ACT.Sin),
                     fn(sB[:, 0:SJ * NT], sA[:, 0:SJ * NT], ACT.Sin, scale=0.5))
                say(act, act_says)
                act.wait_ge(ask_act, 1).then_inc(ask_act, -1)
                link(fn(s16[:, 6, :], s16[:, 6, :], ACT.Exp), fn(s16[:, 7, :], s16[:, 5, :], ACT.Exp))
                say(act, act_says)

                def m2_head():
                    act.wait_ge(ask_act, 1).then_inc(ask_act, -1)
                    link(fn(G[:, 1, :], G[:, 1, :], ACT.Exp), fn(G[:, 2, :], bank[4][:, :], ACT.Exp))
                    say(act, bank_free[4], act_says)

                def m2_square(i):
                    act.wait_ge(ask_act, 1).then_inc(ask_act, -1)
                    link(fn(G[:, 3 + i, :], xbc[:, i, :], ACT.Square))
                    say(act, m2sq_ready)

                preps(2, KD * P)
                m2_head()
                preps(2, KD * P)
                m2_head()
                preps(2, KD * P)
                for i in range(2):
                    emit(MIXB + i, G[:, 4 + i, :])
                m2_square(0)
                m2_head()
                m2_head()
                m2_square(1)
                act.wait_ge(act_bank[7], 1).then_inc(act_bank[7], -1)
                rsqrt_mean(G[:, 5, :], bank[7][:, :], 2 * P)
                say(act, bank_free[7], act_says)
                for i in range(2):
                    emit(MIXD + i, G[:, 3 + i, :])
                act.wait_ge(ask_act, 1).then_inc(ask_act, -1)
                link(fn(u[:, 0, :], u[:, 0, :], ACT.Gelu_apprx_tanh))
                say(act, act_says)
                with act.Fori(0, 4):
                    for p in range(2):
                        prep(p, KD * P)
                        act.wait_ge(ask_act, 1).then_inc(ask_act, -1)
                        link(fn(G[:, 2, :], G[:, p, :], ACT.Square))
                        say(act, sqk_ready)
                        act.wait_ge(act_bank[4], 1).then_inc(act_bank[4], -1)
                        rsqrt_mean(G[:, 3 + p, :], bank[4][:, :], QK)
                        say(act, bank_free[4], act_says)
                preps(2, KD * P)
                preps(2, KEARLY * P)
                act.wait_ge(ask_act, 1).then_inc(ask_act, -1)
                link(fn(u[:, 1, :], u[:, 1, :], ACT.Gelu_apprx_tanh))
                say(act, act_says)
                for i in range(2):
                    act.wait_ge(act_bank[2 + i], 1).then_inc(act_bank[2 + i], -1)
                    link(fn(G[:, 1 + i, :], bank[2 + i][:, :], ACT.Sigmoid, bias=col("bglu", i)))
                    say(act, bank_free[2 + i], act_says)
                for i in range(2):
                    emit(MIXC + i, G[:, 3 + i, :])

                def exps(n):
                    w, s = (n % NQ + 1) * P, n % 2
                    act.wait_ge(exp_go, 1).then_inc(exp_go, -1)
                    link(*[fn(G[:, 2 * s + c, 0:w], bank[(2, 3, 6, 7)[2 * s + c]][:, 0:w], ACT.Exp,
                              bias=soft[:, s, c:c + 1], accum_out=soft[:, s, 2 + c:3 + c]) for c in range(2)])
                    say(act, bank_free[(2, 6)[s]], bank_free[(3, 7)[s]], exp_done)

                def head_square():
                    act.wait_ge(osq_go, 1).then_inc(osq_go, -1)
                    link(fn(pad[:, 0, 4:4 + T], ssum[:, :], ACT.Square))
                    say(act, osq_ready)

                def head_rms():
                    act.wait_ge(act_bank[1], 1).then_inc(act_bank[1], -1)
                    rsqrt_mean(rbc[:, :], bank[1][:, :], P)
                    say(act, bank_free[1], onorm_done)

                exps(0)
                for n in range(4 * HEADS):
                    if n >= NQ and n % NQ == 0:
                        head_square()
                    if n > NQ and n % NQ == 1:
                        head_rms()
                    if n + 1 < 4 * HEADS:
                        exps(n + 1)
                    act.wait_ge(act_bank[4], 1).then_inc(act_bank[4], -1)
                    w = (n % NQ + 1) * P
                    link(fn(G[:, 4 + n % 2, 0:w], bank[4][:, 0:w], ACT.Copy))
                    say(act, bank_free[4], probsT_ready)
                    if n % 2 == 0:
                        prep(n // 2 % 2, (KEARLY if n < 12 else HEADS) * P)
                    if n > NQ and n % NQ == 1:
                        emit(MIXA + n // NQ - 1, ssum[:, :])
                head_square()
                head_rms()
                emit(MIXA + HEADS - 1, ssum[:, :])
                preps(6, HEADS * P)
                preps(2, KD * P)
                inputs("g2")
                prep(0, KD * P)
                rms()
                say(act, rms_ready)

                def ffn_tile(i, cols, first):
                    if not first:
                        prep(0, cols)
                    act.wait_ge(ask_act, 1).then_inc(ask_act, -1)
                    link(fn(G[:, 1, :], G[:, 0, :], ACT.Silu))
                    say(act, act_says)
                    prep(1, cols)
                    act.wait_ge(ask_act, 1).then_inc(ask_act, -1)
                    high(mh[:, bass.ds(i, 1), :].rearrange("p a b -> p (a b)"), G[:, 3, :])
                    say(act, act_says)

                for half in range(2):
                    ffn_tile(0, KD * P, half == 0)
                    with act.Fori(1, FHALF - 1) as i:
                        ffn_tile(i, KD * P, False)
                    ffn_tile(FHALF - 1, FHALF * P, False)
                    preps(6, FHALF * P)
                    if half == 0:
                        preps(2, KD * P)

        @blk.vector
        def _(dve):
            link = linker(dve, dve_own)
            tt, ts, stt = nc.vector.tensor_tensor, nc.vector.tensor_scalar, nc.vector.scalar_tensor_tensor
            copy = nc.vector.tensor_copy
            MUL, ADD, SUB = ALU.mult, ALU.add, ALU.subtract

            def flat(ap):
                return ap.rearrange("p a b -> p (a b)")

            def inputs(gain):
                link(nc.vector.memset(ssum[:, :], 0.0))
                say(dve, x_ready)
                for k in range(KD):
                    dve.wait_ge(sq_full, 1).then_inc(sq_full, -1)
                    link(stt(xl[:, k, :], x[:, k, :], col(gain, k), xh[:, k, :].bitcast(F32), MUL, SUB),
                         tt(ssum[:, :], ssum[:, :], G[:, k % 2, :], ADD))
                    say(dve, xk_ready, sq_free)
                say(dve, ssum_ready)

            def scaled(out, p):
                dve.wait_ge(dve_bank[p], 1).then_inc(dve_bank[p], -1)
                link(tt(out, bank[p][:, :], rbc[:, :], MUL))
                say(dve, bank_free[p])

            def taps(out, p, weights, first, bias=None):
                n = len(weights)
                if bias is None:
                    link(ts(out, pad[:, p, 4:4 + T], weights[n - 1], None, MUL))
                else:
                    link(ts(out, pad[:, p, 4:4 + T], weights[n - 1], bias, MUL, ADD))
                for k in range(1, n):
                    link(stt(out, pad[:, p, 4 - k:4 - k + T], weights[n - 1 - k], out, MUL, ADD))

            def emit(tile, buf):
                say(dve, em_full)
                dve.wait_ge(em_high, 1).then_inc(em_high, -1)
                link(tt(ml[:, tile, :], buf, mh[:, tile, :].bitcast(F32), SUB))
                say(dve, mixed_ready)

            def residual(o, p):
                dve.wait_ge(dve_bank[p], 1).then_inc(dve_bank[p], -1)
                xo = flat(x[:, bass.ds(o, 1), :])
                link(tt(xo, xo, bank[p][:, :], ADD))
                say(dve, bank_free[p])

            def residuals():
                with dve.Fori(0, KD // 2) as o:
                    residual(o * 2, 0)
                    residual(o * 2 + 1, 1)

            def parameters(l):
                link(copy(par[:, :], flat(par_all[:, bass.ds(l, 1), :])))
                w = par[:, PARAMS["wdt"][0]:PARAMS["wdt"][0] + KD * M2H]
                dal = col("dal", 0, 4 * QK).rearrange("p (a b c) -> p a b c", a=2, b=2)
                prod = G[:, 5, 0:2 * QK].rearrange("p (a c) -> p a c", a=2)
                link(copy(flat(wdth[:]), w),
                     ts(col("qkg"), col("qkg"), QK ** -0.5, None, MUL),
                     ts(col("subg"), col("subg"), col("oneml"), None, MUL),
                     tt(prod, dal[:, :, 0, :], dal[:, :, 1, :], MUL))
                link(tt(flat(wdtl[:]), w, flat(wdth[:]).bitcast(F32), SUB),
                     nc.vector.tensor_reduce(lamb[:, 0:2], prod, AX, ADD))
                say(dve, wdt_ready)

            def minus_lambda():
                link(tt(lamb[:, 4:5], lamb[:, 3:4], lamb[:, 2:3], SUB))
                link(tt(lamb[:, 4:5], lamb[:, 4:5], col("linit"), SUB))

            def m2_dt():
                a, e, s, sq, q, rec = [s16[:, i, :] for i in (0, 1, 2, 9, 10, 11)]
                by_head = [P, NQ, M2H]
                dve.wait_ge(dve_bank[5], 1).then_inc(dve_bank[5], -1)
                link(tt(a.rearrange("p (a b) -> p a b", a=NQ), bank[5][:, 0:16].rearrange("p (a b) -> p a b", a=NQ),
                        rtok[:, 0, :, 0:1].broadcast_to(by_head), MUL))
                say(dve, bank_free[5])
                link(tt(a.rearrange("p (a b) -> p a b", a=NQ), a.rearrange("p (a b) -> p a b", a=NQ),
                        col("dtb", 0, M2H).unsqueeze(1).broadcast_to(by_head), ADD))
                link(stt(e, a, -1.0, a, MUL, ALU.max))
                say(dve, ask_act)
                link(ts(a, a, 0.0, None, ALU.max))
                dve.wait_ge(act_says, 1).then_inc(act_says, -1)
                link(ts(rec, e, 2.0, None, ADD))
                link(nc.vector.reciprocal(rec, rec))
                link(tt(s, e, rec, MUL))
                link(tt(sq, s, s, MUL))
                link(ts(q, sq, 1.0 / 17, None, MUL))
                for c in (15, 13, 11, 9, 7, 5, 3):
                    link(stt(q, q, 1.0 / c, sq, ADD, MUL))
                link(stt(q, q, 1.0, s, ADD, MUL))
                link(stt(a, q, 2.0, a, MUL, ADD))
                link(stt(adt.rearrange("p (a b) -> p a b", a=NQ), a.rearrange("p (a b) -> p a b", a=NQ), -1.0,
                         s16[:, 8, 0:M2H].unsqueeze(1).broadcast_to(by_head), MUL, MUL))
                say(dve, adt_ready)

            def reduced(ph, extra, k):
                if extra is not None:
                    link(tt(k, ph, extra, ADD))
                link(ts(k, ph if extra is None else k, INV2PI, ROUND, MUL, ADD))
                link(ts(k, k, ROUND, None, SUB))
                for c in (C1, C2, C3):
                    link(stt(ph, k, -c, ph, MUL, ADD))
                if extra is not None:
                    link(tt(ph, ph, extra, ADD))

            def s5_parameters():
                dt, r, F, rho, th, thl, nre, nim, m2, inv, a, b, c, d, k = [s8[:, i, :] for i in range(15)]
                lre, lim = col("lre", 0, SJ), col("lim", 0, SJ)
                say(dve, ask_act)
                dve.wait_ge(act_says, 1).then_inc(act_says, -1)
                link(tt(r, lre, dt, MUL), tt(th, lim, dt, MUL))
                link(ts(r, r, -100.0, 1.0 / 1024, ALU.max, MUL))
                link(ts(F, r, 1.0 / 5, 1.0, MUL, ADD))
                for n in (4, 3, 2):
                    link(tt(F, F, r, MUL))
                    link(ts(F, F, 1.0 / n, 1.0, MUL, ADD))
                link(tt(F, F, r, MUL))
                for _ in range(10):
                    link(stt(F, F, 2.0, F, ADD, MUL))
                link(ts(rho, F, 1.0, None, ADD))
                reduced(th, None, k)
                link(copy(thh[:, :], th))
                link(tt(thl, th, thh[:, :].bitcast(F32), SUB))
                shape = [P, SJ, NT]
                ph, kk, lo = [t[:, 0:SJ * NT] for t in (sA, sB, sC)]
                ph3, lo3, kk3 = [t.rearrange("p (a b) -> p a b", a=SJ) for t in (ph, lo, kk)]
                st3 = steps.unsqueeze(1).broadcast_to(shape)
                link(tt(ph3, thh[:, :].bitcast(F32).unsqueeze(2).broadcast_to(shape), st3, MUL),
                     tt(lo3, thl.unsqueeze(2).broadcast_to(shape), st3, MUL))
                reduced(ph, lo, kk)
                link(ts(ph, ph, PI_CAP, -PI_CAP, ALU.min, ALU.max))
                say(dve, ask_act)
                link(tt(m2, lre, lre, MUL), tt(a, lim, lim, MUL))
                link(tt(m2, m2, a, ADD))
                link(nc.vector.reciprocal(inv, m2))
                dve.wait_ge(act_says, 1).then_inc(act_says, -1)
                link(tt(lo, kk, kk, MUL))
                link(ts(flat(rot[:, 0]), lo, -2.0, 1.0, MUL, ADD))
                say(dve, rot_ready)
                link(tt(nre, F, rot[:, 0, :, 1], MUL), stt(nim, F, 1.0, rot[:, 1, :, 1], ADD, MUL))
                link(stt(nre, lo3[:, :, 1], -2.0, nre, MUL, ADD))
                link(tt(a, nre, lre, MUL), tt(b, nim, lim, MUL), tt(c, nim, lre, MUL), tt(d, nre, lim, MUL))
                link(tt(a, a, b, ADD), tt(c, c, d, SUB))
                link(tt(a, a, inv, MUL), tt(c, c, inv, MUL))
                cs = [P, SJ, SH]
                A3, B3, C3_, D3 = [t[:, 0:SJ * SH].rearrange("p (a b) -> p a b", a=SJ) for t in (sA, sB, sC, sD)]
                fre, fim = a.unsqueeze(2).broadcast_to(cs), c.unsqueeze(2).broadcast_to(cs)
                link(tt(A3, cmat[:, 0], fre, MUL), tt(B3, cmat[:, 1], fim, MUL),
                     tt(C3_, cmat[:, 0], fim, MUL), tt(D3, cmat[:, 1], fre, MUL))
                link(tt(cf[:, 0], A3, B3, SUB), tt(C3_, C3_, D3, ADD))
                link(ts(cf[:, 1], C3_, -1.0, None, MUL))

            def s5(j):
                cs, sn = rotc[:, :], rots[:, :]
                a, b, c, d, e = sA[:, :], sB[:, :], sC[:, :], sD[:, :], sE[:, :]
                if j % 4:
                    dve.wait_ge(s5x_read, 1).then_inc(s5x_read, -1)
                dve.wait_ge(tab_full, 1).then_inc(tab_full, -1)
                dve.wait_ge(dve_bank[2], 1).then_inc(dve_bank[2], -1)
                dve.wait_ge(dve_bank[3], 1).then_inc(dve_bank[3], -1)
                link(tt(a, bank[2][:, :], cs, MUL), tt(b, bank[3][:, :], sn, MUL),
                     tt(c, bank[3][:, :], cs, MUL), tt(d, bank[2][:, :], sn, MUL))
                say(dve, bank_free[2], bank_free[3])
                link(tt(a, a, b, ADD), tt(c, c, d, SUB))
                rho = s8[:, 3, j:j + 1].broadcast_to([P, T])
                link(nc.vector.tensor_tensor_scan(b, rho, a, 0.0, MUL, ADD),
                     nc.vector.tensor_tensor_scan(d, rho, c, 0.0, MUL, ADD))
                link(tt(a, b, cs, MUL), tt(c, d, sn, MUL))
                link(tt(e, a, c, SUB))
                link(tt(a, b, sn, MUL), tt(c, d, cs, MUL))
                say(dve, tab_free)
                link(tt(a, a, c, ADD))
                say(dve, s5x_ready)

            def s5_finish(i):
                dve.wait_ge(s5x_read, 1).then_inc(s5x_read, -1)
                link(stt(u[:, i, :], u[:, i, :], col("s5d", i), bank[6][:, :], MUL, ADD))
                say(dve, bank_free[6], ask_act)

            def m2_chunks():
                dve.wait_ge(dve_bank[7], 1).then_inc(dve_bank[7], -1)
                link(copy(flat(s16[:, 4:6, :]), bank[7][:, 0:32]))
                say(dve, bank_free[7])
                link(tt(s16[:, 6, :], s16[:, 5, :], s16[:, 4, :], SUB))
                say(dve, ask_act)
                dve.wait_ge(act_says, 1).then_inc(act_says, -1)
                hs = [P, M2H, M2P]
                for t in range(NQ):
                    hc = slice(t * M2H, (t + 1) * M2H)
                    dve.wait_ge(dve_bank[4], 1).then_inc(dve_bank[4], -1)
                    xdt = xbt[:, t, 0:2, :].rearrange("p a b -> p (a b)").rearrange("p (h c) -> p h c", h=M2H)
                    w = [tt(xdt, bank[4][:, 0:2 * P].rearrange("p (h c) -> p h c", h=M2H),
                            s16[:, 0, hc].unsqueeze(2).broadcast_to(hs), MUL)]
                    if t < NQ - 1:
                        w.append(copy(flat(xbt[:, t, 2:4, :]), bank[4][:, 2 * P:4 * P]))
                    link(*w)
                    say(dve, bank_free[4])
                    if t < NQ - 1:
                        link(tt(xds[:, t], xdt, s16[:, 6, hc].unsqueeze(2).broadcast_to(hs), MUL))
                    say(dve, xbt_ready)
                for t in range(NQ - 1):
                    dve.wait_ge(dve_bank[5], 1).then_inc(dve_bank[5], -1)
                    st = bank[5][:, 0:2 * P].rearrange("p (h c) -> p h c", h=M2H)
                    if t == 0:
                        link(copy(hst[:, 0], st))
                    else:
                        cd = s16[:, 7, t * M2H:(t + 1) * M2H].unsqueeze(2).broadcast_to(hs)
                        link(tt(hst[:, t], hst[:, t - 1], cd, MUL))
                        link(tt(hst[:, t], hst[:, t], st, ADD))
                    say(dve, bank_free[5])
                say(dve, hst_ready)

            def m2_head(h):
                dve.wait_ge(dve_bank[4], 1).then_inc(dve_bank[4], -1)
                link(*[stt(G[:, 1, t * P:(t + 1) * P], bank[4][:, t * P:(t + 1) * P],
                           s16[:, 4, t * M2H + h:t * M2H + h + 1], cap, SUB, ALU.min) for t in range(NQ)])
                say(dve, ask_act)
                dve.wait_ge(act_says, 1).then_inc(act_says, -1)
                if h % 2 == 0:
                    dve.wait_ge(dve_bank[7], 1).then_inc(dve_bank[7], -1)
                link(tt(G[:, 2, :], G[:, 2, :], xbc[:, 4 + h // 2, :], MUL), tt(G[:, 1, :], G[:, 1, :], bank[7][:, :], MUL))
                if h % 2:
                    say(dve, bank_free[7])
                say(dve, mix_ready)

            def m2_pair(i):
                link(stt(xbc[:, i, :], xbc[:, i, :], col("m2d", i), bank[5][:, :], MUL, ADD))
                say(dve, bank_free[5])
                link(tt(xbc[:, i, :], xbc[:, i, :], z[:, i, :], MUL))
                say(dve, ask_act)

            def sc_gate(i):
                scaled(G[:, 0, :], i)
                link(tt(G[:, 4 + i, :], G[:, 0, :], G[:, 4 + i, :], MUL))
                emit(MIXB + i, G[:, 4 + i, :])

            def qk_normed(t, p):
                dve.wait_ge(act_says, 1).then_inc(act_says, -1)
                link(stt(flat(qk[:, bass.ds(t, 1), :]), G[:, p, :], col("qkg", p), G[:, 3 + p, :], MUL, MUL))
                say(dve, qkn_ready)

            def qk_turned(t):
                dve.wait_ge(dve_bank[5], 1).then_inc(dve_bank[5], -1)
                q = flat(qk[:, bass.ds(t, 1), :])
                link(tt(G[:, 5, :], bank[5][:, :], sinT, MUL), tt(q, q, cosT, MUL))
                say(dve, bank_free[5])
                link(tt(q, q, G[:, 5, :], ADD))

            def qk_raw(p):
                scaled(G[:, p, :], p)
                say(dve, ask_act)

            def maxima(n):
                s, w = n % 2, (n % NQ + 1) * P
                banks = (2, 3, 6, 7)[2 * s:2 * s + 2]
                for b in banks:
                    dve.wait_ge(dve_bank[b], 1).then_inc(dve_bank[b], -1)
                link(*[nc.vector.tensor_reduce(soft[:, s, c:c + 1], bank[b][:, 0:w], AX, ALU.max, negate=True)
                       for c, b in enumerate(banks)])
                say(dve, exp_go)

            def combine(n):
                s, w = n % 2, (n % NQ + 1) * P
                dve.wait_ge(exp_done, 1).then_inc(exp_done, -1)
                link(nc.vector.reciprocal(soft[:, s, 4:6], soft[:, s, 2:4]))
                link(ts(soft[:, s, 5:6], soft[:, s, 5:6], lamb[:, 4:5], None, MUL))
                link(ts(G[:, 2 * s + 1, 0:w], G[:, 2 * s + 1, 0:w], soft[:, s, 5:6], None, MUL))
                link(stt(G[:, 2 * s, 0:w], G[:, 2 * s, 0:w], soft[:, s, 4:5], G[:, 2 * s + 1, 0:w], MUL, ADD))
                say(dve, probs_ready)

            def head_out():
                dve.wait_ge(dve_bank[5], 1).then_inc(dve_bank[5], -1)
                link(copy(ssum[:, :], bank[5][:, :]))
                say(dve, bank_free[5], osq_go)

            def head_emit(h):
                dve.wait_ge(onorm_done, 1).then_inc(onorm_done, -1)
                link(stt(ssum[:, :], ssum[:, :], col("subg"), rbc[:, :], MUL, MUL))
                emit(MIXA + h, ssum[:, :])

            def ffn_tile(half, i):
                scaled(pad[:, 0, 4:4 + T], 0)
                w0 = PARAMS["ffw"][0] + half * FHALF * 3
                taps(G[:, 0, :], 0, [par[:, bass.ds(i * 3 + (w0 + k), 1)] for k in range(3)], 0)
                say(dve, ask_act)
                scaled(G[:, 2, :], 1)
                dve.wait_ge(act_says, 1).then_inc(act_says, -1)
                link(tt(G[:, 3, :], G[:, 1, :], G[:, 2, :], MUL))
                say(dve, ask_act)
                dve.wait_ge(act_says, 1).then_inc(act_says, -1)
                link(tt(flat(ml[:, bass.ds(i, 1), :]), G[:, 3, :], flat(mh[:, bass.ds(i, 1), :]).bitcast(F32), SUB))
                say(dve, hid_ready)

            link(nc.vector.memset(pad[:, :, :], 0.0))
            say(dve, *bank_free, tab_free, sq_free, sq_free, mats_free)
            dve.wait_ge(x_loaded, 16 * KD).then_inc(x_loaded, -(16 * KD))
            dve.wait_ge(par_loaded, 16).then_inc(par_loaded, -16)
            dve.wait_ge(cst_loaded, 16).then_inc(cst_loaded, -16)
            link(copy(cbf[:, 0, :], ident), copy(cbf[:, 1, :], cst[:, CONSTS["mask"]]))
            say(dve, act_go, pe_go)
            with dve.Fori(0, L) as l:
                parameters(l)
                inputs("g1")
                dve.wait_ge(rms_ready, 1).then_inc(rms_ready, -1)
                minus_lambda()
                for i in range(2):
                    scaled(u[:, i, :], i)
                dve.wait_ge(mats_full, 48).then_inc(mats_full, -48)
                say(dve, u_ready)
                m2_dt()
                for i in range(6):
                    scaled(pad[:, i % 2, 4:4 + T], i % 2)
                    if i >= 2:
                        dve.wait_ge(act_says, 1).then_inc(act_says, -1)
                    taps(G[:, i % 2, :], i % 2, [col("m2w", 4 * i + k) for k in range(4)], 0, col("m2b", i))
                    say(dve, ask_act)
                for i in range(2):
                    scaled(z[:, i, :], i)
                    dve.wait_ge(act_says, 1).then_inc(act_says, -1)
                    say(dve, ask_act)
                say(dve, conv_ready)
                for i in range(2):
                    dve.wait_ge(act_says, 1).then_inc(act_says, -1)
                s5_parameters()
                m2_chunks()
                for i in range(2):
                    scaled(G[:, 4 + i, :], i)
                s5(0)
                m2_head(0)
                for i in range(2):
                    scaled(pad[:, i, 4:4 + T], i)
                    link(tt(pad[:, i, 4:4 + T], pad[:, i, 4:4 + T], G[:, 4 + i, :], MUL))
                    taps(G[:, 4 + i, :], i, [col("scw", 3 * i + k) for k in range(3)], 0)
                s5(1)
                dve.wait_ge(mix_read, 1).then_inc(mix_read, -1)
                m2_head(1)
                for i in range(2):
                    sc_gate(i)
                s5(2)
                dve.wait_ge(mix_read, 1).then_inc(mix_read, -1)
                m2_pair(0)
                m2_head(2)
                s5(3)
                dve.wait_ge(mix_read, 1).then_inc(mix_read, -1)
                m2_head(3)
                dve.wait_ge(mix_read, 1).then_inc(mix_read, -1)
                m2_pair(1)
                dve.wait_ge(act_says, 1).then_inc(act_says, -1)
                link(*[stt(G[:, 3 + i, :], xbc[:, i, :], col("m2g", i), G[:, 5, :], MUL, MUL) for i in range(2)])
                for i in range(2):
                    emit(MIXD + i, G[:, 3 + i, :])
                s5_finish(0)
                dve.wait_ge(act_says, 1).then_inc(act_says, -1)
                qk_raw(0)
                qk_raw(1)
                qk_normed(0, 0)
                with dve.Fori(0, 3) as t:
                    for p in range(2):
                        qk_raw(p)
                        qk_normed(t * 2 + (p + 1), 1 - p)
                        qk_turned(t * 2 + p)
                qk_normed(7, 1)
                qk_turned(6)
                qk_turned(7)
                s5(4)
                s5(5)
                for t in range(NQ):
                    dve.wait_ge(dve_bank[t], 1).then_inc(dve_bank[t], -1)
                    link(ts(v[:, t, :], bank[t][:, :], rtok[:, 0, t, 0:1], None, MUL))
                    say(dve, bank_free[t])
                say(dve, v_ready)
                s5(6)
                s5(7)
                s5_finish(1)
                dve.wait_ge(act_says, 1).then_inc(act_says, -1)
                say(dve, glu_in)
                for i in range(2):
                    dve.wait_ge(act_says, 1).then_inc(act_says, -1)
                    link(tt(G[:, 3 + i, :], G[:, 1 + i, :], u[:, i, :], MUL))
                for i in range(2):
                    emit(MIXC + i, G[:, 3 + i, :])
                say(dve, mats_free)
                maxima(0)
                for n in range(4 * HEADS):
                    if n >= NQ and n % NQ == 0:
                        head_out()
                    if n + 1 < 4 * HEADS:
                        maxima(n + 1)
                    combine(n)
                    if n % 2:
                        residual(n // 2, n // 2 % 2)
                    if n > NQ and n % NQ == 1:
                        head_emit(n // NQ - 1)
                head_out()
                head_emit(HEADS - 1)
                residuals()
                inputs("g2")
                dve.wait_ge(rms_ready, 1).then_inc(rms_ready, -1)
                for half in range(2):
                    with dve.Fori(0, FHALF) as i:
                        ffn_tile(half, i)
                    residuals()
            say(dve, out_ready)


def constants():
    c = np.zeros((P, NCONST), np.float32)
    r = np.arange(P)
    c[:, CONSTS["ident"]] = np.eye(P)
    c[:, CONSTS["ones"]] = 1
    c[:, CONSTS["tri"]] = r[:, None] <= r[None, :]
    perm, cos, sin = np.zeros((P, P)), np.ones((P, T)), np.zeros((P, T))
    inv = (1.0 / (THETA ** (np.arange(0, ROPE, 2, dtype=np.float32) / ROPE))).astype(np.float32)
    ang = np.arange(T, dtype=np.float32)[:, None] * inv[None, :]
    half = ROPE // 2
    for b in range(2):
        for i in range(half):
            lo, hi = b * QK + i, b * QK + half + i
            perm[hi, lo], perm[lo, hi] = -1, 1
            cos[lo], cos[hi] = np.cos(ang[:, i]), np.cos(ang[:, i])
            sin[lo], sin[hi] = np.sin(ang[:, i]), np.sin(ang[:, i])
    c[:, CONSTS["perm"]], c[:, CONSTS["cos"]], c[:, CONSTS["sin"]] = perm, cos, sin
    c[:, CONSTS["block"]] = r[:, None] // QK == r[None, :] // QK
    c[:, CONSTS["cap"]] = np.where(r[None, :] >= r[:, None], 0.0, NEG)
    c[:, CONSTS["mask"]] = np.where(r[None, :] <= r[:, None], 0.0, NEG)
    c[:, CONSTS["steps"]] = np.concatenate([np.arange(FINE), FINE * np.arange(COARSE)])
    c[:, CONSTS["eps"]] = EPS
    return c


def layout(inp):
    def units(w, first_k=0, K=None):
        K = w.shape[1] // P if K is None else K
        w = w[:, first_k * P:(first_k + K) * P].reshape(L, K, P, -1, P)
        return np.ascontiguousarray(w.transpose(0, 3, 2, 1, 4)).reshape(L, -1, P, K * P)

    w = inp["w_in"]
    a, b, c = 512, 1024, 1536
    sc, s5, z, xbc, dt = 1536, 2304, 2560, 2816, 3584
    order = [w[:, :, s5:z], w[:, :, xbc:dt], w[:, :, z:xbc], w[:, :, sc + 256:sc + 512], w[:, :, sc + 512:s5],
             w[:, :, sc:sc + 256]]
    for h in range(HEADS):
        order += [w[:, :, h * P:(h + 1) * P], w[:, :, a + h * P:a + (h + 1) * P]]
    w_in = units(np.concatenate(order, axis=2))
    wv = w[:, :, b:c].reshape(L, 4, 2, P, HEADS * P).transpose(0, 1, 3, 2, 4).reshape(L, 4, P, KD * P)
    w_in = np.concatenate([w_in, wv], axis=1)
    gu = np.stack([units(inp["ffn_w_gate"]), units(inp["ffn_w_up"])], axis=2).reshape(L, 2 * FF, P, KD * P)
    dn = np.stack([units(inp["ffn_w_down"], h * FHALF, FHALF) for h in range(2)], axis=1).reshape(L, 16, P, FHALF * P)

    par = np.zeros((P, L, NPAR), np.float32)

    def put(name, value):
        o, n = PARAMS[name]
        par[:, :, o:o + n] = np.broadcast_to(value, (L, P, n)).transpose(1, 0, 2)

    def tiled(p):
        return p.reshape(L, -1, P).transpose(0, 2, 1)

    put("g1", tiled(inp["ln1_g"]))
    put("g2", tiled(inp["ln2_g"]))
    put("qkg", np.tile(inp["qk_norm_g"], (1, 1, 2)).transpose(0, 2, 1))
    put("subg", tiled(inp["subln_g"]))
    init = np.array([0.8 - 0.6 * np.exp(-0.3 * l) for l in range(L)], np.float32)
    put("linit", init.reshape(L, 1, 1))
    put("oneml", (np.float32(1) - init).reshape(L, 1, 1))
    put("scw", inp["sc_conv_w"].reshape(L, 3, 2, P).transpose(0, 3, 2, 1).reshape(L, P, 6))

    def states(p):
        return p.reshape(L, SJ, P).transpose(0, 2, 1)

    put("lre", states(inp["s5_lam_re"]))
    put("lim", states(inp["s5_lam_im"]))
    put("ldt", states(np.repeat(inp["s5_log_dt"], 64, axis=1)))
    put("s5d", tiled(inp["s5_d"]))
    put("bglu", tiled(inp["s5_b_glu"]))
    put("m2w", inp["m2_conv_w"].reshape(L, 4, 6, P).transpose(0, 3, 2, 1).reshape(L, P, 24))
    put("m2b", tiled(inp["m2_conv_b"]))
    put("dtb", inp["m2_dt_bias"][:, None, :])
    put("alog", inp["m2_a_log"][:, None, :])
    put("m2d", tiled(np.repeat(inp["m2_d"], M2P, axis=1)))
    put("m2g", tiled(inp["m2_norm_g"]))
    put("ffw", inp["ffn_conv_w"].reshape(L, 3, FF, P).transpose(0, 3, 2, 1).reshape(L, P, 3 * FF))
    put("dal", inp["da_lambda"].reshape(L, 1, 4 * QK))
    put("wdt", w[:, :, dt:].reshape(L, KD, P, M2H).transpose(0, 2, 1, 3).reshape(L, P, KD * M2H))

    bmat = np.zeros((L, 2, 4, 2, 16, 2, 2, 64), np.float32)
    cmat = np.zeros((L, 2, 64, 2, SJ, 2, 16), np.float32)
    for ci, (bn, cn) in enumerate((("s5_b_re", "s5_c_re"), ("s5_b_im", "s5_c_im"))):
        bb = inp[bn].reshape(L, 2, 4, 2, 64, 16)
        cc = inp[cn].reshape(L, SJ, 2, 16, 64)
        for g in range(2):
            bmat[:, :, :, g, :, ci, g, :] = bb[:, :, :, g].transpose(0, 1, 2, 4, 3)
            cmat[:, g, :, ci, :, g, :] = cc[:, :, g].transpose(0, 3, 1, 2)
    bmat = bmat.transpose(0, 2, 3, 4, 5, 1, 6, 7).reshape(L, P, 2 * 2 * P)
    cmat = cmat.reshape(L, P, 2 * SJ * SH)
    wglu = inp["s5_w_glu"].reshape(L, 2, P, 256).transpose(0, 2, 1, 3).reshape(L, P, 512)
    return {
        "x": inp["x"].reshape(T, KD, P).transpose(2, 1, 0), "par": par, "cst": constants(),
        "w_in": w_in, "w_oe": units(inp["w_out"], HEADS, KEARLY), "w_ol": units(inp["w_out"], 0, HEADS),
        "w_gu": gu, "w_dn": dn, "bmat": bmat, "cmat": cmat, "wglu": wglu,
    }


def kernel(**inputs):
    import concourse.bacc as bacc
    from concourse.bass_utils import run_bass_kernel_spmd as run

    arrays = layout({k: np.asarray(a) for k, a in inputs.items()})
    arrays = {f"in_{k}": np.ascontiguousarray(a) for k, a in arrays.items()}
    nc = bacc.Bacc("TRN2", target_bir_lowering=False, num_devices=1)
    A = {k[3:]: nc.dram_tensor(k, a.shape, mybir.dt.from_np(a.dtype), kind="ExternalInput").ap()
         for k, a in arrays.items()}
    A["out"] = nc.dram_tensor("out_x", (P, KD, T), F32, kind="ExternalOutput").ap()
    build(nc, A)
    out = run(nc, [arrays], core_ids=[0]).results[0]["out_x"]
    return np.ascontiguousarray(out.transpose(2, 1, 0)).reshape(1, T, D)
```

```python
from contextlib import ExitStack

import numpy as np

import concourse.bass as bass
from concourse import mybir

F32 = mybir.dt.float32
F32R = mybir.dt.float32r
BF16 = mybir.dt.bfloat16
ALU = mybir.AluOpType
ACT = mybir.ActivationFunctionType
AX = mybir.AxisListType.X

L = 2
D, T, P = 1024, 512, 128
KD = D // P
NQ = T // P
HEADS, QK = 4, 64
ROPE = 16
THETA = 500000.0
SJ, SH = 8, 32
M2H, M2P = 4, 64
FF, FHALF = 22, 11
MIXA, MIXB, MIXC, MIXD = 0, 4, 6, 8
MIXED = 10
KEARLY = MIXED - HEADS
STEPS = HEADS * NQ
TABLE_AT = [2, 3, 4, 5] + list(range(13, 25))
EPS = 1e-6
NIN = 28
FINE, COARSE = 32, 16
NT = FINE + COARSE
NEG = -1e30
INV2PI = float(np.float32(1 / (2 * np.pi)))
ROUND = float(1.5 * 2**23)
C1 = 6.28125
C2 = float(np.float32(np.round((2 * np.pi - C1) * 2**21) / 2**21))
C3 = float(np.float32(2 * np.pi - C1 - C2))
PI_CAP = 3.1415925

CONSTS, _o = {}, 0
for _name, _n in [("ident", P), ("ones", P), ("tri", P), ("perm", P), ("block", P), ("cap", P), ("mask", P),
                  ("cos", T), ("sin", T), ("steps", NT), ("eps", 1)]:
    CONSTS[_name] = slice(_o, _o + _n)
    _o += _n
NCONST = _o
PARAMS, _o = {}, 0
for _name, _n in [("g1", KD), ("g2", KD), ("qkg", 2), ("subg", 1), ("oneml", 1), ("scw", 6),
                  ("s5d", 2), ("bglu", 2), ("m2w", 24), ("m2b", 6),
                  ("dtb", M2H), ("alog", M2H), ("m2d", 2), ("m2g", 2), ("ffw", 3 * FF), ("wdt", KD * M2H)]:
    PARAMS[_name] = (_o, _n)
    _o += _n
NPAR = _o
PRE, _o = {}, 0
for _name, _n in [("dal", 4 * QK), ("lre", SJ), ("lim", SJ), ("ldt", SJ), ("linit", 1)]:
    PRE[_name] = slice(_o, _o + _n)
    _o += _n
NPRE = _o


def build(nc, A):
    with ExitStack() as ctx:
        arena_end = [0]

        def sb(name, shape, dt=F32, at=None):
            size = int(np.prod(shape[1:])) * (2 if dt == BF16 else 4)
            size = -(-size // 32) * 32
            off = arena_end[0] if at is None else at
            if at is None:
                arena_end[0] += size
            offsets[name] = off
            return nc.alloc_sbuf_tensor_at(name, list(shape), dt, offset=base + off)

        def sem(name):
            return ctx.enter_context(nc.semaphore(name))

        offsets = {}
        base = -(-nc.sbuf_base // 32) * 32
        arena_bytes = nc.sbuf_bytes_remaining - 32

        x = sb("x", [P, KD, T])
        xh = sb("xh", [P, KD, T], F32R)
        xl = sb("xl", [P, KD, T], F32R)
        mh = sb("mh", [P, FHALF, T], F32R)
        ml = sb("ml", [P, FHALF, T], F32R)
        raw = sb("raw", [P, 2, FHALF * P])
        wh = sb("wh", [P, 2, FHALF * P], F32R)
        wl = sb("wl", [P, 2, FHALF * P], F32R)
        qk = sb("qk", [P, 8, T])
        v = sb("v", [P, NQ, HEADS * P])
        xbc = sb("xbc", [P, 6, T], at=offsets["qk"])
        z = sb("z", [P, 2, T], at=offsets["qk"] + 6 * T * 4)
        xbt = sb("xbt", [P, NQ, 4, P], at=offsets["v"])
        u = sb("u", [P, 2, T])
        pad = sb("pad", [P, 2, 4 + T])
        G = sb("G", [P, 6, T])
        rbc = sb("rbc", [P, T])
        ssum = sb("ssum", [P, T])
        sA, sB, sC, sD = [sb(f"s5{n}", [P, T], at=offsets["mh"] + i * T * 4) for i, n in enumerate("abcd")]
        sE, rotc, rots, s5t = [sb(f"s5{n}", [P, T], at=offsets["ml"] + i * T * 4) for i, n in enumerate("efgh")]
        ex = [sb(f"ex{i}", [P, T], at=offsets[n] + (FHALF - 1) * T * 4) for i, n in enumerate(("mh", "ml"))]
        tab = [(rotc, rots), (ssum, ex[1])]
        m2buf = [(G[:, 1], G[:, 2]), (G[:, 3], ex[0][:, :])]
        pre_end = [offsets["mh"]]

        def early(name, shape, dt=F32):
            t = sb(name, shape, dt, at=pre_end[0])
            pre_end[0] += -(-int(np.prod(shape[1:])) * 4 // 32) * 32
            return t

        pre = early("pre", [P, L, NPRE])
        cmat = early("cmat", [P, L, 2, SJ * SH])
        ph0, kk0, lo0 = [early(n, [P, L * SJ, NT]) for n in ("phase", "turns", "phase_low")]
        ctmp = early("ctmp", [P, 4, SJ * SH])
        lprod = early("lprod", [P, 2, QK])
        lam2 = early("lam2", [P, L, 2])
        s8 = early("s8", [P, 16, L, SJ])
        thh = early("thh", [P, L * SJ], F32R)
        assert pre_end[0] <= offsets["ml"] + FHALF * T * 4
        bmat = sb("bmat", [P, 2, 2, P])
        cf_all = sb("cf_all", [P, L, 2 * SJ * SH])
        cf = sb("cf", [P, 2, SJ, SH])
        wglu = sb("wglu", [P, 2, 256])
        xds = sb("xds", [P, NQ - 1, M2H, M2P])
        hst = sb("hst", [P, NQ - 1, M2H, M2P])
        rot = sb("rot", [P, L, 2, SJ, NT])
        rho_all = sb("rho_all", [P, L, SJ])
        rho = sb("rho", [P, SJ])
        permg = sb("permg", [P, 2, P])
        par_all = sb("par_all", [P, L, NPAR])
        par = sb("par", [P, NPAR])
        cst = sb("cst", [P, NCONST])
        cbf = sb("cbf", [P, 2, P], BF16)
        wdth = sb("wdth", [P, KD, M2H], F32R)
        wdtl = sb("wdtl", [P, KD, M2H], F32R)
        s16 = sb("s16", [P, 12, NQ * M2H])
        rtok = sb("rtok", [P, NQ, 2])
        mlam_all = sb("mlam_all", [P, L])
        mlam = sb("mlam", [P, 1])
        soft = sb("soft", [P, 2, 8])
        assert arena_end[0] <= arena_bytes, (arena_end[0], arena_bytes)

        bank = [ctx.enter_context(nc.psum_tensor(f"bank{b}", [P, T], F32)) for b in range(8)]

        def col(name, i=0, n=1):
            return par[:, PARAMS[name][0] + i:PARAMS[name][0] + i + n]

        ident, ones, tri, perm, block1, cap = [cst[:, CONSTS[k]] for k in ("ident", "ones", "tri", "perm", "block", "cap")]
        cosT, sinT, steps = cst[:, CONSTS["cos"]], cst[:, CONSTS["sin"]], cst[:, CONSTS["steps"]]
        eps = cst[:, CONSTS["eps"]]
        adt = s16[:, 3, :]

        bank_free = [sem(f"bank_free{b}") for b in range(8)]
        dve_bank = [sem(f"dve_bank{b}") for b in range(8)]
        act_bank = [sem(f"act_bank{b}") for b in range(8)]
        raw_full, raw_free = [sem(f"raw_full{p}") for p in range(2)], sem("raw_free")
        wh_full, wh_free, wh_low = sem("wh_full"), sem("wh_free"), sem("wh_low")
        wl_full, wl_free = sem("wl_full"), sem("wl_free")
        x_loaded, par_loaded, cst_loaded = sem("x_loaded"), sem("par_loaded"), sem("cst_loaded")
        act_go, pe_go, pool_go = sem("act_go"), sem("pe_go"), sem("pool_go")
        mats_full, mats_free = sem("mats_full"), sem("mats_free")
        out_ready, out_done = sem("out_ready"), sem("out_done")
        dve_own, act_own, pool_own = sem("dve_own"), sem("act_own"), sem("pool_own")
        pre_loaded = sem("pre_loaded")
        x_ready = sem("x_ready")
        sq_full, sq_free = sem("sq_full"), sem("sq_free")
        xk_ready, ssum_ready = sem("xk_ready"), sem("ssum_ready")
        rms_ready = sem("rms_ready")
        ask_act, act_says = sem("ask_act"), sem("act_says")
        exp_go, exp_done, osq_go, onorm_done = sem("exp_go"), sem("exp_done"), sem("osq_go"), sem("onorm_done")
        em_full, em_high = sem("em_full"), sem("em_high")
        wdt_ready, adt_ready = sem("wdt_ready"), sem("adt_ready")
        u_ready, s5x_ready, s5x_read = sem("u_ready"), sem("s5x_ready"), sem("s5x_read")
        glu_in = sem("glu_in")
        xbc_ready, xbt_ready, hst_ready = sem("xbc_ready"), sem("xbt_ready"), sem("hst_ready")
        mix_ready, mix_read, m2sq_ready = sem("mix_ready"), sem("mix_read"), sem("m2sq_ready")
        sqk_ready, qk_ready = sem("sqk_ready"), sem("qk_ready")
        vch_ready, vch_read = sem("vch_ready"), sem("vch_read")
        v_ready, probs_ready, probsT_ready = sem("v_ready"), sem("probs_ready"), sem("probsT_ready")
        osq_ready = sem("osq_ready")
        mixed_ready, hid_ready = sem("mixed_ready"), sem("hid_ready")
        tab_full, tab_free = sem("tab_full"), sem("tab_free")

        def linker(eng, own):
            def link(*ins):
                for i in ins:
                    i.then_inc(own, 1)
                eng.wait_ge(own, len(ins)).then_inc(own, -(len(ins)))
            return link

        def say(eng, *sems):
            for s in sems:
                eng.sem_inc(s, 1)

        G_IN, G_OE, G_OL, G_GU, G_DN = (A["w_in"], KD * P), (A["w_oe"], KEARLY * P), (A["w_ol"], HEADS * P), \
            (A["w_gu"], KD * P), (A["w_dn"], FHALF * P)

        blk = ctx.enter_context(nc.Block())

        @blk.sync
        def _(sp):
            sp.dma_start(pre[:, :, :], A["pre"]).then_inc(pre_loaded, 16)
            sp.dma_start(cst[:, :], A["cst"]).then_inc(cst_loaded, 16)
            sp.dma_start(cmat[:, :, :, :], A["cmat"]).then_inc(pre_loaded, 16)
            sp.dma_start(par_all[:, :, :], A["par"]).then_inc(par_loaded, 16)
            for i in range(KD):
                sp.dma_start(x[:, i, :], A["x"][:, i, :]).then_inc(x_loaded, 16)

            def stream(group, l, first, n):
                src, cols = group
                with sp.Fori(0, n // 2) as i:
                    for p in range(2):
                        sp.wait_ge(raw_free, 1).then_inc(raw_free, -1)
                        sp.dma_start(raw[:, p, 0:cols], src[bass.ds(l, 1), bass.ds(i * 2 + (first + p), 1)]
                                     .rearrange("a b p c -> (a b p) c")).then_inc(raw_full[p], 16)

            with sp.Fori(0, L) as l:
                stream(G_IN, l, 0, 2)
                sp.wait_ge(mats_free, 1).then_inc(mats_free, -1)
                for dst, name in ((bmat, "bmat"), (wglu, "wglu")):
                    src = A[name][bass.ds(l, 1)]
                    flat = "p a b c -> p (a b c)" if name != "wglu" else "p a b -> p (a b)"
                    sp.dma_start(dst[:].rearrange(flat), src.rearrange("l p c -> (l p) c")).then_inc(mats_full, 16)
                stream(G_IN, l, 2, NIN - 2)
                stream(G_OE, l, 0, 8)
                stream(G_OL, l, 0, 8)
                for half in range(2):
                    stream(G_GU, l, half * 2 * FHALF, 2 * FHALF)
                    stream(G_DN, l, half * 8, 8)
            sp.wait_ge(out_ready, 1).then_inc(out_ready, -1)
            for i in range(KD):
                sp.dma_start(A["out"][:, i, :], x[:, i, :]).then_inc(out_done, 16)
            sp.wait_ge(out_done, 16 * KD)

        @blk.gpsimd
        def _(pool):
            link = linker(pool, pool_own)

            def low(p, cols):
                pool.wait_ge(wh_low, 1).then_inc(wh_low, -1)
                pool.wait_ge(wl_free, 1).then_inc(wl_free, -1)
                link(nc.gpsimd.tensor_tensor(wl[:, p, 0:cols], raw[:, p, 0:cols], wh[:, p, 0:cols].bitcast(F32),
                                             ALU.subtract))
                say(pool, wl_full, raw_free)

            def lows(cols, n):
                with pool.Fori(0, n // 2):
                    for p in range(2):
                        low(p, cols)

            def table(l, j, part):
                if part == 0:
                    pool.wait_ge(tab_free, 1).then_inc(tab_free, -1)
                shape = [P, COARSE, FINE]
                steps_of = [rot[:, bass.ds(l, 1), i, j, :].rearrange("p a b -> p (a b)") for i in range(2)]
                cc, sc = [r[:, FINE:NT].unsqueeze(2).broadcast_to(shape) for r in steps_of]
                cfn, sfn = [r[:, 0:FINE].unsqueeze(1).broadcast_to(shape) for r in steps_of]
                out = tab[j % 2][part]
                out3, t3 = [t[:, :].rearrange("p (a b) -> p a b", a=COARSE) for t in (out, s5t)]
                tt = nc.gpsimd.tensor_tensor
                if part == 0:
                    link(tt(out3, cc, cfn, ALU.mult), tt(t3, sc, sfn, ALU.mult))
                    link(tt(out[:, :], out[:, :], s5t[:, :], ALU.subtract))
                else:
                    link(tt(out3, sc, cfn, ALU.mult), tt(t3, cc, sfn, ALU.mult))
                    link(tt(out[:, :], out[:, :], s5t[:, :], ALU.add))
                    say(pool, tab_full)

            say(pool, raw_free, raw_free, wl_free)
            with pool.Fori(0, L) as l:
                low(0, KD * P)
                for s in range(NIN - 1):
                    low((s + 1) % 2, KD * P)
                    if s in TABLE_AT:
                        table(l, TABLE_AT.index(s) // 2, TABLE_AT.index(s) % 2)
                lows(KEARLY * P, 8)
                lows(HEADS * P, 8)
                for half in range(2):
                    lows(KD * P, 2 * FHALF)
                    lows(FHALF * P, 8)

        @blk.tensor
        def _(pe):
            mm = nc.tensor.matmul

            def unit(p, K, hi, lo, ready=None):
                pe.wait_ge(wh_full, 1).then_inc(wh_full, -1)
                pe.wait_ge(bank_free[p], 1).then_inc(bank_free[p], -1)
                for k in range(K):
                    if ready is not None:
                        pe.wait_ge(ready, 1).then_inc(ready, -1)
                    w = mm(bank[p][:, :], wh[:, p, k * P:(k + 1) * P], lo[:, k, :], start=(k == 0), stop=False)
                    if k == 0:
                        w.then_inc(wl_free, 1)
                for k in range(K):
                    w = mm(bank[p][:, :], wh[:, p, k * P:(k + 1) * P], hi[:, k, :], start=False, stop=False)
                w.then_inc(wh_free, 1)
                pe.wait_ge(wl_full, 1).then_inc(wl_full, -1)
                for k in range(K):
                    w = mm(bank[p][:, :], wl[:, p, k * P:(k + 1) * P], hi[:, k, :], start=False, stop=(k == K - 1))
                w.then_inc(dve_bank[p], 1)

            def units(n, K, hi, lo, ready=None):
                if ready is not None:
                    unit(0, K, hi, lo, ready)
                    unit(1, K, hi, lo)
                    n -= 2
                with pe.Fori(0, n // 2):
                    unit(0, K, hi, lo)
                    unit(1, K, hi, lo)

            def rms_sum():
                pe.wait_ge(ssum_ready, 1).then_inc(ssum_ready, -1)
                pe.wait_ge(bank_free[7], 1).then_inc(bank_free[7], -1)
                mm(bank[7][:, :], ones, ssum[:, :], start=True, stop=True).then_inc(act_bank[7], 1)

            def token_sums():
                pe.wait_ge(bank_free[6], 1).then_inc(bank_free[6], -1)
                for t in range(NQ):
                    w = mm(bank[6][:, 2 * t:2 * t + 2], ssum[:, t * P:(t + 1) * P], ones[:, 0:2], start=True, stop=True)
                w.then_inc(act_bank[6], 1)

            def dt_columns():
                pe.wait_ge(wdt_ready, 1).then_inc(wdt_ready, -1)
                pe.wait_ge(bank_free[5], 1).then_inc(bank_free[5], -1)
                for t in range(NQ):
                    out = bank[5][:, t * M2H:(t + 1) * M2H]
                    for n, (a, b) in enumerate(((xl, wdth), (xh, wdth), (xh, wdtl))):
                        for k in range(KD):
                            w = mm(out, a[:, k, t * P:(t + 1) * P], b[:, k, :], start=(n == k == 0),
                                   stop=(n == 2 and k == KD - 1))
                w.then_inc(dve_bank[5], 1)

            def s5_in(j):
                if j == 0:
                    pe.wait_ge(u_ready, 1).then_inc(u_ready, -1)
                r = SH * (j % 4)
                for c in range(2):
                    pe.wait_ge(bank_free[2 + c], 1).then_inc(bank_free[2 + c], -1)
                    mm(bank[2 + c][:, :], bmat[r:r + SH, c, j // 4, :],
                       u[r:r + SH, j // 4, :], start=True, stop=True).then_inc(dve_bank[2 + c], 1)

            def s5_out(j):
                r = SH * (j % 4)
                if j % 4 == 0:
                    pe.wait_ge(bank_free[6], 1).then_inc(bank_free[6], -1)
                pe.wait_ge(s5x_ready, 1).then_inc(s5x_ready, -1)
                mm(bank[6][r:r + SH, :], cf[:, 0, j, :], sE[:, :], start=True, stop=False)
                w = mm(bank[6][r:r + SH, :], cf[:, 1, j, :], sA[:, :], start=False, stop=True)
                w.then_inc(s5x_read, 1)

            def s5_glu():
                pe.wait_ge(glu_in, 1).then_inc(glu_in, -1)
                for i in range(2):
                    pe.wait_ge(bank_free[6 + i], 1).then_inc(bank_free[6 + i], -1)
                    for k in range(2):
                        w = mm(bank[6 + i][:, :], wglu[:, k, i * P:(i + 1) * P], u[:, k, :], start=(k == 0), stop=(k == 1))
                    w.then_inc(act_bank[6 + i], 1)

            def m2_sums():
                pe.wait_ge(adt_ready, 1).then_inc(adt_ready, -1)
                pe.wait_ge(bank_free[7], 1).then_inc(bank_free[7], -1)
                mm(bank[7][:, 0:16], tri, adt, start=True, stop=True)
                mm(bank[7][:, 16:32], ones, adt, start=True, stop=True).then_inc(dve_bank[7], 1)

            def m2_turn(t):
                b = (4, 7)[t % 2]
                pe.wait_ge(bank_free[b], 1).then_inc(bank_free[b], -1)
                for i in range(4 if t < NQ - 1 else 2):
                    w = nc.tensor.transpose(bank[b][:, i * P:(i + 1) * P], xbc[:, i, t * P:(t + 1) * P], ident)
                w.then_inc(dve_bank[b], 1)

            def m2_states(t):
                pe.wait_ge(xbt_ready, 1).then_inc(xbt_ready, -1)
                if t % 2 == 0:
                    pe.wait_ge(bank_free[5], 1).then_inc(bank_free[5], -1)
                for g in range(2):
                    c = (2 * (t % 2) + g) * P
                    w = mm(bank[5][:, c:c + P], xbt[:, t, 2 + g, :],
                           xds[:, t, 2 * g:2 * g + 2, :].rearrange("p h c -> p (h c)"), start=True, stop=True)
                if t:
                    w.then_inc(dve_bank[5], 1)

            def m2_scores(g):
                pe.wait_ge(bank_free[7], 1).then_inc(bank_free[7], -1)
                for t in range(NQ):
                    c = slice(t * P, (t + 1) * P)
                    w = mm(bank[7][:, c], xbc[:, 2 + g, c], xbc[:, 4 + g, c], start=True, stop=True)
                w.then_inc(dve_bank[7], 1)

            def m2_decays(h):
                pe.wait_ge(bank_free[4], 1).then_inc(bank_free[4], -1)
                for t in range(NQ):
                    c = slice(t * P, (t + 1) * P)
                    w = mm(bank[4][:, c], adt[:, t * M2H + h:t * M2H + h + 1].broadcast_to([P, P]), tri,
                           start=True, stop=True)
                w.then_inc(dve_bank[4], 1)

            def m2_apply(h):
                pe.wait_ge(mix_ready, 1).then_inc(mix_ready, -1)
                if h == 0:
                    pe.wait_ge(hst_ready, 1).then_inc(hst_ready, -1)
                if h % 2 == 0:
                    pe.wait_ge(bank_free[5], 1).then_inc(bank_free[5], -1)
                r = slice(M2P * (h % 2), M2P * (h % 2) + M2P)
                for t in range(NQ):
                    c = slice(t * P, (t + 1) * P)
                    decayed, decayed_c = m2buf[h % 2]
                    w = mm(bank[5][r, c], xbt[:, t, h // 2, r], decayed[:, c], start=True, stop=(t == 0))
                    if t > 0:
                        w = mm(bank[5][r, c], hst[:, t - 1, h, :], decayed_c[:, c], start=False, stop=True)
                w.then_inc(mix_read, 1)

            def m2_norm():
                pe.wait_ge(bank_free[7], 1).then_inc(bank_free[7], -1)
                for i in range(2):
                    pe.wait_ge(m2sq_ready, 1).then_inc(m2sq_ready, -1)
                    w = mm(bank[7][:, :], ones, xbc[:, 2 + i, :], start=(i == 0), stop=(i == 1))
                w.then_inc(act_bank[7], 1)

            def qk_mean(t):
                pe.wait_ge(sqk_ready, 1).then_inc(sqk_ready, -1)
                pe.wait_ge(bank_free[4], 1).then_inc(bank_free[4], -1)
                mm(bank[4][:, :], block1, G[:, 2, :], start=True, stop=True).then_inc(act_bank[4], 1)
                pe.wait_ge(bank_free[5], 1).then_inc(bank_free[5], -1)
                mm(bank[5][:, :], permg[:, t % 2, :], G[:, t % 2, :], start=True, stop=True).then_inc(dve_bank[5], 1)

            def v_turn(h):
                pe.wait_ge(vch_ready, 1).then_inc(vch_ready, -1)
                pe.wait_ge(bank_free[4], 1).then_inc(bank_free[4], -1)
                for t in range(NQ):
                    w = nc.tensor.transpose(bank[4][:, t * P:(t + 1) * P], G[:, h % 2, t * P:(t + 1) * P], ident)
                w.then_inc(act_bank[4], 1)

            def scores(n):
                h, q = n // NQ, n % NQ
                for c in range(2):
                    b = (2, 3, 6, 7)[2 * (n % 2) + c]
                    pe.wait_ge(bank_free[b], 1).then_inc(bank_free[b], -1)
                    r = slice(QK * c, QK * c + QK)
                    qs, last = qk[r, 2 * h, q * P:(q + 1) * P], slice(q * P, (q + 1) * P)
                    if q:
                        mm(bank[b][:, 0:q * P], qs, qk[r, 2 * h + 1, 0:q * P], start=True, stop=True)
                    mm(bank[b][:, last], qs, qk[r, 2 * h + 1, last], start=True, stop=False)
                    mm(bank[b][:, last], cbf[:, 0, :], cbf[:, 1, :], start=False, stop=True).then_inc(dve_bank[b], 1)

            def turn(n):
                pe.wait_ge(probs_ready, 1).then_inc(probs_ready, -1)
                pe.wait_ge(bank_free[4], 1).then_inc(bank_free[4], -1)
                for k in range(n % NQ + 1):
                    w = nc.tensor.transpose(bank[4][:, k * P:(k + 1) * P], G[:, 2 * (n % 2), k * P:(k + 1) * P], ident)
                w.then_inc(act_bank[4], 1)

            def attend(n):
                h, q = n // NQ, n % NQ
                if q == 0:
                    pe.wait_ge(bank_free[5], 1).then_inc(bank_free[5], -1)
                pe.wait_ge(probsT_ready, 1).then_inc(probsT_ready, -1)
                for k in range(q + 1):
                    w = mm(bank[5][:, q * P:(q + 1) * P], v[:, k, h * P:(h + 1) * P], G[:, 4 + n % 2, k * P:(k + 1) * P],
                           start=(k == 0), stop=(k == q))
                if q == NQ - 1:
                    w.then_inc(dve_bank[5], 1)

            def head_sum():
                pe.wait_ge(osq_ready, 1).then_inc(osq_ready, -1)
                pe.wait_ge(bank_free[1], 1).then_inc(bank_free[1], -1)
                mm(bank[1][:, :], ones, pad[:, 0, 4:4 + T], start=True, stop=True).then_inc(act_bank[1], 1)

            pe.wait_ge(pe_go, 1).then_inc(pe_go, -1)
            with pe.Fori(0, L):
                unit(0, KD, xh, xl, xk_ready)
                rms_sum()
                token_sums()
                unit(1, KD, xh, xl)
                dt_columns()
                for s in range(2, NIN):
                    unit(s % 2, KD, xh, xl)
                    if s == 3:
                        m2_sums()
                    if s == 7:
                        for _ in range(4):
                            pe.wait_ge(xbc_ready, 1).then_inc(xbc_ready, -1)
                        m2_turn(0)
                        m2_turn(1)
                    if s == 8:
                        m2_turn(2)
                        m2_turn(3)
                        s5_in(0)
                    if s == 9:
                        m2_decays(0)
                        for _ in range(2):
                            pe.wait_ge(xbc_ready, 1).then_inc(xbc_ready, -1)
                        m2_states(0)
                        m2_states(1)
                        m2_scores(0)
                    if s == 10:
                        m2_states(2)
                        pe.wait_ge(xbt_ready, 1).then_inc(xbt_ready, -1)
                        m2_decays(1)
                    if s == 11:
                        m2_apply(0)
                    if s == 12:
                        m2_apply(1)
                        s5_out(0)
                        s5_in(1)
                        m2_decays(2)
                        m2_scores(1)
                    if s == 13:
                        m2_apply(2)
                        m2_decays(3)
                    if s == 14:
                        m2_apply(3)
                    if s == 15:
                        s5_in(2)
                    if s == 16:
                        s5_out(1)
                        m2_norm()
                    if 17 <= s <= 24:
                        qk_mean(s - 17)
                    if s >= 25:
                        v_turn(s - 25)
                    if s >= 17 and s % 2:
                        s5_out((s - 13) // 2)
                        if s < 27:
                            s5_in((s - 11) // 2)
                pe.wait_ge(qk_ready, 1).then_inc(qk_ready, -1)
                scores(0)
                v_turn(3)
                s5_glu()
                scores(1)
                for n in range(STEPS):
                    if n + 2 < STEPS:
                        scores(n + 2)
                    turn(n)
                    if n == 1:
                        for _ in range(KEARLY):
                            pe.wait_ge(mixed_ready, 1).then_inc(mixed_ready, -1)
                    if n % 2:
                        unit(n // 2 % 2, KEARLY, mh[:, MIXB:MIXED, :], ml[:, MIXB:MIXED, :])
                    if n == 1:
                        for _ in range(HEADS):
                            pe.wait_ge(v_ready, 1).then_inc(v_ready, -1)
                    if n:
                        attend(n - 1)
                    if n > NQ and n % NQ == 2:
                        head_sum()
                attend(STEPS - 1)
                head_sum()
                units(8, HEADS, mh, ml, mixed_ready)
                unit(0, KD, xh, xl, xk_ready)
                rms_sum()
                unit(1, KD, xh, xl)
                units(2 * FHALF - 2, KD, xh, xl)
                units(8, FHALF, mh, ml, hid_ready)
                units(2 * FHALF, KD, xh, xl)
                units(8, FHALF, mh, ml, hid_ready)

        @blk.scalar
        def _(act):
            link = linker(act, act_own)
            fn = nc.scalar.activation

            def prep(p, cols):
                act.wait_ge(raw_full[p], 16).then_inc(raw_full[p], -16)
                act.wait_ge(wh_free, 1).then_inc(wh_free, -1)
                link(fn(wh[:, p, 0:cols], raw[:, p, 0:cols], ACT.Copy))
                say(act, wh_full, wh_low)

            def preps(n, cols):
                with act.Fori(0, n // 2):
                    prep(0, cols)
                    prep(1, cols)

            def inputs(gain):
                act.wait_ge(x_ready, 1).then_inc(x_ready, -1)
                for k in range(KD):
                    act.wait_ge(sq_free, 1).then_inc(sq_free, -1)
                    link(fn(G[:, k % 2, :], x[:, k, :], ACT.Square),
                         fn(xh[:, k, :], x[:, k, :], ACT.Copy, scale=col(gain, k)))
                    say(act, sq_full)

            def rsqrt_mean(out, in_, n):
                link(fn(out, in_, ACT.Ln, scale=1.0 / n, bias=eps))
                link(fn(out, out, ACT.Exp, scale=-0.5))

            def rms():
                act.wait_ge(act_bank[7], 1).then_inc(act_bank[7], -1)
                rsqrt_mean(rbc[:, :], bank[7][:, :], D)
                say(act, bank_free[7])

            def high(dst, src):
                link(fn(dst, src, ACT.Copy))

            def emit(tile, buf):
                act.wait_ge(em_full, 1).then_inc(em_full, -1)
                high(mh[:, tile, :], buf)
                say(act, em_high)

            say(act, wh_free, wh_free)
            act.wait_ge(ask_act, 1).then_inc(ask_act, -1)
            link(fn(s8[:, 0], s8[:, 0], ACT.Exp), fn(lam2[:, :, :], lam2[:, :, :], ACT.Exp))
            say(act, act_says)
            act.wait_ge(ask_act, 1).then_inc(ask_act, -1)
            link(*[fn(rot[:, l, 1].rearrange("p a b -> p (a b)"),
                      ph0[:, l * SJ:(l + 1) * SJ, :].rearrange("p a b -> p (a b)"), ACT.Sin) for l in range(L)],
                 fn(kk0[:].rearrange("p a b -> p (a b)"), ph0[:].rearrange("p a b -> p (a b)"), ACT.Sin, scale=0.5))
            say(act, act_says)
            act.wait_ge(act_go, 1).then_inc(act_go, -1)
            with act.Fori(0, L):
                prep(0, KD * P)
                prep(1, KD * P)
                inputs("g1")
                link(fn(s16[:, 8, 0:M2H], col("alog", 0, M2H), ACT.Exp))
                prep(0, KD * P)
                rms()
                act.wait_ge(act_bank[6], 1).then_inc(act_bank[6], -1)
                rsqrt_mean(rtok[:].rearrange("p a b -> p (a b)"), bank[6][:, 0:2 * NQ], D)
                say(act, bank_free[6], rms_ready)

                def m2_head(h):
                    act.wait_ge(ask_act, 1).then_inc(ask_act, -1)
                    link(fn(m2buf[h % 2][0], m2buf[h % 2][0], ACT.Exp), fn(m2buf[h % 2][1], bank[4][:, :], ACT.Exp))
                    say(act, bank_free[4], act_says)

                def m2_square(i):
                    act.wait_ge(ask_act, 1).then_inc(ask_act, -1)
                    link(fn(xbc[:, 2 + i, :], xbc[:, i, :], ACT.Square))
                    say(act, m2sq_ready)

                def qk_square(t):
                    act.wait_ge(ask_act, 1).then_inc(ask_act, -1)
                    link(fn(G[:, 2, :], G[:, t % 2, :], ACT.Square))
                    say(act, sqk_ready)

                def v_copy(h):
                    act.wait_ge(act_bank[4], 1).then_inc(act_bank[4], -1)
                    link(fn(v[:, :, h * P:(h + 1) * P], bank[4][:, :].rearrange("p (t c) -> p t c", t=NQ), ACT.Copy))
                    say(act, bank_free[4], v_ready, vch_read)

                for s in range(1, NIN):
                    prep(s % 2, (KD if s < NIN - 2 else KEARLY) * P)
                    if s == 1:
                        act.wait_ge(ask_act, 1).then_inc(ask_act, -1)
                        link(fn(s16[:, 1, :], s16[:, 1, :], ACT.Exp, scale=-1.0))
                        say(act, act_says)
                    if 2 <= s <= 7:
                        act.wait_ge(ask_act, 1).then_inc(ask_act, -1)
                        link(fn(xbc[:, s - 2, :], G[:, s % 2, :], ACT.Silu))
                        say(act, act_says, xbc_ready)
                    if s == 4:
                        act.wait_ge(ask_act, 1).then_inc(ask_act, -1)
                        link(fn(s16[:, 6, :], s16[:, 6, :], ACT.Exp), fn(s16[:, 7, :], s16[:, 5, :], ACT.Exp))
                        say(act, act_says)
                    if 8 <= s <= 9:
                        act.wait_ge(ask_act, 1).then_inc(ask_act, -1)
                        link(fn(z[:, s - 8, :], z[:, s - 8, :], ACT.Silu))
                        say(act, act_says)
                    if s == 9:
                        m2_head(0)
                    if 11 <= s <= 13:
                        m2_head(s - 10)
                    if s == 12:
                        m2_square(0)
                    if s == 14:
                        emit(MIXB, G[:, 4, :])
                        m2_square(1)
                    if s == 15:
                        emit(MIXB + 1, G[:, 5, :])
                    if s == 16:
                        act.wait_ge(act_bank[7], 1).then_inc(act_bank[7], -1)
                        rsqrt_mean(z[:, 0, :], bank[7][:, :], 2 * P)
                        say(act, bank_free[7], act_says)
                    if s == 17:
                        for i in range(2):
                            emit(MIXD + i, xbc[:, 4 + i, :])
                    if 17 <= s <= 24:
                        act.wait_ge(act_bank[4], 1).then_inc(act_bank[4], -1)
                        rsqrt_mean(G[:, 3 + (s - 17) % 2, :], bank[4][:, :], QK)
                        say(act, bank_free[4], act_says)
                    if 16 <= s <= 23:
                        qk_square(s - 16)
                    if s >= 25:
                        v_copy(s - 25)
                    if s == 19 or s == 27:
                        i = (s - 19) // 8
                        act.wait_ge(ask_act, 1).then_inc(ask_act, -1)
                        link(fn(u[:, i, :], u[:, i, :], ACT.Gelu_apprx_tanh))
                        say(act, act_says)

                def exps(n):
                    w, s = (n % NQ + 1) * P, n % 2
                    act.wait_ge(exp_go, 1).then_inc(exp_go, -1)
                    link(*[fn(G[:, 2 * s + c, 0:w], bank[(2, 3, 6, 7)[2 * s + c]][:, 0:w], ACT.Exp,
                              bias=soft[:, s, c:c + 1], accum_out=soft[:, s, 2 + c:3 + c]) for c in range(2)])
                    say(act, bank_free[(2, 6)[s]], bank_free[(3, 7)[s]], exp_done)

                def head_square():
                    act.wait_ge(osq_go, 1).then_inc(osq_go, -1)
                    link(fn(pad[:, 0, 4:4 + T], ssum[:, :], ACT.Square))
                    say(act, osq_ready)

                def head_rms():
                    act.wait_ge(act_bank[1], 1).then_inc(act_bank[1], -1)
                    rsqrt_mean(rbc[:, :], bank[1][:, :], P)
                    say(act, bank_free[1], onorm_done)

                v_copy(3)
                exps(0)
                for i, gate in enumerate((sA, sB)):
                    act.wait_ge(act_bank[6 + i], 1).then_inc(act_bank[6 + i], -1)
                    link(fn(gate[:, :], bank[6 + i][:, :], ACT.Sigmoid, bias=col("bglu", i)))
                    say(act, bank_free[6 + i], act_says)
                for i, gated in enumerate((sC, sD)):
                    emit(MIXC + i, gated[:, :])
                for n in range(STEPS):
                    if n + 1 < STEPS:
                        exps(n + 1)
                    act.wait_ge(act_bank[4], 1).then_inc(act_bank[4], -1)
                    w = (n % NQ + 1) * P
                    link(fn(G[:, 4 + n % 2, 0:w], bank[4][:, 0:w], ACT.Copy))
                    say(act, bank_free[4], probsT_ready)
                    if n > NQ and n % NQ == 1:
                        head_square()
                    if n and n % 2 == 0:
                        prep((n // 2 + 1) % 2, (KEARLY if n < 14 else HEADS) * P)
                    if n > NQ and n % NQ == 2:
                        head_rms()
                    if n > NQ and n % NQ == 3:
                        emit(MIXA + n // NQ - 1, ssum[:, :])
                prep(1, HEADS * P)
                head_square()
                head_rms()
                emit(MIXA + HEADS - 1, ssum[:, :])
                preps(6, HEADS * P)
                preps(2, KD * P)
                inputs("g2")
                prep(0, KD * P)
                rms()
                say(act, rms_ready)

                def ffn_tile(i, cols, first):
                    if not first:
                        prep(0, cols)
                    act.wait_ge(ask_act, 1).then_inc(ask_act, -1)
                    link(fn(G[:, 1, :], G[:, 0, :], ACT.Silu))
                    say(act, act_says)
                    prep(1, cols)
                    act.wait_ge(ask_act, 1).then_inc(ask_act, -1)
                    high(mh[:, bass.ds(i, 1), :].rearrange("p a b -> p (a b)"), G[:, 3, :])
                    say(act, act_says)

                for half in range(2):
                    ffn_tile(0, KD * P, half == 0)
                    with act.Fori(1, FHALF - 1) as i:
                        ffn_tile(i, KD * P, False)
                    ffn_tile(FHALF - 1, FHALF * P, False)
                    preps(6, FHALF * P)
                    if half == 0:
                        preps(2, KD * P)

        @blk.vector
        def _(dve):
            link = linker(dve, dve_own)
            tt, ts, stt = nc.vector.tensor_tensor, nc.vector.tensor_scalar, nc.vector.scalar_tensor_tensor
            copy = nc.vector.tensor_copy
            MUL, ADD, SUB = ALU.mult, ALU.add, ALU.subtract

            def flat(ap):
                return ap.rearrange("p a b -> p (a b)")

            def inputs(gain):
                link(nc.vector.memset(ssum[:, :], 0.0))
                say(dve, x_ready)
                for k in range(KD):
                    dve.wait_ge(sq_full, 1).then_inc(sq_full, -1)
                    link(stt(xl[:, k, :], x[:, k, :], col(gain, k), xh[:, k, :].bitcast(F32), MUL, SUB),
                         tt(ssum[:, :], ssum[:, :], G[:, k % 2, :], ADD))
                    say(dve, xk_ready, sq_free)
                say(dve, ssum_ready)

            def scaled(out, p):
                dve.wait_ge(dve_bank[p], 1).then_inc(dve_bank[p], -1)
                link(tt(out, bank[p][:, :], rbc[:, :], MUL))
                say(dve, bank_free[p])

            def taps(out, p, weights, first, bias=None):
                n = len(weights)
                if bias is None:
                    link(ts(out, pad[:, p, 4:4 + T], weights[n - 1], None, MUL))
                else:
                    link(ts(out, pad[:, p, 4:4 + T], weights[n - 1], bias, MUL, ADD))
                for k in range(1, n):
                    link(stt(out, pad[:, p, 4 - k:4 - k + T], weights[n - 1 - k], out, MUL, ADD))

            def emit_low(tile, buf):
                dve.wait_ge(em_high, 1).then_inc(em_high, -1)
                link(tt(ml[:, tile, :], buf, mh[:, tile, :].bitcast(F32), SUB))
                say(dve, mixed_ready)

            def emit(tile, buf):
                say(dve, em_full)
                emit_low(tile, buf)

            def residual(o, p):
                dve.wait_ge(dve_bank[p], 1).then_inc(dve_bank[p], -1)
                xo = flat(x[:, bass.ds(o, 1), :])
                link(tt(xo, xo, bank[p][:, :], ADD))
                say(dve, bank_free[p])

            def residuals():
                with dve.Fori(0, KD // 2) as o:
                    residual(o * 2, 0)
                    residual(o * 2 + 1, 1)

            def parameters(l):
                link(copy(par[:, :], flat(par_all[:, bass.ds(l, 1), :])),
                     copy(cf[:].rearrange("p a b c -> p (a b c)"), flat(cf_all[:, bass.ds(l, 1), :])),
                     copy(rho[:, :], flat(rho_all[:, bass.ds(l, 1), :])), copy(mlam[:, :], mlam_all[:, bass.ds(l, 1)]))
                w = par[:, PARAMS["wdt"][0]:PARAMS["wdt"][0] + KD * M2H]
                link(copy(flat(wdth[:]), w),
                     ts(col("qkg"), col("qkg"), QK ** -0.5, None, MUL),
                     ts(col("subg"), col("subg"), col("oneml"), None, MUL))
                link(tt(flat(wdtl[:]), w, flat(wdth[:]).bitcast(F32), SUB),
                     *[ts(permg[:, i, :], perm, col("qkg", i), None, MUL) for i in range(2)])
                say(dve, wdt_ready)

            def m2_dt():
                a, e, s, sq, q, rec = [s16[:, i, :] for i in (0, 1, 2, 9, 10, 11)]
                by_head = [P, NQ, M2H]
                dve.wait_ge(dve_bank[5], 1).then_inc(dve_bank[5], -1)
                link(tt(a.rearrange("p (a b) -> p a b", a=NQ), bank[5][:, 0:16].rearrange("p (a b) -> p a b", a=NQ),
                        rtok[:, :, 0:1].broadcast_to(by_head), MUL))
                say(dve, bank_free[5])
                link(tt(a.rearrange("p (a b) -> p a b", a=NQ), a.rearrange("p (a b) -> p a b", a=NQ),
                        col("dtb", 0, M2H).unsqueeze(1).broadcast_to(by_head), ADD))
                link(stt(e, a, -1.0, a, MUL, ALU.max))
                say(dve, ask_act)
                link(ts(a, a, 0.0, None, ALU.max))
                dve.wait_ge(act_says, 1).then_inc(act_says, -1)
                link(ts(rec, e, 2.0, None, ADD))
                link(nc.vector.reciprocal(rec, rec))
                link(tt(s, e, rec, MUL))
                link(tt(sq, s, s, MUL))
                link(ts(q, sq, 1.0 / 17, None, MUL))
                for c in (15, 13, 11, 9, 7, 5, 3):
                    link(stt(q, q, 1.0 / c, sq, ADD, MUL))
                link(stt(q, q, 1.0, s, ADD, MUL))
                link(stt(a, q, 2.0, a, MUL, ADD))
                link(stt(adt.rearrange("p (a b) -> p a b", a=NQ), a.rearrange("p (a b) -> p a b", a=NQ), -1.0,
                         s16[:, 8, 0:M2H].unsqueeze(1).broadcast_to(by_head), MUL, MUL))
                say(dve, adt_ready)

            def reduced(ph, extra, k):
                if extra is not None:
                    link(tt(k, ph, extra, ADD))
                link(ts(k, ph if extra is None else k, INV2PI, ROUND, MUL, ADD))
                link(ts(k, k, ROUND, None, SUB))
                for c in (C1, C2, C3):
                    link(stt(ph, k, -c, ph, MUL, ADD))
                if extra is not None:
                    link(tt(ph, ph, extra, ADD))

            def before_layers():
                dt, r, F, _, th, thl, nre, nim, m2, inv, a, b, c, d, k = [s8[:, i] for i in range(15)]
                lre, lim = pre[:, :, PRE["lre"]], pre[:, :, PRE["lim"]]
                link(copy(dt, pre[:, :, PRE["ldt"]]))
                for l in range(L):
                    dal = pre[:, l, PRE["dal"]].rearrange("p (a b c) -> p a b c", a=2, b=2)
                    link(tt(lprod[:, :, :], dal[:, :, 0, :], dal[:, :, 1, :], MUL))
                    link(nc.vector.tensor_reduce(lam2[:, l, :], lprod[:, :, :], AX, ADD))
                say(dve, ask_act)
                link(tt(m2, lre, lre, MUL), tt(a, lim, lim, MUL))
                link(tt(m2, m2, a, ADD))
                link(nc.vector.reciprocal(inv, m2))
                dve.wait_ge(act_says, 1).then_inc(act_says, -1)
                link(tt(th, lim, dt, MUL), tt(r, lre, dt, MUL), tt(mlam_all[:, :], lam2[:, :, 1], lam2[:, :, 0], SUB))
                link(tt(mlam_all[:, :], mlam_all[:, :], pre[:, :, PRE["linit"]].rearrange("p a b -> p (a b)"), SUB))
                reduced(th, None, k)
                th_flat = th.rearrange("p a b -> p (a b)")
                thl_flat = thl.rearrange("p a b -> p (a b)")
                link(copy(thh[:, :], th_flat))
                link(tt(thl_flat, th_flat, thh[:, :].bitcast(F32), SUB))
                shape = [P, L * SJ, NT]
                ph, kk, lo = [flat(t[:]) for t in (ph0, kk0, lo0)]
                st3 = steps.unsqueeze(1).broadcast_to(shape)
                dve.wait_ge(cst_loaded, 16).then_inc(cst_loaded, -16)
                link(tt(ph0[:, :, :], thh[:, :].bitcast(F32).unsqueeze(2).broadcast_to(shape), st3, MUL),
                     tt(lo0[:, :, :], thl_flat.unsqueeze(2).broadcast_to(shape), st3, MUL))
                reduced(ph, lo, kk)
                link(ts(ph, ph, PI_CAP, -PI_CAP, ALU.min, ALU.max))
                say(dve, ask_act)
                link(ts(r, r, -100.0, 1.0 / 1024, ALU.max, MUL))
                link(ts(F, r, 1.0 / 5, 1.0, MUL, ADD))
                for n in (4, 3, 2):
                    link(tt(F, F, r, MUL))
                    link(ts(F, F, 1.0 / n, 1.0, MUL, ADD))
                link(tt(F, F, r, MUL))
                for _ in range(10):
                    link(stt(F, F, 2.0, F, ADD, MUL))
                link(ts(rho_all[:, :, :], F, 1.0, None, ADD))
                dve.wait_ge(act_says, 1).then_inc(act_says, -1)
                link(tt(lo, kk, kk, MUL))
                lo4 = lo0[:].rearrange("p (l j) n -> p l j n", l=L)
                link(*[ts(rot[:, l, 0], lo4[:, l], -2.0, 1.0, MUL, ADD) for l in range(L)])
                link(tt(nre, F, rot[:, :, 0, :, 1], MUL), stt(nim, F, 1.0, rot[:, :, 1, :, 1], ADD, MUL))
                link(stt(nre, lo4[:, :, :, 1], -2.0, nre, MUL, ADD))
                link(tt(a, nre, lre, MUL), tt(b, nim, lim, MUL), tt(c, nim, lre, MUL), tt(d, nre, lim, MUL))
                link(tt(a, a, b, ADD), tt(c, c, d, SUB))
                link(tt(a, a, inv, MUL), tt(c, c, inv, MUL))
                cs = [P, SJ, SH]
                for l in range(L):
                    cre, cim = [cmat[:, l, i].rearrange("p (a b) -> p a b", a=SJ) for i in range(2)]
                    A3, B3, C3_, D3 = [ctmp[:, i].rearrange("p (a b) -> p a b", a=SJ) for i in range(4)]
                    fre, fim = a[:, l].unsqueeze(2).broadcast_to(cs), c[:, l].unsqueeze(2).broadcast_to(cs)
                    link(tt(A3, cre, fre, MUL), tt(B3, cim, fim, MUL), tt(C3_, cre, fim, MUL), tt(D3, cim, fre, MUL))
                    o = SJ * SH
                    link(tt(cf_all[:, l, 0:o], ctmp[:, 0], ctmp[:, 1], SUB), tt(ctmp[:, 2], ctmp[:, 2], ctmp[:, 3], ADD))
                    link(ts(cf_all[:, l, o:2 * o], ctmp[:, 2], -1.0, None, MUL))

            def s5(j):
                cs, sn = [t[:, :] for t in tab[j % 2]]
                a, b, c, d, e = sA[:, :], sB[:, :], sC[:, :], sD[:, :], sE[:, :]
                if j % 4:
                    dve.wait_ge(s5x_read, 1).then_inc(s5x_read, -1)
                dve.wait_ge(tab_full, 1).then_inc(tab_full, -1)
                dve.wait_ge(dve_bank[2], 1).then_inc(dve_bank[2], -1)
                dve.wait_ge(dve_bank[3], 1).then_inc(dve_bank[3], -1)
                link(tt(a, bank[2][:, :], cs, MUL), tt(b, bank[3][:, :], sn, MUL),
                     tt(c, bank[3][:, :], cs, MUL), tt(d, bank[2][:, :], sn, MUL))
                say(dve, bank_free[2], bank_free[3])
                link(tt(a, a, b, ADD), tt(c, c, d, SUB))
                decay = rho[:, j:j + 1].broadcast_to([P, T])
                link(nc.vector.tensor_tensor_scan(b, decay, a, 0.0, MUL, ADD),
                     nc.vector.tensor_tensor_scan(d, decay, c, 0.0, MUL, ADD))
                link(tt(a, b, cs, MUL), tt(c, d, sn, MUL))
                link(tt(e, a, c, SUB))
                link(tt(a, b, sn, MUL), tt(c, d, cs, MUL))
                if j < SJ - 2:
                    say(dve, tab_free)
                link(tt(a, a, c, ADD))
                say(dve, s5x_ready)

            def s5_finish(i):
                dve.wait_ge(s5x_read, 1).then_inc(s5x_read, -1)
                link(stt(u[:, i, :], u[:, i, :], col("s5d", i), bank[6][:, :], MUL, ADD))
                say(dve, bank_free[6], ask_act)

            def m2_sums():
                dve.wait_ge(dve_bank[7], 1).then_inc(dve_bank[7], -1)
                link(copy(flat(s16[:, 4:6, :]), bank[7][:, 0:32]))
                say(dve, bank_free[7])
                link(tt(s16[:, 6, :], s16[:, 5, :], s16[:, 4, :], SUB))
                say(dve, ask_act)

            hs = [P, M2H, M2P]

            def m2_turned(t):
                b, hc = (4, 7)[t % 2], slice(t * M2H, (t + 1) * M2H)
                dve.wait_ge(dve_bank[b], 1).then_inc(dve_bank[b], -1)
                xdt = xbt[:, t, 0:2, :].rearrange("p a b -> p (a b)").rearrange("p (h c) -> p h c", h=M2H)
                w = [tt(xdt, bank[b][:, 0:2 * P].rearrange("p (h c) -> p h c", h=M2H),
                        s16[:, 0, hc].unsqueeze(2).broadcast_to(hs), MUL)]
                if t < NQ - 1:
                    w.append(copy(flat(xbt[:, t, 2:4, :]), bank[b][:, 2 * P:4 * P]))
                link(*w)
                say(dve, bank_free[b])
                if t < NQ - 1:
                    link(tt(xds[:, t], xdt, s16[:, 6, hc].unsqueeze(2).broadcast_to(hs), MUL))
                say(dve, xbt_ready)

            def m2_state(t):
                if t != 1:
                    dve.wait_ge(dve_bank[5], 1).then_inc(dve_bank[5], -1)
                o = 2 * P * (t % 2)
                st = bank[5][:, o:o + 2 * P].rearrange("p (h c) -> p h c", h=M2H)
                if t == 0:
                    link(copy(hst[:, 0], st))
                else:
                    cd = s16[:, 7, t * M2H:(t + 1) * M2H].unsqueeze(2).broadcast_to(hs)
                    link(tt(hst[:, t], hst[:, t - 1], cd, MUL))
                    link(tt(hst[:, t], hst[:, t], st, ADD))
                if t:
                    say(dve, bank_free[5])

            def m2_logs(h):
                dve.wait_ge(dve_bank[4], 1).then_inc(dve_bank[4], -1)
                logs = m2buf[h % 2][0]
                link(*[stt(logs[:, t * P:(t + 1) * P], bank[4][:, t * P:(t + 1) * P],
                           s16[:, 4, t * M2H + h:t * M2H + h + 1], cap, SUB, ALU.min) for t in range(NQ)])
                say(dve, ask_act)

            def m2_mix(h):
                dve.wait_ge(act_says, 1).then_inc(act_says, -1)
                if h % 2 == 0:
                    dve.wait_ge(dve_bank[7], 1).then_inc(dve_bank[7], -1)
                e, ec = m2buf[h % 2]
                link(tt(ec, ec, xbc[:, 4 + h // 2, :], MUL), tt(e, e, bank[7][:, :], MUL))
                if h % 2:
                    say(dve, bank_free[7])
                say(dve, mix_ready)

            def m2_pair(i):
                link(stt(xbc[:, i, :], xbc[:, i, :], col("m2d", i), bank[5][:, :], MUL, ADD))
                say(dve, bank_free[5])
                link(tt(xbc[:, i, :], xbc[:, i, :], z[:, i, :], MUL))
                say(dve, ask_act)

            def sc_product(i):
                scaled(pad[:, i, 4:4 + T], i)
                link(tt(pad[:, i, 4:4 + T], pad[:, i, 4:4 + T], G[:, 4 + i, :], MUL))

            def sc_conv(i):
                taps(G[:, 4 + i, :], i, [col("scw", 3 * i + k) for k in range(3)], 0)

            def sc_gate(i):
                scaled(G[:, 0, :], i)
                link(tt(G[:, 4 + i, :], G[:, 0, :], G[:, 4 + i, :], MUL))
                say(dve, em_full)

            def qk_finish(t):
                p, q = t % 2, qk[:, t, :]
                link(stt(q, G[:, p, :], col("qkg", p), cosT, MUL, MUL))
                dve.wait_ge(dve_bank[5], 1).then_inc(dve_bank[5], -1)
                link(tt(G[:, 5, :], bank[5][:, :], sinT, MUL))
                say(dve, bank_free[5])
                link(tt(q, q, G[:, 5, :], ADD))
                dve.wait_ge(act_says, 1).then_inc(act_says, -1)
                link(tt(q, q, G[:, 3 + p, :], MUL))

            def maxima(n):
                s, w = n % 2, (n % NQ + 1) * P
                banks = (2, 3, 6, 7)[2 * s:2 * s + 2]
                for b in banks:
                    dve.wait_ge(dve_bank[b], 1).then_inc(dve_bank[b], -1)
                link(*[nc.vector.tensor_reduce(soft[:, s, c:c + 1], bank[b][:, 0:w], AX, ALU.max, negate=True)
                       for c, b in enumerate(banks)])
                say(dve, exp_go)

            def combine(n):
                s, w = n % 2, (n % NQ + 1) * P
                dve.wait_ge(exp_done, 1).then_inc(exp_done, -1)
                link(nc.vector.reciprocal(soft[:, s, 4:6], soft[:, s, 2:4]))
                link(ts(G[:, 2 * s + 1, 0:w], G[:, 2 * s + 1, 0:w], soft[:, s, 5:6], mlam[:, :], MUL, MUL))
                link(stt(G[:, 2 * s, 0:w], G[:, 2 * s, 0:w], soft[:, s, 4:5], G[:, 2 * s + 1, 0:w], MUL, ADD))
                say(dve, probs_ready)

            def head_out():
                dve.wait_ge(dve_bank[5], 1).then_inc(dve_bank[5], -1)
                link(copy(ssum[:, :], bank[5][:, :]))
                say(dve, bank_free[5], osq_go)

            def head_emit(h):
                dve.wait_ge(onorm_done, 1).then_inc(onorm_done, -1)
                link(stt(ssum[:, :], ssum[:, :], col("subg"), rbc[:, :], MUL, MUL))
                emit(MIXA + h, ssum[:, :])

            def ffn_tile(half, i):
                scaled(pad[:, 0, 4:4 + T], 0)
                w0 = PARAMS["ffw"][0] + half * FHALF * 3
                taps(G[:, 0, :], 0, [par[:, bass.ds(i * 3 + (w0 + k), 1)] for k in range(3)], 0)
                say(dve, ask_act)
                scaled(G[:, 2, :], 1)
                dve.wait_ge(act_says, 1).then_inc(act_says, -1)
                link(tt(G[:, 3, :], G[:, 1, :], G[:, 2, :], MUL))
                say(dve, ask_act)
                dve.wait_ge(act_says, 1).then_inc(act_says, -1)
                link(tt(flat(ml[:, bass.ds(i, 1), :]), G[:, 3, :], flat(mh[:, bass.ds(i, 1), :]).bitcast(F32), SUB))
                say(dve, hid_ready)

            link(nc.vector.memset(pad[:, :, :], 0.0))
            say(dve, *bank_free, sq_free, sq_free, mats_free)
            dve.wait_ge(pre_loaded, 32).then_inc(pre_loaded, -32)
            before_layers()
            link(copy(cbf[:, 0, :], ident), copy(cbf[:, 1, :], cst[:, CONSTS["mask"]]))
            say(dve, act_go, pe_go)
            dve.wait_ge(par_loaded, 16).then_inc(par_loaded, -16)
            dve.wait_ge(x_loaded, 16 * KD).then_inc(x_loaded, -(16 * KD))
            with dve.Fori(0, L) as l:
                parameters(l)
                inputs("g1")
                dve.wait_ge(rms_ready, 1).then_inc(rms_ready, -1)
                say(dve, tab_free, tab_free)
                for i in range(2):
                    scaled(u[:, i, :], i)
                dve.wait_ge(mats_full, 32).then_inc(mats_full, -32)
                say(dve, u_ready)
                m2_dt()
                for s in range(2, NIN):
                    if 2 <= s <= 7:
                        scaled(pad[:, s % 2, 4:4 + T], s % 2)
                        if s >= 4:
                            dve.wait_ge(act_says, 1).then_inc(act_says, -1)
                        if s == 6:
                            dve.wait_ge(act_says, 1).then_inc(act_says, -1)
                        taps(G[:, s % 2, :], s % 2, [col("m2w", 4 * (s - 2) + k) for k in range(4)], 0,
                             col("m2b", s - 2))
                        say(dve, ask_act)
                    if s == 4:
                        m2_sums()
                    if s == 7:
                        m2_turned(0)
                        m2_turned(1)
                    if 8 <= s <= 9:
                        scaled(z[:, s - 8, :], s % 2)
                        dve.wait_ge(act_says, 1).then_inc(act_says, -1)
                        say(dve, ask_act)
                    if s == 8:
                        m2_turned(2)
                        m2_turned(3)
                    if s == 9:
                        m2_logs(0)
                        m2_state(0)
                        m2_state(1)
                        dve.wait_ge(act_says, 1).then_inc(act_says, -1)
                        dve.wait_ge(act_says, 1).then_inc(act_says, -1)
                        m2_mix(0)
                    if 10 <= s <= 11:
                        scaled(G[:, 4 + s % 2, :], s % 2)
                    if s == 10:
                        m2_state(2)
                        say(dve, hst_ready)
                        s5(0)
                    if s == 11:
                        m2_logs(1)
                        m2_mix(1)
                    if 12 <= s <= 13:
                        sc_product(s % 2)
                        if s == 12:
                            dve.wait_ge(mix_read, 1).then_inc(mix_read, -1)
                            dve.wait_ge(mix_read, 1).then_inc(mix_read, -1)
                        m2_logs(s - 10)
                        if s == 12:
                            m2_pair(0)
                        sc_conv(s % 2)
                        m2_mix(s - 10)
                    if 14 <= s <= 15:
                        sc_gate(s % 2)
                    if s == 14:
                        dve.wait_ge(mix_read, 1).then_inc(mix_read, -1)
                        dve.wait_ge(mix_read, 1).then_inc(mix_read, -1)
                        m2_pair(1)
                        s5(1)
                    if 14 <= s <= 15:
                        emit_low(MIXB + s % 2, G[:, 4 + s % 2, :])
                    if 16 <= s <= 23:
                        scaled(G[:, s % 2, :], s % 2)
                        say(dve, ask_act)
                    if s == 16:
                        dve.wait_ge(act_says, 1).then_inc(act_says, -1)
                        link(*[stt(xbc[:, 4 + i, :], xbc[:, i, :], col("m2g", i), z[:, 0, :], MUL, MUL) for i in range(2)])
                        say(dve, em_full, em_full)
                    if s == 17:
                        for i in range(2):
                            emit_low(MIXD + i, xbc[:, 4 + i, :])
                    if s == 20:
                        dve.wait_ge(act_says, 1).then_inc(act_says, -1)
                    if 17 <= s <= 24:
                        qk_finish(s - 17)
                    if s >= 24:
                        if s >= 26:
                            dve.wait_ge(vch_read, 1).then_inc(vch_read, -1)
                        scaled(G[:, s % 2, :], s % 2)
                        say(dve, vch_ready)
                    if 16 <= s <= 26 and s % 2 == 0:
                        s5((s - 12) // 2)
                    if s == 19:
                        s5_finish(0)
                    if s == 24:
                        say(dve, qk_ready)
                s5_finish(1)
                maxima(0)
                dve.wait_ge(act_says, 1).then_inc(act_says, -1)
                say(dve, glu_in)
                for i, (gate, gated) in enumerate(((sA, sC), (sB, sD))):
                    dve.wait_ge(act_says, 1).then_inc(act_says, -1)
                    link(tt(gated[:, :], gate[:, :], u[:, i, :], MUL))
                    say(dve, em_full)
                say(dve, mats_free)
                for _ in range(2):
                    dve.wait_ge(vch_read, 1).then_inc(vch_read, -1)
                maxima(1)
                for i, gated in enumerate((sC, sD)):
                    emit_low(MIXC + i, gated[:, :])
                combine(0)
                for n in range(STEPS):
                    if n + 2 < STEPS:
                        maxima(n + 2)
                    if n + 1 < STEPS:
                        combine(n + 1)
                    if n and n % 2 == 0:
                        residual(n // 2 - 1, (n // 2 - 1) % 2)
                    if n >= NQ and n % NQ == 0:
                        head_out()
                    if n > NQ and n % NQ == 3:
                        head_emit(n // NQ - 1)
                residual(STEPS // 2 - 1, 1)
                head_out()
                head_emit(HEADS - 1)
                residuals()
                inputs("g2")
                dve.wait_ge(rms_ready, 1).then_inc(rms_ready, -1)
                for half in range(2):
                    with dve.Fori(0, FHALF) as i:
                        ffn_tile(half, i)
                    residuals()
            say(dve, out_ready)


def constants():
    c = np.zeros((P, NCONST), np.float32)
    r = np.arange(P)
    c[:, CONSTS["ident"]] = np.eye(P)
    c[:, CONSTS["ones"]] = 1
    c[:, CONSTS["tri"]] = r[:, None] <= r[None, :]
    perm, cos, sin = np.zeros((P, P)), np.ones((P, T)), np.zeros((P, T))
    inv = (1.0 / (THETA ** (np.arange(0, ROPE, 2, dtype=np.float32) / ROPE))).astype(np.float32)
    ang = np.arange(T, dtype=np.float32)[:, None] * inv[None, :]
    half = ROPE // 2
    for b in range(2):
        for i in range(half):
            lo, hi = b * QK + i, b * QK + half + i
            perm[hi, lo], perm[lo, hi] = -1, 1
            cos[lo], cos[hi] = np.cos(ang[:, i]), np.cos(ang[:, i])
            sin[lo], sin[hi] = np.sin(ang[:, i]), np.sin(ang[:, i])
    c[:, CONSTS["perm"]], c[:, CONSTS["cos"]], c[:, CONSTS["sin"]] = perm, cos, sin
    c[:, CONSTS["block"]] = r[:, None] // QK == r[None, :] // QK
    c[:, CONSTS["cap"]] = np.where(r[None, :] >= r[:, None], 0.0, NEG)
    c[:, CONSTS["mask"]] = np.where(r[None, :] <= r[:, None], 0.0, NEG)
    c[:, CONSTS["steps"]] = np.concatenate([np.arange(FINE), FINE * np.arange(COARSE)])
    c[:, CONSTS["eps"]] = EPS
    return c


def layout(inp):
    def units(w, first_k=0, K=None):
        K = w.shape[1] // P if K is None else K
        w = w[:, first_k * P:(first_k + K) * P].reshape(L, K, P, -1, P)
        return np.ascontiguousarray(w.transpose(0, 3, 2, 1, 4)).reshape(L, -1, P, K * P)

    w = inp["w_in"]
    a, b, c = 512, 1024, 1536
    sc, s5, z, xbc, dt = 1536, 2304, 2560, 2816, 3584
    order = [w[:, :, s5:z], w[:, :, xbc:dt], w[:, :, z:xbc], w[:, :, sc + 256:sc + 512], w[:, :, sc + 512:s5],
             w[:, :, sc:sc + 256]]
    for h in range(HEADS):
        order += [w[:, :, h * P:(h + 1) * P], w[:, :, a + h * P:a + (h + 1) * P]]
    w_in = units(np.concatenate(order + [w[:, :, b:c]], axis=2))
    gu = np.stack([units(inp["ffn_w_gate"]), units(inp["ffn_w_up"])], axis=2).reshape(L, 2 * FF, P, KD * P)
    dn = np.stack([units(inp["ffn_w_down"], h * FHALF, FHALF) for h in range(2)], axis=1).reshape(L, 16, P, FHALF * P)

    par = np.zeros((P, L, NPAR), np.float32)

    def put(name, value):
        o, n = PARAMS[name]
        par[:, :, o:o + n] = np.broadcast_to(value, (L, P, n)).transpose(1, 0, 2)

    def tiled(p):
        return p.reshape(L, -1, P).transpose(0, 2, 1)

    put("g1", tiled(inp["ln1_g"]))
    put("g2", tiled(inp["ln2_g"]))
    put("qkg", np.tile(inp["qk_norm_g"], (1, 1, 2)).transpose(0, 2, 1))
    put("subg", tiled(inp["subln_g"]))
    init = np.array([0.8 - 0.6 * np.exp(-0.3 * l) for l in range(L)], np.float32)
    put("oneml", (np.float32(1) - init).reshape(L, 1, 1))
    put("scw", inp["sc_conv_w"].reshape(L, 3, 2, P).transpose(0, 3, 2, 1).reshape(L, P, 6))

    def states(p):
        return p.reshape(L, SJ, P).transpose(0, 2, 1)

    put("s5d", tiled(inp["s5_d"]))
    put("bglu", tiled(inp["s5_b_glu"]))
    put("m2w", inp["m2_conv_w"].reshape(L, 4, 6, P).transpose(0, 3, 2, 1).reshape(L, P, 24))
    put("m2b", tiled(inp["m2_conv_b"]))
    put("dtb", inp["m2_dt_bias"][:, None, :])
    put("alog", inp["m2_a_log"][:, None, :])
    put("m2d", tiled(np.repeat(inp["m2_d"], M2P, axis=1)))
    put("m2g", tiled(inp["m2_norm_g"]))
    put("ffw", inp["ffn_conv_w"].reshape(L, 3, FF, P).transpose(0, 3, 2, 1).reshape(L, P, 3 * FF))
    put("wdt", w[:, :, dt:].reshape(L, KD, P, M2H).transpose(0, 2, 1, 3).reshape(L, P, KD * M2H))

    pre = np.zeros((P, L, NPRE), np.float32)
    pre[:, :, PRE["lre"]] = states(inp["s5_lam_re"]).transpose(1, 0, 2)
    pre[:, :, PRE["lim"]] = states(inp["s5_lam_im"]).transpose(1, 0, 2)
    pre[:, :, PRE["ldt"]] = states(np.repeat(inp["s5_log_dt"], 64, axis=1)).transpose(1, 0, 2)
    pre[:, :, PRE["dal"]] = inp["da_lambda"].reshape(1, L, 4 * QK)
    pre[:, :, PRE["linit"]] = init.reshape(1, L, 1)

    bmat = np.zeros((L, 2, 4, 2, 16, 2, 2, 64), np.float32)
    cmat = np.zeros((L, 2, 64, 2, SJ, 2, 16), np.float32)
    for ci, (bn, cn) in enumerate((("s5_b_re", "s5_c_re"), ("s5_b_im", "s5_c_im"))):
        bb = inp[bn].reshape(L, 2, 4, 2, 64, 16)
        cc = inp[cn].reshape(L, SJ, 2, 16, 64)
        for g in range(2):
            bmat[:, :, :, g, :, ci, g, :] = bb[:, :, :, g].transpose(0, 1, 2, 4, 3)
            cmat[:, g, :, ci, :, g, :] = cc[:, :, g].transpose(0, 3, 1, 2)
    bmat = bmat.transpose(0, 2, 3, 4, 5, 1, 6, 7).reshape(L, P, 2 * 2 * P)
    cmat = np.ascontiguousarray(cmat.reshape(L, P, 2, SJ * SH).transpose(1, 0, 2, 3))
    wglu = inp["s5_w_glu"].reshape(L, 2, P, 256).transpose(0, 2, 1, 3).reshape(L, P, 512)
    return {
        "x": inp["x"].reshape(T, KD, P).transpose(2, 1, 0), "par": par, "pre": pre, "cst": constants(),
        "w_in": w_in, "w_oe": units(inp["w_out"], HEADS, KEARLY), "w_ol": units(inp["w_out"], 0, HEADS),
        "w_gu": gu, "w_dn": dn, "bmat": bmat, "cmat": cmat, "wglu": wglu,
    }


def kernel(**inputs):
    import concourse.bacc as bacc
    from concourse.bass_utils import run_bass_kernel_spmd as run

    arrays = layout({k: np.asarray(a) for k, a in inputs.items()})
    arrays = {f"in_{k}": np.ascontiguousarray(a) for k, a in arrays.items()}
    nc = bacc.Bacc("TRN2", target_bir_lowering=False, num_devices=1)
    A = {k[3:]: nc.dram_tensor(k, a.shape, mybir.dt.from_np(a.dtype), kind="ExternalInput").ap()
         for k, a in arrays.items()}
    A["out"] = nc.dram_tensor("out_x", (P, KD, T), F32, kind="ExternalOutput").ap()
    build(nc, A)
    out = run(nc, [arrays], core_ids=[0]).results[0]["out_x"]
    return np.ascontiguousarray(out.transpose(2, 1, 0)).reshape(1, T, D)
```

```python
from contextlib import ExitStack

import numpy as np

import concourse.bass as bass
from concourse import mybir

F32 = mybir.dt.float32
F32R = mybir.dt.float32r
BF16 = mybir.dt.bfloat16
ALU = mybir.AluOpType
ACT = mybir.ActivationFunctionType
AX = mybir.AxisListType.X

L = 2
D, T, P = 1024, 512, 128
KD = D // P
NQ = T // P
HEADS, QK = 4, 64
ROPE = 16
THETA = 500000.0
SJ, SH = 8, 32
M2H, M2P = 4, 64
FF, FHALF = 22, 11
MIXA, MIXB, MIXC, MIXD = 0, 4, 6, 8
MIXED = 10
KEARLY = MIXED - HEADS
STEPS = HEADS * NQ
TABLE_AT = [2, 5, 14, 16, 18, 20, 22, 24]
BESIDE = [3, 5, 7, 9, 11, STEPS - 1]
HEAD_BANK = [1, 1, 0, 6]
EPS = 1e-6
NIN = 28
FINE, COARSE = 32, 16
NT = FINE + COARSE
NEG = -1e30
INV2PI = float(np.float32(1 / (2 * np.pi)))
ROUND = float(1.5 * 2**23)
C1 = 6.28125
C2 = float(np.float32(np.round((2 * np.pi - C1) * 2**21) / 2**21))
C3 = float(np.float32(2 * np.pi - C1 - C2))
PI_CAP = 3.1415925

CONSTS, _o = {}, 0
for _name, _n in [("ident", P), ("ones", P), ("tri", P), ("perm", P), ("block", P), ("cap", P), ("eps", 1)]:
    CONSTS[_name] = slice(_o, _o + _n)
    _o += _n
NCONST = _o
PARAMS, _o = {}, 0
for _name, _n in [("g1", KD), ("g2", KD), ("qkg", 2), ("subg", 1), ("oneml", 1), ("scw", 6),
                  ("s5d", 2), ("bglu", 2), ("m2w", 24), ("m2b", 6),
                  ("dtb", M2H), ("alog", M2H), ("m2d", 2), ("m2g", 2), ("ffw", 3 * FF), ("wdt", KD * M2H)]:
    PARAMS[_name] = (_o, _n)
    _o += _n
NPAR = _o
PRE, _o = {}, 0
for _name, _n in [("dal", 4 * QK), ("lre", SJ), ("lim", SJ), ("ldt", SJ), ("linit", 1), ("steps", NT),
                  ("mask", P)]:
    PRE[_name] = slice(_o, _o + _n)
    _o += _n
NPRE = _o


def build(nc, A):
    with ExitStack() as ctx:
        arena_end = [0]

        def sb(name, shape, dt=F32, at=None):
            size = int(np.prod(shape[1:])) * (2 if dt == BF16 else 4)
            size = -(-size // 32) * 32
            off = arena_end[0] if at is None else at
            if at is None:
                arena_end[0] += size
            offsets[name] = off
            return nc.alloc_sbuf_tensor_at(name, list(shape), dt, offset=base + off)

        def sem(name):
            return ctx.enter_context(nc.semaphore(name))

        offsets = {}
        base = -(-nc.sbuf_base // 32) * 32
        arena_bytes = nc.sbuf_bytes_remaining - 32

        x = sb("x", [P, KD, T])
        xh = sb("xh", [P, KD, T], F32R)
        xl = sb("xl", [P, KD, T], F32R)
        mh = sb("mh", [P, FHALF, T], F32R)
        ml = sb("ml", [P, FHALF, T], F32R)
        raw = sb("raw", [P, 2, FHALF * P])
        wh = sb("wh", [P, 2, FHALF * P], F32R)
        wl = sb("wl", [P, 2, FHALF * P], F32R)
        qk = sb("qk", [P, 8, T])
        v = sb("v", [P, NQ, HEADS * P])
        xbc = sb("xbc", [P, 6, T], at=offsets["qk"])
        z = sb("z", [P, 2, T], at=offsets["qk"] + 6 * T * 4)
        xbt = sb("xbt", [P, NQ, 4, P], at=offsets["v"])
        u = sb("u", [P, 2, T])
        pad = sb("pad", [P, 2, 4 + T])
        G = sb("G", [P, 6, T])
        rbc = sb("rbc", [P, T])
        ssum = sb("ssum", [P, T])
        sA, sB, sC, sD = [sb(f"s5{n}", [P, T], at=offsets["mh"] + i * T * 4) for i, n in enumerate("abcd")]
        sE, rotc, rots, s5t = [sb(f"s5{n}", [P, T], at=offsets["ml"] + i * T * 4) for i, n in enumerate("efgh")]
        ex = [sb(f"ex{i}", [P, T], at=offsets[n] + (FHALF - 1) * T * 4) for i, n in enumerate(("mh", "ml"))]
        tab = [(rotc, rots), (ssum, ex[1])]
        m2buf = [(G[:, 1], G[:, 2]), (G[:, 3], ex[0][:, :])]
        pre_end = [offsets["mh"]]

        def early(name, shape, dt=F32):
            t = sb(name, shape, dt, at=pre_end[0])
            pre_end[0] += -(-int(np.prod(shape[1:])) * 4 // 32) * 32
            return t

        pre = early("pre", [P, L, NPRE])
        ph0, kk0, lo0 = [early(n, [P, L * SJ, NT]) for n in ("phase", "turns", "phase_low")]
        lprod = early("lprod", [P, 2, QK])
        lam2 = early("lam2", [P, L, 2])
        s8 = early("s8", [P, 16, L, SJ])
        thh = early("thh", [P, L * SJ], F32R)
        assert pre_end[0] <= offsets["ml"] + FHALF * T * 4
        bmat = sb("bmat", [P, 2, 2, P])
        cmat = sb("cmat", [P, L, 2, SJ * SH])
        factors = sb("factors", [P, 2, L, SJ])
        cf = sb("cf", [P, 2, SJ, SH])
        wglu = sb("wglu", [P, 2, 256])
        xds = sb("xds", [P, NQ - 1, M2H, M2P])
        s5im = sb("s5im", [P, T], at=offsets["xds"])
        hst = sb("hst", [P, NQ - 1, M2H, M2P])
        rot = sb("rot", [P, L, 2, SJ, NT])
        rho_all = sb("rho_all", [P, L, SJ])
        rho = sb("rho", [P, SJ])
        permg = sb("permg", [P, 2, P])
        par_all = sb("par_all", [P, L + 1, NPAR])
        par = sb("par", [P, NPAR])
        cst = sb("cst", [P, NCONST])
        rotary = sb("rotary", [P, 2, T])
        cbf = sb("cbf", [P, 2, P], BF16)
        wdth = sb("wdth", [P, KD, M2H], F32R)
        wdtl = sb("wdtl", [P, KD, M2H], F32R)
        s16 = sb("s16", [P, 12, NQ * M2H])
        mlam_all = sb("mlam_all", [P, L])
        mlam = sb("mlam", [P, 1])
        soft = sb("soft", [P, 2, 8])
        assert arena_end[0] <= arena_bytes, (arena_end[0], arena_bytes)

        bank = [ctx.enter_context(nc.psum_tensor(f"bank{b}", [P, T], F32)) for b in range(8)]

        def col(name, i=0, n=1):
            return par[:, PARAMS[name][0] + i:PARAMS[name][0] + i + n]

        ident, ones, tri, perm, block1, cap = [
            cst[:, CONSTS[k]] for k in ("ident", "ones", "tri", "perm", "block", "cap")]
        cosT, sinT = rotary[:, 0, :], rotary[:, 1, :]
        eps = cst[:, CONSTS["eps"]]
        adt = s16[:, 3, :]

        bank_free = [sem(f"bank_free{b}") for b in range(8)]
        dve_bank = [sem(f"dve_bank{b}") for b in range(8)]
        act_bank = [sem(f"act_bank{b}") for b in range(8)]
        raw_full, raw_free = [sem(f"raw_full{p}") for p in range(2)], sem("raw_free")
        wh_full, wh_free, wh_low = sem("wh_full"), sem("wh_free"), sem("wh_low")
        wl_full, wl_free = sem("wl_full"), sem("wl_free")
        x_loaded = [sem("x_loaded_first"), sem("x_loaded_last")]
        par_loaded, cst_loaded = sem("par_loaded"), sem("cst_loaded")
        act_go, pe_go = sem("act_go"), sem("pe_go")
        mats_full, mats_free = sem("mats_full"), sem("mats_free")
        out_ready, out_done = sem("out_ready"), sem("out_done")
        dve_own, act_own, pool_own = sem("dve_own"), sem("act_own"), sem("pool_own")
        cf_ready = sem("cf_ready")
        pre_loaded, late_loaded = sem("pre_loaded"), sem("late_loaded")
        x_ready = sem("x_ready")
        xh_full, sq_full, sq_free = sem("xh_full"), sem("sq_full"), sem("sq_free")
        xk_ready, ssum_ready = sem("xk_ready"), sem("ssum_ready")
        rms_ready = sem("rms_ready")
        ask_act, act_says = sem("ask_act"), sem("act_says")
        exp_go, exp_done, osq_go, onorm_done = sem("exp_go"), sem("exp_done"), sem("osq_go"), sem("onorm_done")
        em_full, em_high = sem("em_full"), sem("em_high")
        wdt_ready, dt_ready, adt_ready = sem("wdt_ready"), sem("dt_ready"), sem("adt_ready")
        u_ready, s5x_ready, s5x_read = sem("u_ready"), sem("s5x_ready"), sem("s5x_read")
        s5w_ready, s5w_read, s5im_ready, s5im_read = [
            sem(n) for n in ("s5w_ready", "s5w_read", "s5im_ready", "s5im_read")]
        glu_in = sem("glu_in")
        xbc_ready, xbt_ready, hst_ready = sem("xbc_ready"), sem("xbt_ready"), sem("hst_ready")
        mix_ready, mix_read, m2sq_ready = sem("mix_ready"), sem("mix_read"), sem("m2sq_ready")
        sqk_ready, qk_ready = sem("sqk_ready"), sem("qk_ready")
        vch_ready, vch_read = sem("vch_ready"), sem("vch_read")
        v_ready, probs_ready, probsT_ready = sem("v_ready"), sem("probs_ready"), sem("probsT_ready")
        osq_ready = sem("osq_ready")
        mixed_ready, hid_ready = sem("mixed_ready"), sem("hid_ready")
        tab_full, tab_free = sem("tab_full"), sem("tab_free")

        def linker(eng, own):
            def link(*ins):
                for i in ins:
                    i.then_inc(own, 1)
                eng.wait_ge(own, len(ins)).then_inc(own, -(len(ins)))
            return link

        def say(eng, *sems):
            for s in sems:
                eng.sem_inc(s, 1)

        G_FIRST, G_IN, G_OE, G_OL, G_GU, G_DN = (A["w_first"], KD * P), (A["w_in"], KD * P), \
            (A["w_oe"], KEARLY * P), (A["w_ol"], HEADS * P), \
            (A["w_gu"], KD * P), (A["w_dn"], FHALF * P)

        blk = ctx.enter_context(nc.Block())

        @blk.sync
        def _(sp):
            sp.dma_start(pre[:, :, :], A["pre"]).then_inc(pre_loaded, 16)
            sp.dma_start(par_all[:, :, :], A["par"]).then_inc(par_loaded, 16)
            sp.dma_start(cst[:, :], A["cst"]).then_inc(cst_loaded, 16)
            for i in range(KD):
                sp.dma_start(x[:, i, :], A["x"][:, i, :]).then_inc(x_loaded[i // (KD // 2)], 16)

            def stream(group, l, first, n):
                src, cols = group
                with sp.Fori(0, n // 2) as i:
                    for p in range(2):
                        sp.wait_ge(raw_free, 1).then_inc(raw_free, -1)
                        sp.dma_start(raw[:, p, 0:cols], src[bass.ds(l, 1), bass.ds(i * 2 + (first + p), 1)]
                                     .rearrange("a b p c -> (a b p) c")).then_inc(raw_full[p], 16)

            stream(G_FIRST, 0, 0, 2)
            with sp.Fori(0, L) as l:
                sp.wait_ge(mats_free, 1).then_inc(mats_free, -1)
                for dst, name in ((bmat, "bmat"), (wglu, "wglu")):
                    src = A[name][bass.ds(l, 1)]
                    flat = "p a b c -> p (a b c)" if name != "wglu" else "p a b -> p (a b)"
                    sp.dma_start(dst[:].rearrange(flat), src.rearrange("l p c -> (l p) c")).then_inc(mats_full, 16)
                stream(G_IN, l, 0, NIN - 2)
                stream(G_OE, l, 0, 8)
                stream(G_OL, l, 0, 8)
                for half in range(2):
                    stream(G_GU, l, half * 2 * FHALF, 2 * FHALF)
                    stream(G_DN, l, half * 8, 8)
                stream(G_FIRST, l + 1, 0, 2)
            sp.wait_ge(out_ready, 1).then_inc(out_ready, -1)
            for i in range(KD):
                sp.dma_start(A["out"][:, i, :], x[:, i, :]).then_inc(out_done, 16)
            sp.wait_ge(out_done, 16 * KD)

        @blk.gpsimd
        def _(pool):
            link = linker(pool, pool_own)

            def low(p, cols):
                pool.wait_ge(wh_low, 1).then_inc(wh_low, -1)
                pool.wait_ge(wl_free, 1).then_inc(wl_free, -1)
                link(nc.gpsimd.tensor_tensor(wl[:, p, 0:cols], raw[:, p, 0:cols], wh[:, p, 0:cols].bitcast(F32),
                                             ALU.subtract))
                say(pool, wl_full, raw_free)

            def lows(cols, n):
                with pool.Fori(0, n // 2):
                    for p in range(2):
                        low(p, cols)

            def table(l, j, part):
                if part == 0:
                    pool.wait_ge(tab_free, 1).then_inc(tab_free, -1)
                shape = [P, COARSE, FINE]
                steps_of = [rot[:, bass.ds(l, 1), i, j, :].rearrange("p a b -> p (a b)") for i in range(2)]
                cc, sc = [r[:, FINE:NT].unsqueeze(2).broadcast_to(shape) for r in steps_of]
                cfn, sfn = [r[:, 0:FINE].unsqueeze(1).broadcast_to(shape) for r in steps_of]
                out = tab[j % 2][part]
                out3, t3 = [t[:, :].rearrange("p (a b) -> p a b", a=COARSE) for t in (out, s5t)]
                tt = nc.gpsimd.tensor_tensor
                if part == 0:
                    link(tt(out3, cc, cfn, ALU.mult), tt(t3, sc, sfn, ALU.mult))
                    link(tt(out[:, :], out[:, :], s5t[:, :], ALU.subtract))
                else:
                    link(tt(out3, sc, cfn, ALU.mult), tt(t3, cc, sfn, ALU.mult))
                    link(tt(out[:, :], out[:, :], s5t[:, :], ALU.add))
                    say(pool, tab_full)

            def s5_imaginary(j):
                cs, sn = [t[:, :] for t in tab[j % 2]]
                pool.wait_ge(s5w_ready, 1).then_inc(s5w_ready, -1)
                if j:
                    pool.wait_ge(s5im_read, 1).then_inc(s5im_read, -1)
                link(nc.gpsimd.tensor_tensor(s5im[:, :], sB[:, :], sn, ALU.mult),
                     nc.gpsimd.tensor_tensor(s5t[:, :], sD[:, :], cs, ALU.mult))
                say(pool, s5w_read)
                link(nc.gpsimd.tensor_tensor(s5im[:, :], s5im[:, :], s5t[:, :], ALU.add))
                say(pool, s5im_ready)

            def output_matrix(l):
                tt, cs = nc.gpsimd.tensor_tensor, [P, SJ, SH]
                c_re, c_im = [cmat[:, bass.ds(l, 1), i].rearrange("p a (b c) -> p (a b) c", b=SJ) for i in range(2)]
                f_re, f_im = [factors[:, i, bass.ds(l, 1)].rearrange("p a b -> p (a b)").unsqueeze(2).broadcast_to(cs)
                              for i in range(2)]
                t = [G[:, 2 + i // 2, (i % 2) * SJ * SH:(i % 2 + 1) * SJ * SH].rearrange("p (a b) -> p a b", a=SJ)
                     for i in range(4)]
                link(tt(t[0], c_re, f_re, ALU.mult), tt(t[1], c_im, f_im, ALU.mult),
                     tt(t[2], c_re, f_im, ALU.mult), tt(t[3], c_im, f_re, ALU.mult))
                link(tt(cf[:, 0], t[0], t[1], ALU.add), tt(cf[:, 1], t[2], t[3], ALU.subtract))
                say(pool, cf_ready)

            say(pool, raw_free, raw_free, wl_free)
            low(0, KD * P)
            with pool.Fori(0, L) as l:
                for s in range(NIN - 1):
                    low((s + 1) % 2, KD * P)
                    if s == 3:
                        output_matrix(l)
                    if s in TABLE_AT:
                        table(l, TABLE_AT.index(s), 0)
                        table(l, TABLE_AT.index(s), 1)
                    if s == 11 or s == 15 or s >= 17 and s % 2:
                        s5_imaginary(0 if s == 11 else (s - 13) // 2)
                s5_imaginary(SJ - 1)
                lows(KEARLY * P, 8)
                lows(HEADS * P, 8)
                for _ in range(2):
                    lows(KD * P, 2 * FHALF)
                    lows(FHALF * P, 8)
                low(0, KD * P)

        @blk.tensor
        def _(pe):
            mm = nc.tensor.matmul

            def unit(p, K, hi, lo, ready=None):
                pe.wait_ge(wh_full, 1).then_inc(wh_full, -1)
                pe.wait_ge(bank_free[p], 1).then_inc(bank_free[p], -1)
                parts = [range(K)] if ready is None else [range(K - 1), [K - 1]]
                for part, ks in enumerate(parts):
                    for k in ks:
                        if ready is not None:
                            pe.wait_ge(ready, 1).then_inc(ready, -1)
                        w = mm(bank[p][:, :], wh[:, p, k * P:(k + 1) * P], lo[:, k, :], start=(k == 0), stop=False)
                        if k == 0:
                            w.then_inc(wl_free, 1)
                    for k in ks:
                        w = mm(bank[p][:, :], wh[:, p, k * P:(k + 1) * P], hi[:, k, :], start=False, stop=False)
                    if ks[-1] == K - 1:
                        w.then_inc(wh_free, 1)
                    if part == 0:
                        pe.wait_ge(wl_full, 1).then_inc(wl_full, -1)
                    for k in ks:
                        w = mm(bank[p][:, :], wl[:, p, k * P:(k + 1) * P], hi[:, k, :], start=False, stop=(k == K - 1))
                w.then_inc(dve_bank[p], 1)

            def units(n, K, hi, lo, ready=None):
                if ready is not None:
                    unit(0, K, hi, lo, ready)
                    unit(1, K, hi, lo)
                    n -= 2
                with pe.Fori(0, n // 2):
                    unit(0, K, hi, lo)
                    unit(1, K, hi, lo)

            def rms_sum():
                pe.wait_ge(ssum_ready, 1).then_inc(ssum_ready, -1)
                pe.wait_ge(bank_free[7], 1).then_inc(bank_free[7], -1)
                mm(bank[7][:, :], ones, ssum[:, :], start=True, stop=True).then_inc(act_bank[7], 1)

            def dt_rows():
                pe.wait_ge(wdt_ready, 1).then_inc(wdt_ready, -1)
                pe.wait_ge(bank_free[5], 1).then_inc(bank_free[5], -1)
                for n, (a, b) in enumerate(((wdth, xl), (wdth, xh), (wdtl, xh))):
                    for k in range(KD):
                        w = mm(bank[5][0:M2H, :], a[:, k, :], b[:, k, :], start=(n == k == 0),
                               stop=(n == 2 and k == KD - 1))
                w.then_inc(dve_bank[5], 1)

            def dt_turn():
                pe.wait_ge(dt_ready, 1).then_inc(dt_ready, -1)
                pe.wait_ge(bank_free[5], 1).then_inc(bank_free[5], -1)
                for t in range(NQ):
                    w = nc.tensor.transpose(bank[5][:, t * M2H:(t + 1) * M2H], G[0:M2H, 5, t * P:(t + 1) * P],
                                            ident[0:M2H, 0:M2H])
                w.then_inc(dve_bank[5], 1)

            def s5_in(j):
                if j == 0:
                    pe.wait_ge(u_ready, 1).then_inc(u_ready, -1)
                    pe.wait_ge(cf_ready, 1).then_inc(cf_ready, -1)
                r = SH * (j % 4)
                for c in range(2):
                    pe.wait_ge(bank_free[2 + c], 1).then_inc(bank_free[2 + c], -1)
                    mm(bank[2 + c][:, :], bmat[r:r + SH, c, j // 4, :],
                       u[r:r + SH, j // 4, :], start=True, stop=True).then_inc(dve_bank[2 + c], 1)

            def s5_out(j):
                r = SH * (j % 4)
                if j % 4 == 0:
                    pe.wait_ge(bank_free[6], 1).then_inc(bank_free[6], -1)
                pe.wait_ge(s5x_ready, 1).then_inc(s5x_ready, -1)
                w = mm(bank[6][r:r + SH, :], cf[:, 0, j, :], sE[:, :], start=True, stop=False)
                if j % 4 < 3:
                    w.then_inc(s5x_read, 1)
                pe.wait_ge(s5im_ready, 1).then_inc(s5im_ready, -1)
                w = mm(bank[6][r:r + SH, :], cf[:, 1, j, :], s5im[:, :], start=False, stop=True)
                w.then_inc(s5im_read if j % 4 < 3 else s5x_read, 1)

            def s5_glu():
                pe.wait_ge(glu_in, 1).then_inc(glu_in, -1)
                for i in range(2):
                    pe.wait_ge(bank_free[i], 1).then_inc(bank_free[i], -1)
                    for k in range(2):
                        w = mm(bank[i][:, :], wglu[:, k, i * P:(i + 1) * P], u[:, k, :], start=(k == 0), stop=(k == 1))
                    w.then_inc(act_bank[i], 1)

            def m2_sums():
                pe.wait_ge(adt_ready, 1).then_inc(adt_ready, -1)
                pe.wait_ge(bank_free[7], 1).then_inc(bank_free[7], -1)
                mm(bank[7][:, 0:16], tri, adt, start=True, stop=True)
                mm(bank[7][:, 16:32], ones, adt, start=True, stop=True).then_inc(dve_bank[7], 1)

            def m2_turn(t):
                b = (4, 7)[t % 2]
                pe.wait_ge(bank_free[b], 1).then_inc(bank_free[b], -1)
                for i in range(4 if t < NQ - 1 else 2):
                    w = nc.tensor.transpose(bank[b][:, i * P:(i + 1) * P], xbc[:, i, t * P:(t + 1) * P], ident)
                w.then_inc(dve_bank[b], 1)

            def m2_states(t):
                pe.wait_ge(xbt_ready, 1).then_inc(xbt_ready, -1)
                if t % 2 == 0:
                    pe.wait_ge(bank_free[5], 1).then_inc(bank_free[5], -1)
                for g in range(2):
                    c = (2 * (t % 2) + g) * P
                    w = mm(bank[5][:, c:c + P], xbt[:, t, 2 + g, :],
                           xds[:, t, 2 * g:2 * g + 2, :].rearrange("p h c -> p (h c)"), start=True, stop=True)
                if t:
                    w.then_inc(dve_bank[5], 1)

            def m2_scores(g):
                pe.wait_ge(bank_free[7], 1).then_inc(bank_free[7], -1)
                for t in range(NQ):
                    c = slice(t * P, (t + 1) * P)
                    w = mm(bank[7][:, c], xbc[:, 2 + g, c], xbc[:, 4 + g, c], start=True, stop=True)
                w.then_inc(dve_bank[7], 1)

            def m2_decays(h):
                pe.wait_ge(bank_free[4], 1).then_inc(bank_free[4], -1)
                for t in range(NQ):
                    c = slice(t * P, (t + 1) * P)
                    w = mm(bank[4][:, c], adt[:, t * M2H + h:t * M2H + h + 1].broadcast_to([P, P]), tri,
                           start=True, stop=True)
                w.then_inc(dve_bank[4], 1)

            def m2_apply(h):
                pe.wait_ge(mix_ready, 1).then_inc(mix_ready, -1)
                if h == 0:
                    pe.wait_ge(hst_ready, 1).then_inc(hst_ready, -1)
                if h % 2 == 0:
                    pe.wait_ge(bank_free[5], 1).then_inc(bank_free[5], -1)
                r = slice(M2P * (h % 2), M2P * (h % 2) + M2P)
                for t in range(NQ):
                    c = slice(t * P, (t + 1) * P)
                    decayed, decayed_c = m2buf[h % 2]
                    w = mm(bank[5][r, c], xbt[:, t, h // 2, r], decayed[:, c], start=True, stop=(t == 0))
                    if t > 0:
                        w = mm(bank[5][r, c], hst[:, t - 1, h, :], decayed_c[:, c], start=False, stop=True)
                w.then_inc(mix_read, 1)

            def m2_norm():
                pe.wait_ge(bank_free[7], 1).then_inc(bank_free[7], -1)
                for i in range(2):
                    pe.wait_ge(m2sq_ready, 1).then_inc(m2sq_ready, -1)
                    w = mm(bank[7][:, :], ones, xbc[:, 2 + i, :], start=(i == 0), stop=(i == 1))
                w.then_inc(act_bank[7], 1)

            def qk_mean(t):
                pe.wait_ge(sqk_ready, 1).then_inc(sqk_ready, -1)
                pe.wait_ge(bank_free[4], 1).then_inc(bank_free[4], -1)
                mm(bank[4][:, :], block1, G[:, 2, :], start=True, stop=True).then_inc(act_bank[4], 1)
                pe.wait_ge(bank_free[5], 1).then_inc(bank_free[5], -1)
                mm(bank[5][:, :], permg[:, t % 2, :], G[:, t % 2, :], start=True, stop=True).then_inc(dve_bank[5], 1)

            def v_turn(h):
                pe.wait_ge(vch_ready, 1).then_inc(vch_ready, -1)
                pe.wait_ge(bank_free[4], 1).then_inc(bank_free[4], -1)
                for t in range(NQ):
                    w = nc.tensor.transpose(bank[4][:, t * P:(t + 1) * P], G[:, h % 2, t * P:(t + 1) * P], ident)
                w.then_inc(act_bank[4], 1)

            def scores(n):
                h, q = n // NQ, n % NQ
                for c in range(2):
                    b = (2, 3, 6, 7)[2 * (n % 2) + c]
                    pe.wait_ge(bank_free[b], 1).then_inc(bank_free[b], -1)
                    r = slice(QK * c, QK * c + QK)
                    qs, last = qk[r, 2 * h, q * P:(q + 1) * P], slice(q * P, (q + 1) * P)
                    if q:
                        mm(bank[b][:, 0:q * P], qs, qk[r, 2 * h + 1, 0:q * P], start=True, stop=True)
                    mm(bank[b][:, last], qs, qk[r, 2 * h + 1, last], start=True, stop=False)
                    mm(bank[b][:, last], cbf[:, 0, :], cbf[:, 1, :], start=False, stop=True).then_inc(dve_bank[b], 1)

            def turn(n):
                pe.wait_ge(probs_ready, 1).then_inc(probs_ready, -1)
                pe.wait_ge(bank_free[4], 1).then_inc(bank_free[4], -1)
                for k in range(n % NQ + 1):
                    w = nc.tensor.transpose(bank[4][:, k * P:(k + 1) * P], G[:, 2 * (n % 2), k * P:(k + 1) * P], ident)
                w.then_inc(act_bank[4], 1)

            def attend(n):
                h, q = n // NQ, n % NQ
                if q == 0:
                    pe.wait_ge(bank_free[5], 1).then_inc(bank_free[5], -1)
                pe.wait_ge(probsT_ready, 1).then_inc(probsT_ready, -1)
                for k in range(q + 1):
                    w = mm(bank[5][:, q * P:(q + 1) * P], v[:, k, h * P:(h + 1) * P],
                           G[:, 4 + n % 2, k * P:(k + 1) * P], start=(k == 0), stop=(k == q))
                if q == NQ - 1:
                    w.then_inc(dve_bank[5], 1)

            def head_sum(b):
                pe.wait_ge(osq_ready, 1).then_inc(osq_ready, -1)
                pe.wait_ge(bank_free[b], 1).then_inc(bank_free[b], -1)
                mm(bank[b][:, :], ones, pad[:, 0, 4:4 + T], start=True, stop=True).then_inc(act_bank[b], 1)

            pe.wait_ge(pe_go, 1).then_inc(pe_go, -1)
            with pe.Fori(0, L):
                unit(0, KD, xh, xl, xk_ready)
                rms_sum()
                unit(1, KD, xh, xl)
                dt_rows()
                for s in range(2, NIN):
                    unit(s % 2, KD, xh, xl)
                    if s == 2:
                        dt_turn()
                    if s == 6:
                        m2_sums()
                    if s == 7:
                        for _ in range(4):
                            pe.wait_ge(xbc_ready, 1).then_inc(xbc_ready, -1)
                        m2_turn(0)
                        m2_turn(1)
                    if s == 8:
                        m2_turn(2)
                        m2_turn(3)
                    if s == 9:
                        m2_decays(0)
                        for _ in range(2):
                            pe.wait_ge(xbc_ready, 1).then_inc(xbc_ready, -1)
                        m2_states(0)
                        m2_states(1)
                        m2_scores(0)
                    if s == 10:
                        m2_states(2)
                        pe.wait_ge(xbt_ready, 1).then_inc(xbt_ready, -1)
                        m2_decays(1)
                        s5_in(0)
                    if s == 11:
                        m2_apply(0)
                    if s == 12:
                        m2_apply(1)
                        s5_out(0)
                        m2_decays(2)
                        m2_scores(1)
                    if s == 13:
                        m2_apply(2)
                        m2_decays(3)
                    if s == 14:
                        m2_apply(3)
                        s5_in(1)
                    if s == 16:
                        m2_norm()
                    if 17 <= s <= 24:
                        qk_mean(s - 17)
                    if s >= 25:
                        v_turn(s - 25)
                    if s >= 16 and s % 2 == 0:
                        s5_in((s - 12) // 2)
                    if s >= 17 and s % 2:
                        s5_out((s - 15) // 2)
                pe.wait_ge(qk_ready, 1).then_inc(qk_ready, -1)
                scores(0)
                v_turn(3)
                s5_out(SJ - 1)
                scores(1)
                for n in range(STEPS):
                    if n + 2 < STEPS:
                        scores(n + 2)
                    if n == BESIDE[-1]:
                        unit(1, KEARLY, mh[:, MIXB:MIXED, :], ml[:, MIXB:MIXED, :])
                    turn(n)
                    if n == 0:
                        s5_glu()
                    if n == 3:
                        for _ in range(KEARLY):
                            pe.wait_ge(mixed_ready, 1).then_inc(mixed_ready, -1)
                    if n in BESIDE[:-1]:
                        unit(BESIDE.index(n) % 2, KEARLY, mh[:, MIXB:MIXED, :], ml[:, MIXB:MIXED, :])
                    if n == 1:
                        for _ in range(HEADS):
                            pe.wait_ge(v_ready, 1).then_inc(v_ready, -1)
                    if n:
                        attend(n - 1)
                    if n > NQ and n % NQ == 2:
                        head_sum(HEAD_BANK[n // NQ - 1])
                attend(STEPS - 1)
                unit(0, KEARLY, mh[:, MIXB:MIXED, :], ml[:, MIXB:MIXED, :])
                head_sum(HEAD_BANK[HEADS - 1])
                unit(1, KEARLY, mh[:, MIXB:MIXED, :], ml[:, MIXB:MIXED, :])
                units(8, HEADS, mh, ml, mixed_ready)
                unit(0, KD, xh, xl, xk_ready)
                rms_sum()
                unit(1, KD, xh, xl)
                units(2 * FHALF - 2, KD, xh, xl)
                units(8, FHALF, mh, ml, hid_ready)
                units(2 * FHALF, KD, xh, xl)
                units(8, FHALF, mh, ml, hid_ready)

        @blk.scalar
        def _(act):
            link = linker(act, act_own)
            fn = nc.scalar.activation

            def prep(p, cols):
                act.wait_ge(raw_full[p], 16).then_inc(raw_full[p], -16)
                act.wait_ge(wh_free, 1).then_inc(wh_free, -1)
                link(fn(wh[:, p, 0:cols], raw[:, p, 0:cols], ACT.Copy))
                say(act, wh_full, wh_low)

            def preps(n, cols):
                with act.Fori(0, n // 2):
                    prep(0, cols)
                    prep(1, cols)

            def norm_tile(k, p, gain):
                xk, hk = [t[:, bass.ds(k, 1), :].rearrange("p a b -> p (a b)") for t in (x, xh)]
                g0 = PARAMS[gain][0]
                act.wait_ge(x_ready, 1).then_inc(x_ready, -1)
                fn(hk, xk, ACT.Copy, scale=par[:, bass.ds(k + g0, 1)]).then_inc(xh_full, 1)
                act.wait_ge(sq_free, 1).then_inc(sq_free, -1)
                fn(G[:, p, :], xk, ACT.Square).then_inc(sq_full, 1)

            def norm_beside(cols, next_cols, gain):
                with act.Fori(0, KD // 2 - 1) as i:
                    for p in range(2):
                        norm_tile(i * 2 + p, p, gain)
                        prep(p, cols)
                for p in range(2):
                    norm_tile(KD - 2 + p, p, gain)
                    prep(p, next_cols)

            def rsqrt_mean(out, in_, n):
                link(fn(out, in_, ACT.Ln, scale=1.0 / n, bias=eps))
                link(fn(out, out, ACT.Exp, scale=-0.5))

            def rms():
                act.wait_ge(act_bank[7], 1).then_inc(act_bank[7], -1)
                rsqrt_mean(rbc[:, :], bank[7][:, :], D)
                say(act, bank_free[7], rms_ready)

            def high(dst, src):
                link(fn(dst, src, ACT.Copy))

            def emit(tile, buf):
                act.wait_ge(em_full, 1).then_inc(em_full, -1)
                high(mh[:, tile, :], buf)
                say(act, em_high)

            say(act, wh_free, wh_free)
            act.wait_ge(ask_act, 1).then_inc(ask_act, -1)
            link(fn(s8[:, 0], s8[:, 0], ACT.Exp), fn(lam2[:, :, :], lam2[:, :, :], ACT.Exp))
            say(act, act_says)
            nc.scalar.dma_start(rotary[:, :, :], A["rotary"]).then_inc(late_loaded, 16)
            nc.scalar.dma_start(cmat[:, :, :, :], A["cmat"]).then_inc(late_loaded, 16)
            act.wait_ge(act_go, 1).then_inc(act_go, -1)
            norm_tile(0, 0, "g1")
            prep(0, KD * P)
            norm_tile(1, 1, "g1")
            prep(1, KD * P)
            with act.Fori(1, KD // 2) as i:
                norm_tile(i * 2, 0, "g1")
                norm_tile(i * 2 + 1, 1, "g1")
            act.wait_ge(ask_act, 1).then_inc(ask_act, -1)
            link(*[fn(rot[:, l, 1].rearrange("p a b -> p (a b)"),
                      ph0[:, l * SJ:(l + 1) * SJ, :].rearrange("p a b -> p (a b)"), ACT.Sin) for l in range(L)],
                 fn(kk0[:].rearrange("p a b -> p (a b)"), ph0[:].rearrange("p a b -> p (a b)"), ACT.Sin, scale=0.5))
            say(act, act_says)
            with act.Fori(0, L):
                link(fn(s16[:, 8, 0:M2H], col("alog", 0, M2H), ACT.Exp))
                prep(0, KD * P)
                rms()


                def m2_head(h):
                    act.wait_ge(ask_act, 1).then_inc(ask_act, -1)
                    link(fn(m2buf[h % 2][0], m2buf[h % 2][0], ACT.Exp), fn(m2buf[h % 2][1], bank[4][:, :], ACT.Exp))
                    say(act, bank_free[4], act_says)

                def m2_square(i):
                    act.wait_ge(ask_act, 1).then_inc(ask_act, -1)
                    link(fn(xbc[:, 2 + i, :], xbc[:, i, :], ACT.Square))
                    say(act, m2sq_ready)

                def qk_square(t):
                    act.wait_ge(ask_act, 1).then_inc(ask_act, -1)
                    link(fn(G[:, 2, :], G[:, t % 2, :], ACT.Square))
                    say(act, sqk_ready)

                def gelu(i):
                    act.wait_ge(ask_act, 1).then_inc(ask_act, -1)
                    link(fn(u[:, i, :], u[:, i, :], ACT.Gelu_apprx_tanh))
                    say(act, act_says)

                def v_copy(h):
                    act.wait_ge(act_bank[4], 1).then_inc(act_bank[4], -1)
                    link(fn(v[:, :, h * P:(h + 1) * P], bank[4][:, :].rearrange("p (t c) -> p t c", t=NQ), ACT.Copy))
                    say(act, bank_free[4], v_ready, vch_read)

                for s in range(1, NIN):
                    prep(s % 2, (KD if s < NIN - 2 else KEARLY) * P)
                    if s == 2:
                        act.wait_ge(ask_act, 1).then_inc(ask_act, -1)
                        link(fn(s16[:, 1, :], s16[:, 1, :], ACT.Exp, scale=-1.0))
                        say(act, act_says)
                    if 2 <= s <= 7:
                        act.wait_ge(ask_act, 1).then_inc(ask_act, -1)
                        link(fn(xbc[:, s - 2, :], G[:, s % 2, :], ACT.Silu))
                        say(act, act_says, xbc_ready)
                    if s == 6:
                        act.wait_ge(ask_act, 1).then_inc(ask_act, -1)
                        link(fn(s16[:, 6, :], s16[:, 6, :], ACT.Exp), fn(s16[:, 7, :], s16[:, 5, :], ACT.Exp))
                        say(act, act_says)
                    if 8 <= s <= 9:
                        act.wait_ge(ask_act, 1).then_inc(ask_act, -1)
                        link(fn(z[:, s - 8, :], z[:, s - 8, :], ACT.Silu))
                        say(act, act_says)
                    if s == 9:
                        m2_head(0)
                    if 11 <= s <= 13:
                        m2_head(s - 10)
                    if s == 12:
                        m2_square(0)
                    if s == 14:
                        emit(MIXB, G[:, 4, :])
                        m2_square(1)
                    if s == 15:
                        emit(MIXB + 1, G[:, 5, :])
                    if s == 16:
                        act.wait_ge(act_bank[7], 1).then_inc(act_bank[7], -1)
                        rsqrt_mean(z[:, 0, :], bank[7][:, :], 2 * P)
                        say(act, bank_free[7], act_says)
                    if s == 17:
                        for i in range(2):
                            emit(MIXD + i, xbc[:, 4 + i, :])
                    if 17 <= s <= 24:
                        act.wait_ge(act_bank[4], 1).then_inc(act_bank[4], -1)
                        rsqrt_mean(G[:, 3 + (s - 17) % 2, :], bank[4][:, :], QK)
                        say(act, bank_free[4], act_says)
                    if 16 <= s <= 23:
                        qk_square(s - 16)
                    if s >= 25:
                        v_copy(s - 25)
                    if s == 21:
                        gelu(0)

                def exps(n):
                    w, s = (n % NQ + 1) * P, n % 2
                    both = []
                    for c in range(2):
                        act.wait_ge(exp_go, 1).then_inc(exp_go, -1)
                        both.append(fn(G[:, 2 * s + c, 0:w], bank[(2, 3, 6, 7)[2 * s + c]][:, 0:w], ACT.Exp,
                                       bias=soft[:, s, c:c + 1], accum_out=soft[:, s, 2 + c:3 + c]))
                    link(*both)
                    say(act, bank_free[(2, 6)[s]], bank_free[(3, 7)[s]], exp_done)

                def head_square():
                    act.wait_ge(osq_go, 1).then_inc(osq_go, -1)
                    link(fn(pad[:, 0, 4:4 + T], ssum[:, :], ACT.Square))
                    say(act, osq_ready)

                def head_log(b):
                    act.wait_ge(act_bank[b], 1).then_inc(act_bank[b], -1)
                    link(fn(rbc[:, :], bank[b][:, :], ACT.Ln, scale=1.0 / P, bias=eps))
                    say(act, bank_free[b])

                def head_rms():
                    link(fn(rbc[:, :], rbc[:, :], ACT.Exp, scale=-0.5))
                    say(act, onorm_done)

                v_copy(3)
                exps(0)
                gelu(1)
                for n in range(STEPS):
                    if n + 1 < STEPS:
                        exps(n + 1)
                    if n > NQ and n % NQ == 3:
                        head_rms()
                    act.wait_ge(act_bank[4], 1).then_inc(act_bank[4], -1)
                    w = (n % NQ + 1) * P
                    link(fn(G[:, 4 + n % 2, 0:w], bank[4][:, 0:w], ACT.Copy))
                    say(act, bank_free[4], probsT_ready)
                    if n == 0:
                        for i, gate in enumerate((sA, sB)):
                            act.wait_ge(act_bank[i], 1).then_inc(act_bank[i], -1)
                            link(fn(gate[:, :], bank[i][:, :], ACT.Sigmoid, bias=col("bglu", i)))
                            say(act, bank_free[i], act_says)
                    if n == 1:
                        for i, gated in enumerate((sC, sD)):
                            emit(MIXC + i, gated[:, :])
                    if n > NQ and n % NQ == 1:
                        head_square()
                    if n - 1 in BESIDE:
                        prep(BESIDE.index(n - 1) % 2, KEARLY * P)
                    if n > NQ and n % NQ == 2:
                        head_log(HEAD_BANK[n // NQ - 1])
                    if n > NQ and n % NQ == 3:
                        emit(MIXA + n // NQ - 1, ssum[:, :])
                prep(1, KEARLY * P)
                head_square()
                prep(0, HEADS * P)
                head_log(HEAD_BANK[HEADS - 1])
                head_rms()
                emit(MIXA + HEADS - 1, ssum[:, :])
                prep(1, HEADS * P)
                norm_beside(HEADS * P, KD * P, "g2")
                prep(0, KD * P)
                rms()

                def ffn_tile(i, cols, first):
                    if not first:
                        prep(0, cols)
                    act.wait_ge(ask_act, 1).then_inc(ask_act, -1)
                    link(fn(G[:, 1, :], G[:, 0, :], ACT.Silu))
                    say(act, act_says)
                    prep(1, cols)
                    act.wait_ge(ask_act, 1).then_inc(ask_act, -1)
                    high(mh[:, bass.ds(i, 1), :].rearrange("p a b -> p (a b)"), G[:, 3, :])
                    say(act, act_says)

                for half in range(2):
                    ffn_tile(0, KD * P, half == 0)
                    with act.Fori(1, FHALF - 1) as i:
                        ffn_tile(i, KD * P, False)
                    ffn_tile(FHALF - 1, FHALF * P, False)
                    if half == 0:
                        preps(6, FHALF * P)
                        preps(2, KD * P)
                norm_beside(FHALF * P, KD * P, "g1")

        @blk.vector
        def _(dve):
            link = linker(dve, dve_own)
            tt, ts, stt = nc.vector.tensor_tensor, nc.vector.tensor_scalar, nc.vector.scalar_tensor_tensor
            copy = nc.vector.tensor_copy
            MUL, ADD, SUB = ALU.mult, ALU.add, ALU.subtract

            def flat(ap):
                return ap.rearrange("p a b -> p (a b)")

            def norm_tile(k, p, gain):
                xk, hk, lk = [flat(t[:, bass.ds(k, 1), :]) for t in (x, xh, xl)]
                g0 = PARAMS[gain][0]
                dve.wait_ge(xh_full, 1).then_inc(xh_full, -1)
                stt(lk, xk, par[:, bass.ds(k + g0, 1)], hk.bitcast(F32), MUL, SUB).then_inc(xk_ready, 1)
                dve.wait_ge(sq_full, 1).then_inc(sq_full, -1)
                link(tt(ssum[:, :], ssum[:, :], G[:, p, :], ADD))
                say(dve, sq_free)

            def scaled(out, p):
                dve.wait_ge(dve_bank[p], 1).then_inc(dve_bank[p], -1)
                link(tt(out, bank[p][:, :], rbc[:, :], MUL))
                say(dve, bank_free[p])

            def taps(out, p, weights, first, bias=None):
                n = len(weights)
                if bias is None:
                    link(ts(out, pad[:, p, 4:4 + T], weights[n - 1], None, MUL))
                else:
                    link(ts(out, pad[:, p, 4:4 + T], weights[n - 1], bias, MUL, ADD))
                for k in range(1, n):
                    link(stt(out, pad[:, p, 4 - k:4 - k + T], weights[n - 1 - k], out, MUL, ADD))

            def emit_low(tile, buf):
                dve.wait_ge(em_high, 1).then_inc(em_high, -1)
                tt(ml[:, tile, :], buf, mh[:, tile, :].bitcast(F32), SUB).then_inc(mixed_ready, 1)

            def emit(tile, buf):
                say(dve, em_full)
                emit_low(tile, buf)

            def residual(o, p):
                dve.wait_ge(dve_bank[p], 1).then_inc(dve_bank[p], -1)
                xo = flat(x[:, bass.ds(o, 1), :])
                link(tt(xo, xo, bank[p][:, :], ADD))
                say(dve, bank_free[p])

            def residuals():
                with dve.Fori(0, KD // 2) as o:
                    residual(o * 2, 0)
                    residual(o * 2 + 1, 1)

            def finish_x(gain):
                link(nc.vector.memset(ssum[:, :], 0.0))
                residual(0, 0)
                say(dve, x_ready)
                with dve.Fori(0, KD // 2 - 1) as i:
                    for p in range(2):
                        residual(i * 2 + (p + 1), 1 - p)
                        say(dve, x_ready)
                        norm_tile(i * 2 + p, p, gain)
                residual(KD - 1, 1)
                say(dve, x_ready)
                norm_tile(KD - 2, 0, gain)
                norm_tile(KD - 1, 1, gain)
                say(dve, ssum_ready)

            def layer_values(l):
                link(copy(rho[:, :], flat(rho_all[:, bass.ds(l, 1), :])), copy(mlam[:, :], mlam_all[:, bass.ds(l, 1)]))

            def parameters(l):
                link(copy(par[:, :], flat(par_all[:, bass.ds(l, 1), :])))
                w = par[:, PARAMS["wdt"][0]:PARAMS["wdt"][0] + KD * M2H]
                link(copy(flat(wdth[:]), w),
                     ts(col("qkg"), col("qkg"), QK ** -0.5, None, MUL),
                     ts(col("subg"), col("subg"), col("oneml"), None, MUL))
                link(tt(flat(wdtl[:]), w, flat(wdth[:]).bitcast(F32), SUB),
                     *[ts(permg[:, i, :], perm, col("qkg", i), None, MUL) for i in range(2)])
                say(dve, wdt_ready)

            def dt_scaled():
                dve.wait_ge(dve_bank[5], 1).then_inc(dve_bank[5], -1)
                link(tt(G[0:M2H, 5, :], bank[5][0:M2H, :], rbc[0:M2H, :], MUL))
                say(dve, bank_free[5], dt_ready)

            def m2_dt():
                a, e, s, sq, q, rec = [s16[:, i, :] for i in (0, 1, 2, 9, 10, 11)]
                by_head = [P, NQ, M2H]
                dve.wait_ge(dve_bank[5], 1).then_inc(dve_bank[5], -1)
                link(tt(a.rearrange("p (a b) -> p a b", a=NQ), bank[5][:, 0:16].rearrange("p (a b) -> p a b", a=NQ),
                        col("dtb", 0, M2H).unsqueeze(1).broadcast_to(by_head), ADD))
                say(dve, bank_free[5])
                link(stt(e, a, -1.0, a, MUL, ALU.max))
                say(dve, ask_act)
                link(ts(a, a, 0.0, None, ALU.max))

            def m2_log():
                e, s, sq, rec = [s16[:, i, :] for i in (1, 2, 9, 11)]
                dve.wait_ge(act_says, 1).then_inc(act_says, -1)
                link(ts(rec, e, 2.0, None, ADD))
                link(nc.vector.reciprocal(rec, rec))
                link(tt(s, e, rec, MUL))
                link(tt(sq, s, s, MUL))

            def m2_series():
                sq, q = [s16[:, i, :] for i in (9, 10)]
                link(ts(q, sq, 1.0 / 17, None, MUL))
                for c in (15, 13, 11, 9, 7, 5, 3):
                    link(stt(q, q, 1.0 / c, sq, ADD, MUL))

            def m2_steps():
                a, s, q = [s16[:, i, :] for i in (0, 2, 10)]
                by_head = [P, NQ, M2H]
                link(stt(q, q, 1.0, s, ADD, MUL))
                link(stt(a, q, 2.0, a, MUL, ADD))
                link(stt(adt.rearrange("p (a b) -> p a b", a=NQ), a.rearrange("p (a b) -> p a b", a=NQ), -1.0,
                         s16[:, 8, 0:M2H].unsqueeze(1).broadcast_to(by_head), MUL, MUL))
                say(dve, adt_ready)

            def reduced(ph, extra, k):
                if extra is not None:
                    link(tt(k, ph, extra, ADD))
                link(ts(k, ph if extra is None else k, INV2PI, ROUND, MUL, ADD))
                link(ts(k, k, ROUND, None, SUB))
                for c in (C1, C2, C3):
                    link(stt(ph, k, -c, ph, MUL, ADD))
                if extra is not None:
                    link(tt(ph, ph, extra, ADD))

            dt, r, F, _, th, thl, nre, nim, m2, inv, a, b, c, d, k = [s8[:, i] for i in range(15)]
            lre, lim = pre[:, :, PRE["lre"]], pre[:, :, PRE["lim"]]
            ph, kk, lo = [flat(t[:]) for t in (ph0, kk0, lo0)]

            def s5_angles():
                link(copy(dt, pre[:, :, PRE["ldt"]]))
                for l in range(L):
                    dal = pre[:, l, PRE["dal"]].rearrange("p (a b c) -> p a b c", a=2, b=2)
                    link(tt(lprod[:, :, :], dal[:, :, 0, :], dal[:, :, 1, :], MUL))
                    link(nc.vector.tensor_reduce(lam2[:, l, :], lprod[:, :, :], AX, ADD))
                say(dve, ask_act)
                link(tt(m2, lre, lre, MUL), tt(a, lim, lim, MUL))
                link(tt(m2, m2, a, ADD))
                link(nc.vector.reciprocal(inv, m2))
                dve.wait_ge(act_says, 1).then_inc(act_says, -1)
                link(tt(th, lim, dt, MUL), tt(r, lre, dt, MUL), tt(mlam_all[:, :], lam2[:, :, 1], lam2[:, :, 0], SUB))
                link(tt(mlam_all[:, :], mlam_all[:, :], pre[:, :, PRE["linit"]].rearrange("p a b -> p (a b)"), SUB))
                reduced(th, None, k)

            def s5_phases():
                th_flat = th.rearrange("p a b -> p (a b)")
                thl_flat = thl.rearrange("p a b -> p (a b)")
                link(copy(thh[:, :], th_flat))
                link(tt(thl_flat, th_flat, thh[:, :].bitcast(F32), SUB))
                shape = [P, L * SJ, NT]
                st3 = pre[:, 0, PRE["steps"]].unsqueeze(1).broadcast_to(shape)
                link(tt(ph0[:, :, :], thh[:, :].bitcast(F32).unsqueeze(2).broadcast_to(shape), st3, MUL),
                     tt(lo0[:, :, :], thl_flat.unsqueeze(2).broadcast_to(shape), st3, MUL))
                reduced(ph, lo, kk)
                link(ts(ph, ph, PI_CAP, -PI_CAP, ALU.min, ALU.max))
                say(dve, ask_act)

            def s5_decay(part):
                if part == 0:
                    link(ts(r, r, -100.0, 1.0 / 1024, ALU.max, MUL))
                    link(ts(F, r, 1.0 / 5, 1.0, MUL, ADD))
                    for n in (4, 3, 2):
                        link(tt(F, F, r, MUL))
                        link(ts(F, F, 1.0 / n, 1.0, MUL, ADD))
                    link(tt(F, F, r, MUL))
                elif part <= 5:
                    for _ in range(2):
                        link(stt(F, F, 2.0, F, ADD, MUL))

            def s5_values():
                link(ts(rho_all[:, :, :], F, 1.0, None, ADD))
                link(tt(lo, kk, kk, MUL))
                lo4 = lo0[:].rearrange("p (l j) n -> p l j n", l=L)
                link(*[ts(rot[:, l, 0], lo4[:, l], -2.0, 1.0, MUL, ADD) for l in range(L)])
                link(tt(nre, F, rot[:, :, 0, :, 1], MUL), stt(nim, F, 1.0, rot[:, :, 1, :, 1], ADD, MUL))
                link(stt(nre, lo4[:, :, :, 1], -2.0, nre, MUL, ADD))
                link(tt(a, nre, lre, MUL), tt(b, nim, lim, MUL), tt(c, nim, lre, MUL), tt(d, nre, lim, MUL))
                link(tt(a, a, b, ADD), tt(c, d, c, SUB))
                link(tt(factors[:, 0], a, inv, MUL), tt(factors[:, 1], c, inv, MUL))
                dve.wait_ge(late_loaded, 32).then_inc(late_loaded, -32)

            a5, b5, c5, d5, e5 = [t[:, :] for t in (sA, sB, sC, sD, sE)]

            def s5_scan(j):
                cs, sn = [t[:, :] for t in tab[j % 2]]
                dve.wait_ge(tab_full, 1).then_inc(tab_full, -1)
                dve.wait_ge(dve_bank[2], 1).then_inc(dve_bank[2], -1)
                dve.wait_ge(dve_bank[3], 1).then_inc(dve_bank[3], -1)
                if j:
                    dve.wait_ge(s5w_read, 1).then_inc(s5w_read, -1)
                link(tt(a5, bank[2][:, :], cs, MUL), tt(b5, bank[3][:, :], sn, MUL),
                     tt(c5, bank[3][:, :], cs, MUL), tt(d5, bank[2][:, :], sn, MUL))
                say(dve, bank_free[2], bank_free[3])
                link(tt(a5, a5, b5, ADD), tt(c5, c5, d5, SUB))
                decay = rho[:, j:j + 1].broadcast_to([P, T])
                link(nc.vector.tensor_tensor_scan(b5, decay, a5, 0.0, MUL, ADD),
                     nc.vector.tensor_tensor_scan(d5, decay, c5, 0.0, MUL, ADD))
                say(dve, s5w_ready)

            def s5_back(j):
                cs, sn = [t[:, :] for t in tab[j % 2]]
                link(tt(a5, b5, cs, MUL), tt(c5, d5, sn, MUL))
                if j < SJ - 2:
                    say(dve, tab_free)
                if j % 4:
                    dve.wait_ge(s5x_read, 1).then_inc(s5x_read, -1)
                tt(e5, a5, c5, SUB).then_inc(s5x_ready, 1)

            def s5_finish(i):
                dve.wait_ge(s5x_read, 1).then_inc(s5x_read, -1)
                if i == 1:
                    dve.wait_ge(s5w_read, 1).then_inc(s5w_read, -1)
                link(stt(u[:, i, :], u[:, i, :], col("s5d", i), bank[6][:, :], MUL, ADD))
                say(dve, bank_free[6], ask_act)
                if i == 0:
                    say(dve, s5im_read)

            def m2_sums():
                dve.wait_ge(dve_bank[7], 1).then_inc(dve_bank[7], -1)
                link(copy(flat(s16[:, 4:6, :]), bank[7][:, 0:32]))
                say(dve, bank_free[7])
                link(tt(s16[:, 6, :], s16[:, 5, :], s16[:, 4, :], SUB))
                say(dve, ask_act)

            hs = [P, M2H, M2P]

            def m2_turned(t):
                b, hc = (4, 7)[t % 2], slice(t * M2H, (t + 1) * M2H)
                dve.wait_ge(dve_bank[b], 1).then_inc(dve_bank[b], -1)
                xdt = xbt[:, t, 0:2, :].rearrange("p a b -> p (a b)").rearrange("p (h c) -> p h c", h=M2H)
                w = [tt(xdt, bank[b][:, 0:2 * P].rearrange("p (h c) -> p h c", h=M2H),
                        s16[:, 0, hc].unsqueeze(2).broadcast_to(hs), MUL)]
                if t < NQ - 1:
                    w.append(copy(flat(xbt[:, t, 2:4, :]), bank[b][:, 2 * P:4 * P]))
                link(*w)
                say(dve, bank_free[b])
                if t < NQ - 1:
                    link(tt(xds[:, t], xdt, s16[:, 6, hc].unsqueeze(2).broadcast_to(hs), MUL))
                say(dve, xbt_ready)

            def m2_state(t):
                if t != 1:
                    dve.wait_ge(dve_bank[5], 1).then_inc(dve_bank[5], -1)
                o = 2 * P * (t % 2)
                st = bank[5][:, o:o + 2 * P].rearrange("p (h c) -> p h c", h=M2H)
                if t == 0:
                    link(copy(hst[:, 0], st))
                else:
                    cd = s16[:, 7, t * M2H:(t + 1) * M2H].unsqueeze(2).broadcast_to(hs)
                    link(tt(hst[:, t], hst[:, t - 1], cd, MUL))
                    link(tt(hst[:, t], hst[:, t], st, ADD))
                if t:
                    say(dve, bank_free[5])

            def m2_logs(h):
                dve.wait_ge(dve_bank[4], 1).then_inc(dve_bank[4], -1)
                logs = m2buf[h % 2][0]
                link(*[stt(logs[:, t * P:(t + 1) * P], bank[4][:, t * P:(t + 1) * P],
                           s16[:, 4, t * M2H + h:t * M2H + h + 1], cap, SUB, ALU.min) for t in range(NQ)])
                say(dve, ask_act)

            def m2_mix(h):
                dve.wait_ge(act_says, 1).then_inc(act_says, -1)
                if h % 2 == 0:
                    dve.wait_ge(dve_bank[7], 1).then_inc(dve_bank[7], -1)
                e, ec = m2buf[h % 2]
                link(tt(ec, ec, xbc[:, 4 + h // 2, :], MUL), tt(e, e, bank[7][:, :], MUL))
                if h % 2:
                    say(dve, bank_free[7])
                say(dve, mix_ready)

            def m2_pair(i):
                link(stt(xbc[:, i, :], xbc[:, i, :], col("m2d", i), bank[5][:, :], MUL, ADD))
                say(dve, bank_free[5])
                link(tt(xbc[:, i, :], xbc[:, i, :], z[:, i, :], MUL))
                say(dve, ask_act)

            def sc_product(i):
                scaled(pad[:, i, 4:4 + T], i)
                link(tt(pad[:, i, 4:4 + T], pad[:, i, 4:4 + T], G[:, 4 + i, :], MUL))

            def sc_conv(i):
                taps(G[:, 4 + i, :], i, [col("scw", 3 * i + k) for k in range(3)], 0)

            def sc_gate(i):
                scaled(G[:, 0, :], i)
                link(tt(G[:, 4 + i, :], G[:, 0, :], G[:, 4 + i, :], MUL))
                say(dve, em_full)

            def qk_finish(t):
                p, q = t % 2, qk[:, t, :]
                link(stt(q, G[:, p, :], col("qkg", p), cosT, MUL, MUL))
                dve.wait_ge(dve_bank[5], 1).then_inc(dve_bank[5], -1)
                link(tt(G[:, 5, :], bank[5][:, :], sinT, MUL))
                say(dve, bank_free[5])
                link(tt(q, q, G[:, 5, :], ADD))
                dve.wait_ge(act_says, 1).then_inc(act_says, -1)
                link(tt(q, q, G[:, 3 + p, :], MUL))

            def maxima(n):
                s, w = n % 2, (n % NQ + 1) * P
                banks = (2, 3, 6, 7)[2 * s:2 * s + 2]
                for c, b in enumerate(banks):
                    dve.wait_ge(dve_bank[b], 1).then_inc(dve_bank[b], -1)
                    nc.vector.tensor_reduce(soft[:, s, c:c + 1], bank[b][:, 0:w], AX, ALU.max,
                                            negate=True).then_inc(exp_go, 1)

            def combine(n):
                s, w = n % 2, (n % NQ + 1) * P
                dve.wait_ge(exp_done, 1).then_inc(exp_done, -1)
                link(nc.vector.reciprocal(soft[:, s, 4:6], soft[:, s, 2:4]))
                link(ts(G[:, 2 * s + 1, 0:w], G[:, 2 * s + 1, 0:w], soft[:, s, 5:6], mlam[:, :], MUL, MUL))
                link(stt(G[:, 2 * s, 0:w], G[:, 2 * s, 0:w], soft[:, s, 4:5], G[:, 2 * s + 1, 0:w], MUL, ADD))
                say(dve, probs_ready)

            def head_out():
                dve.wait_ge(dve_bank[5], 1).then_inc(dve_bank[5], -1)
                link(copy(ssum[:, :], bank[5][:, :]))
                say(dve, bank_free[5], osq_go)

            def head_emit(h):
                dve.wait_ge(onorm_done, 1).then_inc(onorm_done, -1)
                link(stt(ssum[:, :], ssum[:, :], col("subg"), rbc[:, :], MUL, MUL))
                emit(MIXA + h, ssum[:, :])

            def ffn_tile(half, i):
                scaled(pad[:, 0, 4:4 + T], 0)
                w0 = PARAMS["ffw"][0] + half * FHALF * 3
                taps(G[:, 0, :], 0, [par[:, bass.ds(i * 3 + (w0 + k), 1)] for k in range(3)], 0)
                say(dve, ask_act)
                scaled(G[:, 2, :], 1)
                dve.wait_ge(act_says, 1).then_inc(act_says, -1)
                link(tt(G[:, 3, :], G[:, 1, :], G[:, 2, :], MUL))
                say(dve, ask_act)
                dve.wait_ge(act_says, 1).then_inc(act_says, -1)
                link(tt(flat(ml[:, bass.ds(i, 1), :]), G[:, 3, :], flat(mh[:, bass.ds(i, 1), :]).bitcast(F32), SUB))
                say(dve, hid_ready)

            link(nc.vector.memset(pad[:, :, :], 0.0))
            say(dve, *bank_free, sq_free, sq_free, mats_free)
            dve.wait_ge(pre_loaded, 16).then_inc(pre_loaded, -16)
            s5_angles()
            dve.wait_ge(cst_loaded, 16).then_inc(cst_loaded, -16)
            link(copy(cbf[:, 0, :], ident), copy(cbf[:, 1, :], pre[:, 0, PRE["mask"]]))
            dve.wait_ge(par_loaded, 16).then_inc(par_loaded, -16)
            parameters(0)
            link(nc.vector.memset(ssum[:, :], 0.0))
            say(dve, act_go, pe_go)
            for k in range(KD):
                if k % (KD // 2) == 0:
                    dve.wait_ge(x_loaded[2 * k // KD], 8 * KD).then_inc(x_loaded[2 * k // KD], -(8 * KD))
                    say(dve, *[x_ready] * (KD // 2))
                norm_tile(k, k % 2, "g1")
                s5_decay(k)
            say(dve, ssum_ready)
            s5_phases()
            dve.wait_ge(act_says, 1).then_inc(act_says, -1)
            s5_values()
            with dve.Fori(0, L) as l:
                layer_values(l)
                dve.wait_ge(rms_ready, 1).then_inc(rms_ready, -1)
                say(dve, tab_free, tab_free)
                for i in range(2):
                    scaled(u[:, i, :], i)
                dve.wait_ge(mats_full, 32).then_inc(mats_full, -32)
                say(dve, u_ready)
                dt_scaled()
                for s in range(2, NIN):
                    if 2 <= s <= 7:
                        scaled(pad[:, s % 2, 4:4 + T], s % 2)
                        if s == 2:
                            m2_dt()
                        if s == 3:
                            m2_log()
                        if s >= 4:
                            dve.wait_ge(act_says, 1).then_inc(act_says, -1)
                        if s == 4:
                            m2_series()
                        taps(G[:, s % 2, :], s % 2, [col("m2w", 4 * (s - 2) + k) for k in range(4)], 0,
                             col("m2b", s - 2))
                        say(dve, ask_act)
                    if s == 4:
                        m2_steps()
                    if s == 6:
                        m2_sums()
                    if s == 7:
                        dve.wait_ge(act_says, 1).then_inc(act_says, -1)
                        dve.wait_ge(act_says, 1).then_inc(act_says, -1)
                        m2_turned(0)
                        m2_turned(1)
                    if 8 <= s <= 9:
                        scaled(z[:, s - 8, :], s % 2)
                        if s == 9:
                            dve.wait_ge(act_says, 1).then_inc(act_says, -1)
                        say(dve, ask_act)
                    if s == 8:
                        m2_turned(2)
                        m2_turned(3)
                    if s == 9:
                        m2_logs(0)
                        m2_state(0)
                        m2_state(1)
                        dve.wait_ge(act_says, 1).then_inc(act_says, -1)
                        dve.wait_ge(act_says, 1).then_inc(act_says, -1)
                        m2_mix(0)
                    if 10 <= s <= 11:
                        scaled(G[:, 4 + s % 2, :], s % 2)
                    if s == 10:
                        m2_state(2)
                        say(dve, hst_ready)
                        s5_scan(0)
                    if s == 11:
                        m2_logs(1)
                        m2_mix(1)
                        s5_back(0)
                    if 12 <= s <= 13:
                        sc_product(s % 2)
                        if s == 12:
                            dve.wait_ge(mix_read, 1).then_inc(mix_read, -1)
                            dve.wait_ge(mix_read, 1).then_inc(mix_read, -1)
                        m2_logs(s - 10)
                        if s == 12:
                            m2_pair(0)
                        sc_conv(s % 2)
                        m2_mix(s - 10)
                    if 14 <= s <= 15:
                        sc_gate(s % 2)
                    if s == 14:
                        dve.wait_ge(mix_read, 1).then_inc(mix_read, -1)
                        dve.wait_ge(mix_read, 1).then_inc(mix_read, -1)
                        m2_pair(1)
                        s5_scan(1)
                    if 14 <= s <= 15:
                        emit_low(MIXB + s % 2, G[:, 4 + s % 2, :])
                    if s == 15:
                        s5_back(1)
                    if 16 <= s <= 23:
                        scaled(G[:, s % 2, :], s % 2)
                        say(dve, ask_act)
                    if s == 16:
                        dve.wait_ge(act_says, 1).then_inc(act_says, -1)
                        link(*[stt(xbc[:, 4 + i, :], xbc[:, i, :], col("m2g", i), z[:, 0, :], MUL, MUL)
                               for i in range(2)])
                        say(dve, em_full, em_full)
                    if s == 17:
                        for i in range(2):
                            emit_low(MIXD + i, xbc[:, 4 + i, :])
                    if s == 22:
                        dve.wait_ge(act_says, 1).then_inc(act_says, -1)
                    if 17 <= s <= 24:
                        qk_finish(s - 17)
                    if s >= 24:
                        if s >= 26:
                            dve.wait_ge(vch_read, 1).then_inc(vch_read, -1)
                        scaled(G[:, s % 2, :], s % 2)
                        say(dve, vch_ready)
                    if s == 21:
                        s5_finish(0)
                    if s >= 16:
                        (s5_back if s % 2 else s5_scan)((s - 12) // 2)
                    if s == 24:
                        say(dve, qk_ready)
                maxima(0)
                s5_finish(1)
                dve.wait_ge(act_says, 1).then_inc(act_says, -1)
                say(dve, glu_in)
                for _ in range(2):
                    dve.wait_ge(vch_read, 1).then_inc(vch_read, -1)
                maxima(1)
                combine(0)
                for n in range(STEPS):
                    if n - 1 in BESIDE:
                        residual(BESIDE.index(n - 1), BESIDE.index(n - 1) % 2)
                    if n + 1 < STEPS:
                        combine(n + 1)
                    if n + 2 < STEPS:
                        maxima(n + 2)
                    if n == 0:
                        for i, (gate, gated) in enumerate(((sA, sC), (sB, sD))):
                            dve.wait_ge(act_says, 1).then_inc(act_says, -1)
                            link(tt(gated[:, :], gate[:, :], u[:, i, :], MUL))
                            say(dve, em_full)
                        say(dve, mats_free)
                    if n == 1:
                        for i, gated in enumerate((sC, sD)):
                            emit_low(MIXC + i, gated[:, :])
                    if n >= NQ and n % NQ == 0:
                        head_out()
                    if n > NQ and n % NQ == 3:
                        head_emit(n // NQ - 1)
                residual(KD - 3, 1)
                head_out()
                residual(KD - 2, 0)
                head_emit(HEADS - 1)
                residual(KD - 1, 1)
                finish_x("g2")
                dve.wait_ge(rms_ready, 1).then_inc(rms_ready, -1)
                for half in range(2):
                    with dve.Fori(0, FHALF) as i:
                        ffn_tile(half, i)
                    if half == 0:
                        residuals()
                parameters(l + 1)
                finish_x("g1")
            say(dve, out_ready)


def constants():
    c = np.zeros((P, NCONST), np.float32)
    r = np.arange(P)
    c[:, CONSTS["ident"]] = np.eye(P)
    c[:, CONSTS["ones"]] = 1
    c[:, CONSTS["tri"]] = r[:, None] <= r[None, :]
    perm, cos, sin = np.zeros((P, P)), np.ones((P, T)), np.zeros((P, T))
    inv = (1.0 / (THETA ** (np.arange(0, ROPE, 2, dtype=np.float32) / ROPE))).astype(np.float32)
    ang = np.arange(T, dtype=np.float32)[:, None] * inv[None, :]
    half = ROPE // 2
    for b in range(2):
        for i in range(half):
            lo, hi = b * QK + i, b * QK + half + i
            perm[hi, lo], perm[lo, hi] = -1, 1
            cos[lo], cos[hi] = np.cos(ang[:, i]), np.cos(ang[:, i])
            sin[lo], sin[hi] = np.sin(ang[:, i]), np.sin(ang[:, i])
    c[:, CONSTS["perm"]] = perm
    c[:, CONSTS["block"]] = r[:, None] // QK == r[None, :] // QK
    c[:, CONSTS["cap"]] = np.where(r[None, :] >= r[:, None], 0.0, NEG)
    c[:, CONSTS["eps"]] = EPS
    return c, np.stack([cos, sin], axis=1).astype(np.float32)


def layout(inp):
    def units(w, first_k=0, K=None):
        K = w.shape[1] // P if K is None else K
        w = w[:, first_k * P:(first_k + K) * P].reshape(L, K, P, -1, P)
        return np.ascontiguousarray(w.transpose(0, 3, 2, 1, 4)).reshape(L, -1, P, K * P)

    w = inp["w_in"]
    a, b, c = 512, 1024, 1536
    sc, s5, z, xbc, dt = 1536, 2304, 2560, 2816, 3584
    order = [w[:, :, s5:z], w[:, :, xbc:dt], w[:, :, z:xbc], w[:, :, sc + 256:sc + 512], w[:, :, sc + 512:s5],
             w[:, :, sc:sc + 256]]
    for h in range(HEADS):
        order += [w[:, :, h * P:(h + 1) * P], w[:, :, a + h * P:a + (h + 1) * P]]
    w_in = units(np.concatenate(order + [w[:, :, b:c]], axis=2))
    w_first = np.concatenate([w_in[:, :2], w_in[-1:, :2]])
    gu = np.stack([units(inp["ffn_w_gate"]), units(inp["ffn_w_up"])], axis=2).reshape(L, 2 * FF, P, KD * P)
    dn = np.stack([units(inp["ffn_w_down"], h * FHALF, FHALF) for h in range(2)], axis=1).reshape(L, 16, P, FHALF * P)

    par = np.zeros((P, L, NPAR), np.float32)

    def put(name, value):
        o, n = PARAMS[name]
        par[:, :, o:o + n] = np.broadcast_to(value, (L, P, n)).transpose(1, 0, 2)

    def tiled(p):
        return p.reshape(L, -1, P).transpose(0, 2, 1)

    put("g1", tiled(inp["ln1_g"]))
    put("g2", tiled(inp["ln2_g"]))
    put("qkg", np.tile(inp["qk_norm_g"], (1, 1, 2)).transpose(0, 2, 1))
    put("subg", tiled(inp["subln_g"]))
    init = np.array([0.8 - 0.6 * np.exp(-0.3 * l) for l in range(L)], np.float32)
    put("oneml", (np.float32(1) - init).reshape(L, 1, 1))
    put("scw", inp["sc_conv_w"].reshape(L, 3, 2, P).transpose(0, 3, 2, 1).reshape(L, P, 6))

    def states(p):
        return p.reshape(L, SJ, P).transpose(0, 2, 1)

    put("s5d", tiled(inp["s5_d"]))
    put("bglu", tiled(inp["s5_b_glu"]))
    put("m2w", inp["m2_conv_w"].reshape(L, 4, 6, P).transpose(0, 3, 2, 1).reshape(L, P, 24))
    put("m2b", tiled(inp["m2_conv_b"]))
    put("dtb", inp["m2_dt_bias"][:, None, :])
    put("alog", inp["m2_a_log"][:, None, :])
    put("m2d", tiled(np.repeat(inp["m2_d"], M2P, axis=1)))
    put("m2g", tiled(inp["m2_norm_g"]))
    put("ffw", inp["ffn_conv_w"].reshape(L, 3, FF, P).transpose(0, 3, 2, 1).reshape(L, P, 3 * FF))
    put("wdt", w[:, :, dt:].reshape(L, KD, P, M2H).transpose(0, 2, 1, 3).reshape(L, P, KD * M2H))

    pre = np.zeros((P, L, NPRE), np.float32)
    pre[:, :, PRE["lre"]] = states(inp["s5_lam_re"]).transpose(1, 0, 2)
    pre[:, :, PRE["lim"]] = states(inp["s5_lam_im"]).transpose(1, 0, 2)
    pre[:, :, PRE["ldt"]] = states(np.repeat(inp["s5_log_dt"], 64, axis=1)).transpose(1, 0, 2)
    pre[:, :, PRE["dal"]] = inp["da_lambda"].reshape(1, L, 4 * QK)
    pre[:, :, PRE["linit"]] = init.reshape(1, L, 1)
    pre[:, :, PRE["mask"]] = np.where(np.arange(P)[None, :] <= np.arange(P)[:, None], 0.0, NEG)[:, None]
    pre[:, :, PRE["steps"]] = np.concatenate([np.arange(FINE), FINE * np.arange(COARSE)])

    par = np.concatenate([par, par[:, -1:]], axis=1)
    constant, rotary = constants()

    bmat = np.zeros((L, 2, 4, 2, 16, 2, 2, 64), np.float32)
    cmat = np.zeros((L, 2, 64, 2, SJ, 2, 16), np.float32)
    for ci, (bn, cn) in enumerate((("s5_b_re", "s5_c_re"), ("s5_b_im", "s5_c_im"))):
        bb = inp[bn].reshape(L, 2, 4, 2, 64, 16)
        cc = inp[cn].reshape(L, SJ, 2, 16, 64)
        for g in range(2):
            bmat[:, :, :, g, :, ci, g, :] = bb[:, :, :, g].transpose(0, 1, 2, 4, 3)
            cmat[:, g, :, ci, :, g, :] = cc[:, :, g].transpose(0, 3, 1, 2)
    bmat = bmat.transpose(0, 2, 3, 4, 5, 1, 6, 7).reshape(L, P, 2 * 2 * P)
    cmat = np.ascontiguousarray(cmat.reshape(L, P, 2, SJ * SH).transpose(1, 0, 2, 3))
    wglu = inp["s5_w_glu"].reshape(L, 2, P, 256).transpose(0, 2, 1, 3).reshape(L, P, 512)
    return {
        "x": inp["x"].reshape(T, KD, P).transpose(2, 1, 0), "par": par, "pre": pre, "cst": constant, "rotary": rotary,
        "w_first": w_first, "w_in": np.ascontiguousarray(w_in[:, 2:]),
        "w_oe": units(inp["w_out"], HEADS, KEARLY), "w_ol": units(inp["w_out"], 0, HEADS),
        "w_gu": gu, "w_dn": dn, "bmat": bmat, "cmat": cmat, "wglu": wglu,
    }


def kernel(**inputs):
    import concourse.bacc as bacc
    from concourse.bass_utils import run_bass_kernel_spmd as run

    arrays = layout({k: np.asarray(a) for k, a in inputs.items()})
    arrays = {f"in_{k}": np.ascontiguousarray(a) for k, a in arrays.items()}
    nc = bacc.Bacc("TRN2", target_bir_lowering=False, num_devices=1)
    A = {k[3:]: nc.dram_tensor(k, a.shape, mybir.dt.from_np(a.dtype), kind="ExternalInput").ap()
         for k, a in arrays.items()}
    A["out"] = nc.dram_tensor("out_x", (P, KD, T), F32, kind="ExternalOutput").ap()
    build(nc, A)
    out = run(nc, [arrays], core_ids=[0]).results[0]["out_x"]
    return np.ascontiguousarray(out.transpose(2, 1, 0)).reshape(1, T, D)
```
